# Optimizing a Trainium2 kernel written in Bass

```python
import math
import numpy as np
import jax
import jax.numpy as jnp
from jax import lax

D_MODEL = 1024
BATCH = 1
SEQ = 512
DEPTH = 2

MEM_LEN = 256
NORM_EPS = 1e-6
ROPE_THETA = 10000.0
NEG_INF = -1e30
FORCE_SCORE = 1e9

NSA_HEADS = 8
NSA_KV_GROUPS = 2
NSA_HEAD_DIM = 64
NSA_CMP_BLOCK = 32
NSA_CMP_STRIDE = 16
NSA_SEL_BLOCK = 64
NSA_TOPK = 16
NSA_WINDOW = 512
NSA_Q_BLOCK = 128
NSA_Q_WIDTH = NSA_HEADS * NSA_HEAD_DIM
NSA_KV_WIDTH = NSA_KV_GROUPS * NSA_HEAD_DIM

SSM_INNER = 512
SSM_HEAD_DIM = 64
SSM_HEADS = SSM_INNER // SSM_HEAD_DIM
SSM_GROUPS = 2
SSM_STATE = 64
SSM_CONV = 4
SSM_CHUNK = 128
SSM_CONV_DIM = SSM_INNER + 2 * SSM_GROUPS * SSM_STATE
DT_MIN = 1e-3
DT_MAX = 1e-1

HG_HEADS = 4
HG_KEY_DIM = 128
HG_VAL_DIM = 128
HG_WIDTH = HG_HEADS * HG_KEY_DIM
HG_CHUNK = 64

XA_HEADS = 4
XA_HEAD_DIM = 128
XA_WIDTH = XA_HEADS * XA_HEAD_DIM

FFN_HIDDEN = -(-(8 * D_MODEL) // (3 * 256)) * 256

SPLIT_SIZES = (
    NSA_Q_WIDTH,
    NSA_KV_WIDTH, NSA_KV_WIDTH,
    NSA_KV_WIDTH, NSA_KV_WIDTH,
    NSA_KV_WIDTH, NSA_KV_WIDTH,
    3 * NSA_HEADS,
    SSM_INNER,
    SSM_CONV_DIM,
    SSM_HEADS,
    HG_WIDTH, HG_WIDTH,
    HG_HEADS * HG_VAL_DIM,
    HG_HEADS * HG_VAL_DIM,
    D_MODEL, D_MODEL, D_MODEL,
)
IN_DIM = sum(SPLIT_SIZES)

kernel_name = 'hybrid_nsa_ssd_hgrn2_decoder'

def rms_norm(x, w):
    xf = x.astype(jnp.float32)
    y = xf * lax.rsqrt(jnp.mean(xf * xf, axis=-1, keepdims=True) + NORM_EPS)
    return (y * w.astype(jnp.float32)).astype(x.dtype)

def rope(x, pos):
    half = x.shape[-1] // 2
    inv = 1.0 / (ROPE_THETA ** (jnp.arange(half, dtype=jnp.float32) / half))
    ang = pos.astype(jnp.float32)[:, None] * inv[None, :]
    cos = jnp.cos(ang)[:, None, :]
    sin = jnp.sin(ang)[:, None, :]
    xf = x.astype(jnp.float32)
    x1, x2 = xf[..., :half], xf[..., half:]
    return jnp.concatenate([x1 * cos - x2 * sin, x2 * cos + x1 * sin], axis=-1).astype(x.dtype)

def masked_softmax(s, mask):
    s = jnp.where(mask, s.astype(jnp.float32), NEG_INF)
    return jnp.where(mask, jax.nn.softmax(s, axis=-1), 0.0)

def compress_blocks(kv, pos_emb, w1, w2):
    bsz, s, g, hd = kv.shape
    nb = (s - NSA_CMP_BLOCK) // NSA_CMP_STRIDE + 1
    idx = jnp.arange(nb)[:, None] * NSA_CMP_STRIDE + jnp.arange(NSA_CMP_BLOCK)[None, :]
    blk = kv[:, idx] + pos_emb[None, None, :, None, :]
    blk = blk.transpose(0, 1, 3, 2, 4).reshape(bsz, nb, g, NSA_CMP_BLOCK * hd)
    return jax.nn.silu(blk @ w1) @ w2

def nsa_mixer(q, k_cmp, v_cmp, k_slc, v_slc, k_win, v_win, gate_logits, q_norm, k_norm,
              cmp_pos_k, cmp_pos_v, cmp_w1_k, cmp_w2_k, cmp_w1_v, cmp_w2_v):
    bsz, s, _ = q.shape
    H, G, hd = NSA_HEADS, NSA_KV_GROUPS, NSA_HEAD_DIM
    R = H // G
    Lc, stride, Ls, W, QB = NSA_CMP_BLOCK, NSA_CMP_STRIDE, NSA_SEL_BLOCK, NSA_WINDOW, NSA_Q_BLOCK
    scale = hd ** -0.5
    pos = jnp.arange(s)

    def heads(t, n):
        return t.reshape(bsz, s, n, hd)

    q = rope(rms_norm(heads(q, H), q_norm), pos).reshape(bsz, s, G, R, hd)
    ks = rope(rms_norm(heads(k_slc, G), k_norm), pos)
    kw = rope(rms_norm(heads(k_win, G), k_norm), pos)
    vs = heads(v_slc, G)
    vw = heads(v_win, G)

    nb = (s - Lc) // stride + 1
    pos_c = jnp.arange(nb) * stride + Lc - 1
    kc = rope(rms_norm(compress_blocks(heads(k_cmp, G), cmp_pos_k, cmp_w1_k, cmp_w2_k), k_norm), pos_c)
    vc = compress_blocks(heads(v_cmp, G), cmp_pos_v, cmp_w1_v, cmp_w2_v)

    nsel = s // Ls
    n_top = min(NSA_TOPK, nsel)
    ks_blk = ks.reshape(bsz, nsel, Ls, G, hd).transpose(0, 3, 1, 2, 4)
    vs_blk = vs.reshape(bsz, nsel, Ls, G, hd).transpose(0, 3, 1, 2, 4)
    c_start = jnp.arange(nb) * stride
    s_start = jnp.arange(nsel) * Ls
    cover = jnp.clip(jnp.minimum(c_start[:, None] + Lc, s_start[None, :] + Ls)
                     - jnp.maximum(c_start[:, None], s_start[None, :]), 0, None)
    w_cover = cover.astype(jnp.float32) / stride

    kw_pad = jnp.pad(kw, ((0, 0), (W, 0), (0, 0), (0, 0)))
    vw_pad = jnp.pad(vw, ((0, 0), (W, 0), (0, 0), (0, 0)))
    gates = jax.nn.sigmoid(gate_logits.astype(jnp.float32)).reshape(bsz, s, G, R, 3)
    b_idx = jnp.arange(bsz)[:, None, None, None]
    g_idx = jnp.arange(G)[None, :, None, None]
    blk_ids = jnp.arange(nsel)

    def block_fn(qb):
        start = qb * QB
        t = start + jnp.arange(QB)
        qblk = lax.dynamic_slice_in_dim(q, start, QB, axis=1)
        s_c = jnp.einsum('bqgrd,bngd->bgrqn', qblk, kc) * scale
        p_c = masked_softmax(s_c, pos_c[None, :] <= t[:, None])
        o_c = jnp.einsum('bgrqn,bngd->bqgrd', p_c, vc)
        imp = jnp.einsum('bgrqn,nj->bgqj', p_c, w_cover)
        cur = (t // Ls)[:, None]
        forced = (blk_ids[None, :] == 0) | (blk_ids[None, :] == cur) | (blk_ids[None, :] == cur - 1)
        valid = blk_ids[None, :] * Ls <= t[:, None]
        imp = jnp.where(forced, FORCE_SCORE, jnp.where(valid, imp, NEG_INF))
        _, sel = lax.top_k(imp, n_top)
        k_sel = ks_blk[b_idx, g_idx, sel]
        v_sel = vs_blk[b_idx, g_idx, sel]
        key_pos = sel[..., None] * Ls + jnp.arange(Ls)
        mask_s = (key_pos <= t[None, None, :, None, None]).reshape(bsz, G, 1, QB, n_top * Ls)
        s_s = jnp.einsum('bqgrd,bgqkld->bgrqkl', qblk, k_sel).reshape(bsz, G, R, QB, n_top * Ls) * scale
        p_s = masked_softmax(s_s, mask_s).reshape(bsz, G, R, QB, n_top, Ls)
        o_s = jnp.einsum('bgrqkl,bgqkld->bqgrd', p_s, v_sel)
        k_w = lax.dynamic_slice_in_dim(kw_pad, start, QB + W, axis=1)
        v_w = lax.dynamic_slice_in_dim(vw_pad, start, QB + W, axis=1)
        key_pos_w = start - W + jnp.arange(QB + W)
        dlt = t[:, None] - key_pos_w[None, :]
        mask_w = (dlt >= 0) & (dlt < W) & (key_pos_w[None, :] >= 0)
        s_w = jnp.einsum('bqgrd,bkgd->bgrqk', qblk, k_w) * scale
        p_w = masked_softmax(s_w, mask_w)
        o_w = jnp.einsum('bgrqk,bkgd->bqgrd', p_w, v_w)
        gt = lax.dynamic_slice_in_dim(gates, start, QB, axis=1)
        return gt[..., 0:1] * o_c + gt[..., 1:2] * o_s + gt[..., 2:3] * o_w

    out = lax.map(block_fn, jnp.arange(s // QB))
    return out.transpose(1, 0, 2, 3, 4, 5).reshape(bsz, s, H * hd)

def ssd_chunked(x, a, bm, cm):
    bsz, s, H, P = x.shape
    G, N = bm.shape[-2], bm.shape[-1]
    Hg, L = H // G, SSM_CHUNK
    nc = s // L
    x = x.reshape(bsz, nc, L, G, Hg, P)
    a = a.reshape(bsz, nc, L, G, Hg)
    bm = bm.reshape(bsz, nc, L, G, N)
    cm = cm.reshape(bsz, nc, L, G, N)
    a_cum = jnp.cumsum(a, axis=2)
    tri = jnp.tril(jnp.ones((L, L), dtype=bool))[None, None, :, :, None, None]
    seg = a_cum[:, :, :, None] - a_cum[:, :, None, :]
    decay = jnp.exp(jnp.where(tri, seg, NEG_INF))
    cb = jnp.einsum('bctgn,bcsgn->bctsg', cm, bm)
    y_diag = jnp.einsum('bctsgh,bcsghp->bctghp', cb[..., None] * decay, x)
    decay_end = jnp.exp(a_cum[:, :, -1:] - a_cum)
    states = jnp.einsum('bcsgn,bcsghp->bcghpn', bm, x * decay_end[..., None])
    chunk_decay = jnp.exp(a_cum[:, :, -1])

    def step(h, inp):
        st, dec = inp
        return h * dec[..., None, None] + st, h

    h0 = jnp.zeros((bsz, G, Hg, P, N), jnp.float32)
    _, prev = lax.scan(step, h0, (states.transpose(1, 0, 2, 3, 4, 5), chunk_decay.transpose(1, 0, 2, 3)))
    prev = prev.transpose(1, 0, 2, 3, 4, 5)
    y_off = jnp.einsum('bctgn,bcghpn->bctghp', cm, prev) * jnp.exp(a_cum)[..., None]
    return (y_diag + y_off).reshape(bsz, s, H, P)

def mamba2_mixer(z, xbc, dt_raw, conv_w, conv_b, dt_bias, a_log, d_skip, norm_w):
    bsz, s, _ = xbc.shape
    G, N = SSM_GROUPS, SSM_STATE
    xpad = jnp.pad(xbc, ((0, 0), (SSM_CONV - 1, 0), (0, 0)))
    conv = conv_b
    for k in range(SSM_CONV):
        conv = conv + xpad[:, k:k + s] * conv_w[k]
    xbc = jax.nn.silu(conv.astype(jnp.float32))
    xs = xbc[..., :SSM_INNER].reshape(bsz, s, SSM_HEADS, SSM_HEAD_DIM)
    bm = xbc[..., SSM_INNER:SSM_INNER + G * N].reshape(bsz, s, G, N)
    cm = xbc[..., SSM_INNER + G * N:].reshape(bsz, s, G, N)
    dt = jax.nn.softplus(dt_raw.astype(jnp.float32) + dt_bias)
    a = -jnp.exp(a_log.astype(jnp.float32))
    y = ssd_chunked(xs * dt[..., None], dt * a, bm, cm) + xs * d_skip[:, None]
    y = y.reshape(bsz, s, SSM_INNER) * jax.nn.silu(z.astype(jnp.float32))
    y = rms_norm(y.reshape(bsz, s, G, SSM_INNER // G), norm_w.reshape(G, SSM_INNER // G))
    return y.reshape(bsz, s, SSM_INNER)

def hgrn2_mixer(q_raw, f_raw, i_raw, g_raw, lb, norm_w):
    bsz, s, _ = q_raw.shape
    C, dk, dv = HG_CHUNK, HG_KEY_DIM, HG_VAL_DIM
    nc = s // C
    q = jax.nn.silu(q_raw.astype(jnp.float32)) * dk ** -0.5
    fr = f_raw.astype(jnp.float32)
    log_f = jnp.log(lb + (1.0 - lb) * jax.nn.sigmoid(fr))
    k = (1.0 - lb) * jax.nn.sigmoid(-fr)
    v = i_raw.astype(jnp.float32)

    def to_chunks(t, d):
        return t.reshape(bsz, nc, C, HG_HEADS, d).transpose(1, 0, 3, 2, 4)

    tri = jnp.tril(jnp.ones((C, C), dtype=bool))[None, None, :, :, None]

    def step(state, inp):
        qc, kc, vc, gc = inp
        b = jnp.cumsum(gc, axis=2)
        o_inter = jnp.einsum('bhtd,bhde->bhte', qc * jnp.exp(b), state)
        seg = b[:, :, :, None, :] - b[:, :, None, :, :]
        dec = jnp.exp(jnp.where(tri, seg, NEG_INF))
        att = jnp.einsum('bhtd,bhsd,bhtsd->bhts', qc, kc, dec)
        o_intra = jnp.einsum('bhts,bhse->bhte', att, vc)
        b_last = b[:, :, -1:, :]
        state = state * jnp.exp(b_last[:, :, 0, :, None]) + jnp.einsum('bhsd,bhse->bhde', kc * jnp.exp(b_last - b), vc)
        return state, o_inter + o_intra

    s0 = jnp.zeros((bsz, HG_HEADS, dk, dv), jnp.float32)
    _, o = lax.scan(step, s0, (to_chunks(q, dk), to_chunks(k, dk), to_chunks(v, dv), to_chunks(log_f, dk)))
    o = o.transpose(1, 0, 3, 2, 4).reshape(bsz, s, HG_HEADS, dv)
    o = rms_norm(o, norm_w) * jax.nn.silu(g_raw.astype(jnp.float32)).reshape(bsz, s, HG_HEADS, dv)
    return o.reshape(bsz, s, HG_HEADS * dv)

def memory_cross_attention(h, mem, mem_norm, w_q, w_k, w_v, w_o, q_norm, k_norm):
    bsz, s, _ = h.shape
    m_len = mem.shape[1]
    q = rms_norm((h @ w_q).reshape(bsz, s, XA_HEADS, XA_HEAD_DIM), q_norm)
    m = rms_norm(mem, mem_norm)
    k = rms_norm((m @ w_k).reshape(bsz, m_len, XA_HEADS, XA_HEAD_DIM), k_norm)
    v = (m @ w_v).reshape(bsz, m_len, XA_HEADS, XA_HEAD_DIM)
    sc = jnp.einsum('bshd,bmhd->bhsm', q, k).astype(jnp.float32) * XA_HEAD_DIM ** -0.5
    p = jax.nn.softmax(sc, axis=-1)
    o = jnp.einsum('bhsm,bmhd->bshd', p, v)
    return o.reshape(bsz, s, XA_WIDTH) @ w_o

def swiglu_ffn(h, w_gate, w_up, w_down):
    return (jax.nn.silu(h @ w_gate) * (h @ w_up)) @ w_down

def setup_inputs(seed: int = 0) -> dict:
    key = jax.random.key(seed)
    keys = iter(jax.random.split(key, 64))

    def nrm(shape, scale):
        return jax.random.normal(next(keys), shape, jnp.float32) * scale

    def gain(shape):
        return 1.0 + nrm(shape, 0.05)

    L, D, hd = DEPTH, D_MODEL, NSA_HEAD_DIM
    dt0 = jnp.exp(jax.random.uniform(next(keys), (L, SSM_HEADS), jnp.float32, math.log(DT_MIN), math.log(DT_MAX)))
    a0 = jax.random.uniform(next(keys), (L, SSM_HEADS), jnp.float32, 1.0, 16.0)
    return {
        'x': nrm((BATCH, SEQ, D), 1.0),
        'mem': nrm((BATCH, MEM_LEN, D), 1.0),
        'norm_mix': gain((L, D)),
        'w_in': nrm((L, D, IN_DIM), D ** -0.5),
        'nsa_q_norm': gain((L, hd)),
        'nsa_k_norm': gain((L, hd)),
        'nsa_cmp_pos_k': nrm((L, NSA_CMP_BLOCK, hd), 0.1),
        'nsa_cmp_pos_v': nrm((L, NSA_CMP_BLOCK, hd), 0.1),
        'nsa_cmp_w1_k': nrm((L, NSA_CMP_BLOCK * hd, hd), (NSA_CMP_BLOCK * hd) ** -0.5),
        'nsa_cmp_w2_k': nrm((L, hd, hd), hd ** -0.5),
        'nsa_cmp_w1_v': nrm((L, NSA_CMP_BLOCK * hd, hd), (NSA_CMP_BLOCK * hd) ** -0.5),
        'nsa_cmp_w2_v': nrm((L, hd, hd), hd ** -0.5),
        'w_nsa_o': nrm((L, NSA_Q_WIDTH, D), NSA_Q_WIDTH ** -0.5),
        'ssm_conv_w': nrm((L, SSM_CONV, SSM_CONV_DIM), SSM_CONV ** -0.5),
        'ssm_conv_b': nrm((L, SSM_CONV_DIM), 0.02),
        'ssm_dt_bias': dt0 + jnp.log(-jnp.expm1(-dt0)),
        'ssm_a_log': jnp.log(a0),
        'ssm_d': 1.0 + nrm((L, SSM_HEADS), 0.1),
        'ssm_norm': gain((L, SSM_INNER)),
        'w_ssm_o': nrm((L, SSM_INNER, D), SSM_INNER ** -0.5),
        'hg_lb_logits': nrm((L, HG_WIDTH), 0.1),
        'hg_norm': gain((L, HG_VAL_DIM)),
        'w_hg_o': nrm((L, HG_HEADS * HG_VAL_DIM, D), (HG_HEADS * HG_VAL_DIM) ** -0.5),
        'w_out': nrm((L, D, D), D ** -0.5),
        'norm_xa': gain((L, D)),
        'norm_mem': gain((L, D)),
        'xa_w_q': nrm((L, D, XA_WIDTH), D ** -0.5),
        'xa_w_k': nrm((L, D, XA_WIDTH), D ** -0.5),
        'xa_w_v': nrm((L, D, XA_WIDTH), D ** -0.5),
        'xa_q_norm': gain((L, XA_HEAD_DIM)),
        'xa_k_norm': gain((L, XA_HEAD_DIM)),
        'xa_w_o': nrm((L, XA_WIDTH, D), XA_WIDTH ** -0.5),
        'norm_ffn': gain((L, D)),
        'ffn_w_gate': nrm((L, D, FFN_HIDDEN), D ** -0.5),
        'ffn_w_up': nrm((L, D, FFN_HIDDEN), D ** -0.5),
        'ffn_w_down': nrm((L, FFN_HIDDEN, D), FFN_HIDDEN ** -0.5),
    }

def reference(x, mem, norm_mix, w_in, nsa_q_norm, nsa_k_norm, nsa_cmp_pos_k, nsa_cmp_pos_v,
              nsa_cmp_w1_k, nsa_cmp_w2_k, nsa_cmp_w1_v, nsa_cmp_w2_v, w_nsa_o,
              ssm_conv_w, ssm_conv_b, ssm_dt_bias, ssm_a_log, ssm_d, ssm_norm, w_ssm_o,
              hg_lb_logits, hg_norm, w_hg_o, w_out,
              norm_xa, norm_mem, xa_w_q, xa_w_k, xa_w_v, xa_q_norm, xa_k_norm, xa_w_o,
              norm_ffn, ffn_w_gate, ffn_w_up, ffn_w_down):
    lb_sm = jax.nn.softmax(hg_lb_logits.astype(jnp.float32), axis=0)
    lb_all = jnp.cumsum(lb_sm, axis=0) - lb_sm[0:1]
    split_points = np.cumsum(SPLIT_SIZES)[:-1].tolist()
    for l in range(DEPTH):
        h = rms_norm(x, norm_mix[l])
        (a_q, a_kc, a_vc, a_ks, a_vs, a_kw, a_vw, a_gate,
         b_z, b_xbc, b_dt, c_q, c_f, c_i, c_g, g_a, g_b, g_c) = jnp.split(h @ w_in[l], split_points, axis=-1)
        y_a = nsa_mixer(a_q, a_kc, a_vc, a_ks, a_vs, a_kw, a_vw, a_gate, nsa_q_norm[l], nsa_k_norm[l],
                        nsa_cmp_pos_k[l], nsa_cmp_pos_v[l], nsa_cmp_w1_k[l], nsa_cmp_w2_k[l],
                        nsa_cmp_w1_v[l], nsa_cmp_w2_v[l]) @ w_nsa_o[l]
        y_b = mamba2_mixer(b_z, b_xbc, b_dt, ssm_conv_w[l], ssm_conv_b[l], ssm_dt_bias[l],
                           ssm_a_log[l], ssm_d[l], ssm_norm[l]) @ w_ssm_o[l]
        y_c = hgrn2_mixer(c_q, c_f, c_i, c_g, lb_all[l], hg_norm[l]) @ w_hg_o[l]
        merged = jax.nn.sigmoid(g_a) * y_a + jax.nn.sigmoid(g_b) * y_b + jax.nn.sigmoid(g_c) * y_c
        x = x + (merged @ w_out[l]).astype(x.dtype)
        x = x + memory_cross_attention(rms_norm(x, norm_xa[l]), mem, norm_mem[l], xa_w_q[l], xa_w_k[l],
                                       xa_w_v[l], xa_w_o[l], xa_q_norm[l], xa_k_norm[l]).astype(x.dtype)
        x = x + swiglu_ffn(rms_norm(x, norm_ffn[l]), ffn_w_gate[l], ffn_w_up[l], ffn_w_down[l]).astype(x.dtype)
    return x


_drawn_inputs = setup_inputs


def setup_inputs(seed=0):
    import zlib

    import numpy as np

    out = dict(_drawn_inputs(seed))
    spreads = {}
    factors = {'nsa_q_norm': 8.0,
     'nsa_k_norm': 8.0,
     'nsa_cmp_pos_k': 8.0,
     'ssm_conv_b': 2.714,
     'hg_lb_logits': 8.0,
     'hg_norm': 2.747,
     'norm_xa': 8.0,
     'norm_mem': 5.272,
     'xa_q_norm': 8.0,
     'xa_k_norm': 8.0}
    for name, (base, spread) in spreads.items():
        noise = np.random.default_rng([zlib.crc32(name.encode()), seed]).standard_normal(out[name].shape)
        drawn = base * np.exp(spread * noise) if base else spread * noise
        out[name] = jnp.asarray(drawn.astype(out[name].dtype))
    for name, factor in factors.items():
        out[name] = (out[name] * factor).astype(out[name].dtype)
    return out
```

```python
import numpy as np
import concourse.bass as bass
from concourse import mybir
from contextlib import ExitStack

F32, F32R, BF16 = mybir.dt.float32, mybir.dt.float32r, mybir.dt.bfloat16
ACT, ALU = mybir.ActivationFunctionType, mybir.AluOpType
AX = mybir.AxisListType.X

DEPTH, D, S, MEM = 2, 1024, 512, 256
GB = ((0, 1), (2,), (3,), (4,), (5,), (6, 7))
HG = (("hg0", "hg1"), ("hg2", "hg3"), ("gC0",), ("gC1",), ("gC2", "gC3", "gC4", "gC5", "gC6", "gC7"))
P = 128
KC = D // P
NT = S // P
EPS = 1e-6
NEG = -float(2 ** 100)
FFN_PASSES = (8, 8, 6)
SLOTS = 4
UNIT = 1024

PLAN = ([("params", 1), ("q", 4), ("kv", 4), ("gd", 1), ("kc", 1), ("vc", 1), ("w1k", 1), ("w1v", 1)]
        + [(f"gA{m}", 1) for m in range(8)] + [(f"yA{m}", 1) for m in range(4)]
        + [(f"xbc{m}", 1) for m in range(6)] + [("z", 4)]
        + [(f"gB{m}", 1) for m in range(8)] + [(f"yB{m}", 1) for m in range(4)]
        + [(f"hf{m}", 1) for m in range(4)] + [(f"hq{m}", 1) for m in range(4)] + [("hv", 4)]
        + [(f"hg{m}", 1) for m in range(4)]
        + [(f"gC{m}", 1) for m in range(8)] + [(f"yC{m}", 1) for m in range(4)]
        + [(f"o{m}", 1) for m in range(8)]
        + [(f"xk{m}", 1) for m in range(4)] + [("xv", 4)]
        + [(f"xq{m}", 1) for m in range(4)] + [(f"xo{m}", 1) for m in range(4)])
for _p, _n in enumerate(FFN_PASSES):
    for _c in range(_n):
        PLAN += [(f"fg{_p}_{_c}", 1), (f"fu{_p}_{_c}", 1)]
    PLAN += [(f"fd{_p}_{m}", 1) for m in range(8)]
UNIT_OF, NU = {}, 0
for _name, _n in PLAN:
    UNIT_OF[_name] = NU
    NU += _n
assert NU % SLOTS == 0, NU
COPIED = ("params", "w1k", "w1v")
COPIED_U = {UNIT_OF[n]: n for n in COPIED}
NSPLIT = NU - len(COPIED)


def split_before(u):
    return u - sum(1 for c in COPIED_U if c < u)


PC, _c = {}, 0
for _name, _n in (("norm_mix", 8), ("norm_xa", 8), ("norm_mem", 8), ("norm_ffn", 8), ("conv_w", 24), ("conv_b", 6),
                  ("lb", 8), ("hg_norm", 1), ("xa_q", 1), ("xa_k", 1), ("ssm_norm", 4), ("q_norm", 64),
                  ("k_norm", 64), ("dt_bias", 8), ("a_log", 8), ("ssm_d", 8), ("pos_k", 16), ("pos_v", 16),
                  ("w2k", 64), ("w2v", 64), ("layer", 1)):
    PC[_name] = (_c, _c + _n)
    _c += _n
NPRM = _c

CC, _c = {}, 0
for _name, _n in (("ident", 128), ("triu", 128), ("ones", 128), ("maskq", 128), ("maskt", 128), ("hgmask", 64),
                  ("cos", 128), ("sin", 128), ("cosc", 32), ("sinc", 32), ("maskc", 128), ("valid", 4), ("eps", 1)):
    CC[_name] = (_c, _c + _n)
    _c += _n
NCST = _c


SHARED = {name: s for s, names in {
    "y_hi": ("yA_hi", "yB_hi", "yC_hi", "xo_hi"), "y_lo": ("yA_lo", "yB_lo", "yC_lo", "xo_lo"),
    "y_scaled": ("yB_t", "yC_t"), "merged": ("merge_A", "merge_B", "merge_C"),
    "residual": ("res_o", "res_o_x", "res_xo", "res_xo_x", "res_f0", "res_f1", "res_f2"),
    "h_lo": ("h_mix", "h_xa", "h_ffn"), "ffn_lo": ("ffn_lo0", "ffn_lo1", "ffn_lo2"),
    "compress_pe": ("cmp_mm", "cmp_qk", "cmp_tr", "cmp_pv"),
    "compress_dve": ("cmp_dve", "cmp_sc", "cmp_sub", "cmp_p", "cmp_o"),
    "compress_act": ("cmp_th", "cmp_exp", "cmp_ptc"),
    "ssd_pe": ("acum", "xs_tr", "cb", "seg", "ydiag", "yoff", "st"),
    "ssd_dve": ("dt", "conv_raw", "conv", "xdt", "ssd_xe", "ssd_m", "ssd_y", "ssd_st", "ssd_ss", "ssd_yn"),
    "ssd_act": ("dt_act", "z_th", "conv_th", "xs_ev", "bt_ev", "ssd_dec", "ssd_rs"),
    "hgrn_pe": ("hg_att", "hg_ketr", "hg_st", "hg_o", "hg_ss"),
    "hgrn_dve": ("lb", "hb", "hq_ev", "hg_ev", "hg_arg", "hg_q", "hg_kt", "hg_qb", "hg_ke", "hg_attm", "hg_state"),
    "hgrn_act": ("lb_exp", "hf_s", "hf_ev", "hf_ln", "hq_th", "hg_th", "hg_ex", "hg_ket", "hg_sq", "hg_rl", "hg_rs"),
    "cross_pe": ("x_ss", "xqk", "xptr", "xpv"), "cross_act": ("x_sq", "x_ln", "x_rs", "xexp", "xptc", "xv_ev"),
    "cross_dve": ("xk_ev", "xq_ev", "xnb", "xpn", "xptd"),
}.items() for name in names}


def build(nc, x_d, mem_d, w_d, cst_d, out_d, totals, n_layers=DEPTH):
    count, marks = {}, {}
    ctx = ExitStack()
    sems = {}

    def sem(name):
        if name not in sems:
            sems[name] = ctx.enter_context(nc.semaphore("s_" + name))
        return sems[name]

    layer, recent = {"l": 0}, [None]

    def inc(name, mark=None, by=1):
        recent[0] = name
        s = SHARED.get(name, name)
        count[s] = count.get(s, 0) + by
        if mark is not None:
            assert (name, mark) not in marks, (name, mark)
            marks[name, mark] = count[s]
        return sem(s), by

    def aft(name, mark=None):
        s = SHARED.get(name, name)
        if mark is None:
            n = count[s]
        elif totals is None:
            n = 1
        else:
            n = totals["marks"][name, mark]
        per_layer = 1 if totals is None else totals["count"][s]
        return sem(s), layer["l"] * per_layer + n

    for name in ([] if totals is None else sorted(totals["count"])):
        sem(name)

    base = -(-nc.sbuf_base // 64) * 64
    end = nc.sbuf_usable_end
    top = [base]

    def place(name, shape, dt=F32, at=None):
        size = int(np.prod(shape[1:])) * (2 if dt == BF16 else 4)
        size = -(-size // 32) * 32
        off = top[0] if at is None else at
        if at is None:
            top[0] += size
        assert off + size <= end, (name, off + size - end)
        return nc.alloc_sbuf_tensor_at(name, list(shape), dt, offset=off)

    xT = place("xT", [P, KC, S])
    h_hi, h_lo = place("h_hi", [P, KC, S], F32R), place("h_lo", [P, KC, S], F32R)
    stage = place("stage", [P, SLOTS, UNIT])
    w_hi, w_lo = place("w_hi", [P, SLOTS, UNIT], F32R), place("w_lo", [P, SLOTS, UNIT], F32R)
    cst = place("cst", [P, NCST])
    identb, maskqb, masktb = (place(n, [P, P], BF16) for n in ("identb", "maskqb", "masktb"))
    prm = place("prm", [P, NPRM])
    rstd, acc = place("rstd", [P, S]), place("acc", [P, S])
    tmp = place("tmp", [P, 2, S])
    region = top[0]

    def C(name):
        return cst[:, CC[name][0]:CC[name][1]]

    def PR(name, i=0, n=None):
        a, b = PC[name]
        return prm[:, a + i:(a + i + n if n else b)]

    def col(name, i):
        return prm[:, PC[name][0] + i:PC[name][0] + i + 1]

    ident, triu, ones = C("ident"), C("triu"), C("ones")
    epsc = C("eps")

    merged = place("merged", [P, KC, S])
    w1 = place("w1", [P, 2, UNIT], at=region)
    sg_at = top[0]
    sg = place("sg", [P, KC, S])
    y_at = top[0]
    y_hi, y_lo = place("y_hi", [P, 4, S], F32R), place("y_lo", [P, 4, S], F32R)
    scratch = top[0]

    def row(start):
        at = [start]

        def take(name, shape, dt=F32):
            t = place(name, shape, dt, at=at[0])
            at[0] += -(-int(np.prod(shape[1:])) * (2 if dt == BF16 else 4) // 32) * 32
            return t
        return take

    t_ = row(scratch)
    qr = t_("qr", [P, NT, S])
    kvr = t_("kvr", [P, NT, S])
    rt = t_("rt", [P, NT, S])
    qT = t_("qT", [P, 4, S])
    kT = t_("kT", [P, 4, S])
    o_acc = rt
    gd = t_("gd", [P, NT, 32])
    nsa_end = scratch + 5 * NT * S * 4 + NT * 32 * 4
    kcs = place("kcs", [P, 2, 2, 528], at=y_at)
    t_ = row(y_at)
    Pb = t_("Pb", [P, 2, S])
    PTs = t_("PTs", [P, 2, S])
    kcbd = t_("kcbd", [P, 2, 2, 32])
    vcbd = t_("vcbd", [P, 2, 4, 64])
    kcr = t_("kcr", [P, 2, 64])
    h1 = t_("h1", [64, 4, 64])
    h1v = t_("h1v", [64, 2, 4, 32])
    posb = t_("posb", [64, 2])
    ptc = t_("ptc", [P, 256])
    small = (end - 5120) // 64 * 64
    t_ = row(small)
    ssq = t_("ssq", [P, NT, 12])
    rsq = t_("rsq", [P, NT, 12])
    ssc = t_("ssc", [P, 2])
    sc_c = t_("sc_c", [P, 8, 32])
    mx_c = t_("mx_c", [P, 8])
    sum_c = t_("sum_c", [P, 8])
    nmx = t_("nmx", [P, 2])
    sums = t_("sums", [P, 2, 8])
    coef = t_("coef", [P, 8])
    gth = t_("gth", [P, NT, 24])
    dtb = t_("dtb", [P, 6, 32])
    da, nac, eac, edec, dend, dth = (t_(n, [P, NT, 8]) for n in ("da", "nac", "eac", "edec", "dend", "dth"))
    aexp = t_("aexp", [P, 8])
    dsk = t_("dsk", [P, 8])
    ssy = t_("ssy", [P, NT, 2])
    lbt = t_("lbt", [P, 8, 4])
    eblast = t_("eblast", [P, 4, 8])
    pool_mark = t_("pool_mark", [P, 4])

    t_ = row(scratch)
    xr = t_("xr", [P, 6, S + 3])
    xdt = place("xdt", [P, NT, S], at=scratch)
    cv = t_("cv", [P, 6, S])
    xs = t_("xs", [P, NT, S])
    zs = t_("zs", [P, NT, S])
    Bt = t_("Bt", [P, NT, P])
    assert scratch + 4 * (6 * 515 + 6 * 512 + 8 * 512 + 4 * 128) <= small
    t_ = row(y_at)
    dec = t_("dec", [P, 2, 4, P])
    xe = t_("xe", [P, S])
    hst = t_("hst", [P, 256])
    ssd_y = place("ssd_y", [P, NT, S], at=y_at + 8192)

    t_ = row(scratch)
    hq, hk, hb, hgt, hv = (t_(n, [P, 4, S]) for n in ("hq", "hk", "hb", "hgt", "hv"))
    hQ = t_("hQ", [P, S])
    hKT = place("hKT", [P, 4, 8, 64], at=y_at)
    assert scratch + 4 * 21 * S <= small
    t_ = row(y_at + 8192)
    hatt = t_("hatt", [P, 4, 4, 64])
    hst2 = t_("hst2", [P, 4, P])
    het = t_("het", [P, S])

    t_ = row(scratch)
    kx, vx = t_("kx", [P, 4, MEM]), t_("vx", [P, 2, S])
    rsx = place("rsx", [P, 4, S], at=scratch + 8192)
    mraw = t_("mraw", [P, KC, MEM])
    m_hi, m_lo = t_("m_hi", [P, KC, MEM], F32R), t_("m_lo", [P, KC, MEM], F32R)
    macc, mr, mt = t_("macc", [P, MEM]), t_("mr", [P, MEM]), t_("mt", [P, 2, MEM])
    t_ = row(region)
    qx = t_("qx", [P, 4, S])
    sqx = t_("sqx", [P, 4, S])
    px = t_("px", [P, 2, 4, MEM])
    ptx = t_("ptx", [P, 2, 2, S])
    nbx, smx = (place(n, [P, 2, 4], at=small + 4096 + o) for n, o in (("nbx", 0), ("smx", 32)))
    t_ = row(region)
    a_hi, a_lo = t_("a_hi", [P, 8, S], F32R), t_("a_lo", [P, 8, S], F32R)
    sl = t_("sl", [P, 2, S])
    ft = t_("ft", [P, 2, S])

    ps = ctx.enter_context(nc.psum_tensor("ps", [P, 8, S], F32))

    block = ctx.enter_context(nc.Block())

    mq = 128 ** -0.5

    def x_ready(l, m=7):
        return sem("x_ready"), l * 8 + (m + 1)

    @block.sync
    def _(sp):
        sp.dma_start(xT[:], x_d).then_inc(sem("x_loaded"), 16)
        sp.dma_start(cst[:], cst_d).then_inc(sem("cst_loaded"), 16)
        load = [sem(f"stage_loaded{i}") for i in range(SLOTS)]
        for i in range(SLOTS):
            sp.dma_start(stage[:, i], w_d[i]).then_inc(load[i], 16)
        with sp.Fori(1, n_layers * NU // SLOTS) as g:
            freed = [sp.snap(g * SLOTS - (SLOTS - 1 - i)) for i in range(SLOTS)]
            src = [sp.snap(g * SLOTS + i) for i in range(SLOTS)]
            for i in range(SLOTS):
                sp.wait_ge(sem("stage_freed"), freed[i])
                sp.dma_start(stage[:, i], w_d[bass.ds(src[i], 1)].rearrange("a p n -> (a p) n")).then_inc(load[i], 16)
        sp.wait_ge(sem("x_ready"), 8 * (n_layers + 1))
        sp.dma_start(out_d, xT[:]).then_inc(sem("x_stored"), 16)
        sp.wait_ge(sem("x_stored"), 16)

    @block.gpsimd
    def _(pool):
        with pool.Fori(0, n_layers) as l:
            for u in range(NU):
                slot = u % SLOTS
                pool.wait_ge(sem("unit_rounded"), l * NU + (u + 1))
                if u in COPIED_U:
                    one = stage[:, slot, 0:1]
                    nc.gpsimd.tensor_tensor(pool_mark[:, u % 4:u % 4 + 1], one, one, ALU.subtract)\
                        .then_inc(sem("stage_freed"), 1)
                else:
                    nc.gpsimd.tensor_tensor(w_lo[:, slot], stage[:, slot], w_hi[:, slot].bitcast(F32),
                                            ALU.subtract).then_inc(sem("stage_freed"), 1)

    bank_of = {}

    @block.tensor
    def _(pe):
        MM = nc.tensor.matmul
        pe.wait_ge(sem("cst_loaded"), 16)
        pe.wait_ge(sem("masks_ready"), 3)
        user = {}

        def own(*banks):
            for key in sorted({user[b] for b in banks if user.get(b)}):
                pe.wait_ge(*aft(*key))
            for b in banks:
                user[b] = None

        def unit(u):
            pe.wait_ge(sem("stage_freed"), layer["l"] * NU + (u + 1))

        fb, fbanks = [0], [0, 1, 2, 3]

        def f_job(name, reader, rhs=None, nk=KC, outs=1, n=S, first=None, at=None):
            u = UNIT_OF[name]
            slot = u % SLOTS
            ah, al = rhs or (h_hi, h_lo)
            unit(u)
            for o in range(outs):
                b, c0 = at or (fbanks[fb[0] % len(fbanks)], 0)
                fb[0] += not at
                own(b)
                for k in range(nk):
                    c = (o * nk + k) * P
                    if first and o == 0:
                        pe.wait_ge(*aft(first, k))
                    lh, ll = w_hi[:, slot, c:c + P], w_lo[:, slot, c:c + P]
                    MM(ps[:, b, c0:c0 + n], lh, ah[:, k, :n], start=k == 0, stop=False)
                    MM(ps[:, b, c0:c0 + n], lh, al[:, k, :n], start=False, stop=False)
                    last = MM(ps[:, b, c0:c0 + n], ll, ah[:, k, :n], start=False, stop=k == nk - 1)
                job = name if outs == 1 else f"{name}.{o}"
                last.then_inc(*inc("dense_done", job))
                user[b] = (reader, job) if reader else None
                bank_of[job] = b
            marks["dense_done", ("unit", u)] = count["dense_done"]

        def t_job(name, reader, lhs=None, banks=(0, 1, 2, 3), first=None, between=None):
            u = UNIT_OF[name]
            ah, al = lhs or (h_hi, h_lo)
            own(*banks)
            for j in range(4):
                unit(u + j)
                slot = (u + j) % SLOTS
                for t, b in enumerate(banks):
                    for kk in range(2):
                        k = 2 * j + kk
                        if first and t == 0:
                            pe.wait_ge(*aft(first, k))
                        rh, rl = w_hi[:, slot, kk * S:(kk + 1) * S], w_lo[:, slot, kk * S:(kk + 1) * S]
                        lh, ll = ah[:, k, t * P:(t + 1) * P], al[:, k, t * P:(t + 1) * P]
                        MM(ps[:, b], lh, rh, start=k == 0, stop=False)
                        MM(ps[:, b], lh, rl, start=False, stop=False)
                        last = MM(ps[:, b], ll, rh, start=False, stop=k == KC - 1)
                last.then_inc(*inc("dense_done", name if j == 3 else None))
                marks["dense_done", ("unit", u + j)] = count["dense_done"]
                if between:
                    between(j)
            for b in banks:
                user[b] = (reader, name)
            fb[0] = 0

        def norm_sum(tag):
            own(4)
            MM(ps[:, 4], ones, acc[:], start=True, stop=True).then_inc(*inc("norm_sum", tag))
            user[4] = ("rstd_ready", tag)

        with pe.Fori(0, n_layers) as l:
            layer["l"] = l
            pe.wait_ge(*x_ready(l))
            norm_sum("mix")
            t_job("q", "ev_q", first="h_mix")
            t_job("kv", "ev_kv")
            u = UNIT_OF["gd"]
            slot = u % SLOTS
            own(0)
            unit(u)
            for t in range(NT):
                for k in range(KC):
                    lh, ll = h_hi[:, k, t * P:(t + 1) * P], h_lo[:, k, t * P:(t + 1) * P]
                    rh, rl = w_hi[:, slot, k * 32:(k + 1) * 32], w_lo[:, slot, k * 32:(k + 1) * 32]
                    o = ps[:, 0, t * 32:(t + 1) * 32]
                    MM(o, lh, rh, start=k == 0, stop=False)
                    MM(o, lh, rl, start=False, stop=False)
                    last = MM(o, ll, rh, start=False, stop=k == KC - 1)
            last.then_inc(*inc("dense_done", "gd"))
            marks["dense_done", ("unit", u)] = count["dense_done"]
            user[0] = ("ev_nsa", "gd")
            fb[0] = 1
            f_job("kc", "ev_nsa")
            f_job("vc", "ev_nsa")
            pe.wait_ge(*aft("ev_nsa", "vc"))
            pe.wait_ge(*aft("copied_out", "w1v"))
            own(5)
            for w in range(2):
                for m in range(16):
                    MM(ps[0:64, 5, w * 64:(w + 1) * 64].rearrange("p (a b) -> p a b", a=2), w1[:, w, m * 64:(m + 1) * 64],
                       kcs[:, w, :, 2 * m:2 * m + 497:16], start=m == 0, stop=m == 15)
                for m in range(16):
                    pc = PC["pos_k"][0] + 16 * w + m
                    last = MM(ps[0:64, 5, 128 + w:129 + w], w1[:, w, m * 64:(m + 1) * 64],
                              prm[:, pc:pc + 1], start=m == 0, stop=m == 15)
            last.then_inc(*inc("cmp_mm", "h"))
            user[5] = ("cmp_dve", "h1")
            for m in range(8):
                f_job(f"gA{m}", "sig_ready")
                if m == 1:
                    pe.wait_ge(*aft("cmp_dve", "h1"))
                    own(5)
                    for g in range(2):
                        MM(ps[:, 5, 64 + g * 64:128 + g * 64], h1v[:, g].rearrange("p a b -> p (a b)"),
                           PR("w2v")[0:64], start=True, stop=True)
                    MM(ps[0:64, 5, 0:64], h1[:, 0], PR("w2k")[0:64], start=True, stop=True).then_inc(*inc("cmp_mm", "kv"))
                    user[5] = ("cmp_dve", "kc_raw")
            for c in range(4):
                own(4 + c)
                pe.wait_ge(*aft("q_rot", 3))
                for t in range(NT):
                    last = nc.tensor.transpose(ps[:, 4 + c, t * P:(t + 1) * P], qr[:, t, c * P:(c + 1) * P], ident)
                last.then_inc(*inc("q_tr", c))
                user[4 + c] = ("q_trc", c)
            pe.wait_ge(*aft("k_rot", 3))
            own(6)
            pe.wait_ge(*aft("cmp_dve", "kc_rot"))
            for br in range(2):
                own(4 + br)
                for t in range(NT):
                    last = nc.tensor.transpose(ps[:, 4 + br, t * P:(t + 1) * P], kvr[:, t, br * P:(br + 1) * P], ident)
                last.then_inc(*inc("k_tr", br))
                user[4 + br] = ("k_trc", br)
            nc.tensor.transpose(ps[0:64, 6, 0:64], kcr[0:64, 0], ident[0:64, 0:64]).then_inc(*inc("cmp_mm", "kc_tr"))
            user[6] = ("cmp_dve", "kcbd")
            steps = [(i, br, h) for i in range(NT) for br in range(2) for h in range(8)]
            pe.wait_ge(*aft("q_trc", 3))
            pe.wait_ge(*aft("k_trc", 1))
            pe.wait_ge(*aft("cmp_dve", "kcbd"))

            def qk(n):
                i, br, h = steps[n]
                b = 4 + n % 2
                own(b)
                p0, wid = 64 * (h % 2), (i + 1) * P
                MM(ps[:, b, 0:wid], qT[p0:p0 + 64, h // 2, i * P:(i + 1) * P],
                   kT[p0:p0 + 64, 2 * br + h // 4, 0:wid], start=True, stop=False)
                MM(ps[:, b, i * P:wid], identb[:], maskqb[:], start=False, stop=True).then_inc(*inc("qk", n))
                user[b] = ("exp", n)

            def tr(n):
                i = steps[n][0]
                b = (6, 3)[n % 2]
                pe.wait_ge(*aft("exp", n))
                own(b)
                for j in range(i + 1):
                    last = nc.tensor.transpose(ps[:, b, j * P:(j + 1) * P], Pb[:, n % 2, j * P:(j + 1) * P], ident)
                last.then_inc(*inc("ptr", n))
                user[b] = ("ptc_act" if n % 2 == 0 else "ptc_dve", n)

            def pv(n):
                i, br, h = steps[n]
                b = (7, 2)[(n // 8) % 2]
                pe.wait_ge(*aft("ptc_act" if n % 2 == 0 else "ptc_dve", n))
                if h == 0:
                    own(b)
                for j in range(i + 1):
                    v0 = 256 + br * P + (h // 4) * 64
                    last = MM(ps[:, b, h * 64:(h + 1) * 64], PTs[:, n % 2, j * P:(j + 1) * P],
                              kvr[:, j, v0:v0 + 64], start=j == 0, stop=j == i)
                last.then_inc(*inc("pv", n))
                if h == 7:
                    user[b] = ("o_add", n // 8)

            def cmp_part(i, part):
                if part == 0:
                    own(0)
                    for c in range(4):
                        last = MM(ps[:, 0, c * 64:(c + 1) * 64], qT[:, c, i * P:(i + 1) * P],
                                  kcbd[:, c // 2].rearrange("p a b -> p (a b)"), start=True, stop=True)
                    last.then_inc(*inc("cmp_qk", i))
                    user[0] = ("cmp_sc", i)
                elif part == 1:
                    pe.wait_ge(*aft("cmp_p", i))
                    own(1)
                    for g in range(2):
                        last = nc.tensor.transpose(ps[:, 1, g * P:(g + 1) * P],
                                                   sc_c[:, 4 * g:4 * g + 4].rearrange("p a b -> p (a b)"), ident)
                    last.then_inc(*inc("cmp_tr", i))
                    user[1] = ("cmp_ptc", i)
                else:
                    pe.wait_ge(*aft("cmp_ptc", i))
                    own(0)
                    for g in range(2):
                        last = MM(ps[:, 0, g * 256:(g + 1) * 256], ptc[:, g * P:(g + 1) * P],
                                  vcbd[:, g].rearrange("p a b -> p (a b)"), start=True, stop=True)
                    last.then_inc(*inc("cmp_pv", i))
                    user[0] = ("cmp_o", i)

            for n in range(-1, 65):
                if n + 1 < 64:
                    if (n + 1) % 16 == 0:
                        cmp_part((n + 1) // 16, 0)
                    qk(n + 1)
                if 0 <= n < 64:
                    tr(n)
                if n % 16 == 5 and n < 64:
                    cmp_part(n // 16, 1)
                if n % 16 == 9 and n < 64:
                    cmp_part(n // 16, 2)
                if 0 <= n - 1:
                    pv(n - 1)
            pe.wait_ge(*aft("o_add", 7))
            for c in range(4):
                own(4 + c)
                for t in range(NT):
                    last = nc.tensor.transpose(ps[:, 4 + c, t * P:(t + 1) * P], o_acc[:, t, c * P:(c + 1) * P], ident)
                last.then_inc(*inc("o_tr", c))
                user[4 + c] = ("yA_lo", c)
            for m in range(4):
                f_job(f"yA{m}", "merge_A", rhs=(y_hi, y_lo), nk=4, outs=2, first="yA_lo" if m == 0 else None)
            for m in range(6):
                f_job(f"xbc{m}", "xbc_ev")
            t_job("z", "z_ev")
            for m in GB[0]:
                f_job(f"gB{m}", "sig_ready")
            own(4)
            pe.wait_ge(*aft("dt", "da"))
            for k in range(2):
                for t in range(NT):
                    last = MM(ps[:, 4, k * 32 + t * 8:k * 32 + t * 8 + 8], (triu, ones)[k], da[:, t],
                              start=True, stop=True)
            last.then_inc(*inc("acum", "a"))
            user[4] = ("dt", "args")
            for t in range(NT):
                b = 4 + t
                own(b)
                for c in range(4):
                    if t == 0:
                        pe.wait_ge(*aft("conv", c))
                    last = nc.tensor.transpose(ps[:, b, c * P:(c + 1) * P], cv[:, c, t * P:(t + 1) * P], ident)
                last.then_inc(*inc("xs_tr", t))
                user[b] = ("xs_ev", t)
            own(0)
            pe.wait_ge(*aft("conv", 5))
            for t in range(NT):
                last = nc.tensor.transpose(ps[:, 0, t * P:(t + 1) * P], cv[:, 4, t * P:(t + 1) * P], ident)
            last.then_inc(*inc("xs_tr", "B"))
            user[0] = ("bt_ev", "B")
            fbanks[:] = [0, 1]
            for t in range(NT):
                tk = slice(t * P, (t + 1) * P)
                own(5, 7)
                for g in range(2):
                    gp = slice(64 * g, 64 * g + 64)
                    last = MM(ps[:, 5 + 2 * g, 0:P], cv[gp, 4, tk], cv[gp, 5, tk], start=True, stop=True)
                last.then_inc(*inc("cb", t))
                user[5] = user[7] = ("ssd_m", (t, 1))
                for g in range(2):
                    own(2 + g)
                    for h in range(4):
                        o = ps[:, 2 + g, h * P:(h + 1) * P]
                        hh = 4 * g + h
                        MM(o, da[:, t, hh:hh + 1].to_broadcast([P, P]), triu, start=True, stop=False)
                        last = MM(o, identb[:], masktb[:], start=False, stop=True)
                    last.then_inc(*inc("seg", (t, g)))
                    user[2 + g] = ("ssd_dec", (t, g))
                for m in GB[1 + t]:
                    f_job(f"gB{m}", "sig_ready")
                own(4)
                if t == 0:
                    pe.wait_ge(*aft("xdt", 3))
                for g in range(2):
                    pe.wait_ge(*aft("ssd_m", (t, g)))
                    for h in range(4):
                        hc = slice((4 * g + h) * 64, (4 * g + h + 1) * 64)
                        last = MM(ps[:, 4, hc], dec[:, g, h], xdt[:, t, hc], start=True, stop=True)
                    last.then_inc(*inc("ydiag", (t, g)))
                user[4] = ("ssd_y", t)
                if t > 0:
                    own(5, 7)
                    pe.wait_ge(*aft("ssd_st", t - 1))
                    for g in range(2):
                        gp = slice(64 * g, 64 * g + 64)
                        last = MM(ps[:, 5 + 2 * g, 256:512], cv[gp, 5, tk], hst[gp], start=True, stop=True)
                    last.then_inc(*inc("yoff", t))
                    user[5] = user[7] = ("ssd_y", t)
                if t < NT - 1:
                    own(6)
                    if t == 0:
                        pe.wait_ge(*aft("bt_ev", "B"))
                    pe.wait_ge(*aft("ssd_xe", t))
                    MM(ps[:, 6], Bt[:, t], xe[:], start=True, stop=True).then_inc(*inc("st", t))
                    user[6] = ("ssd_st", t)
            fbanks[:] = [0, 1, 2, 3]
            for m in GB[5]:
                f_job(f"gB{m}", "sig_ready")
            for c in range(4):
                own(4 + c)
                pe.wait_ge(*aft("ssd_yn", 3))
                for t in range(NT):
                    last = nc.tensor.transpose(ps[:, 4 + c, t * P:(t + 1) * P], ssd_y[:, t, c * P:(c + 1) * P], ident)
                last.then_inc(*inc("y_tr", c))
                user[4 + c] = ("yB_t", c)
            for m in range(4):
                f_job(f"yB{m}", "merge_B", rhs=(y_hi, y_lo), nk=4, outs=2, first="yB_lo" if m == 0 else None)
            for m in range(4):
                f_job(f"hf{m}", "hf_ev")
            for m in range(4):
                f_job(f"hq{m}", "hq_ev")
            t_job("hv", "hv_ev")
            for hd in range(4):
                for name in HG[hd]:
                    f_job(name, "hg_ev" if name[0] == "h" else "sig_ready")
                own(4)
                pe.wait_ge(*aft("hg_kt", hd))
                pe.wait_ge(*aft("hg_q", hd))
                for c in range(8):
                    pp = 64 * (c % 2)
                    for T in range(4):
                        o = (c // 2) * 64 + 16 * T
                        last = MM(ps[pp:pp + 64, 4, o:o + 16], hKT[:, T, c], hQ[:, c * 64 + 16 * T:c * 64 + 16 * T + 16],
                                  start=True, stop=True)
                last.then_inc(*inc("hg_att", hd))
                user[4] = ("hg_attm", hd)
                own(5)
                pe.wait_ge(*aft("hg_ke", hd))
                for t in range(NT):
                    last = nc.tensor.transpose(ps[:, 5, t * P:(t + 1) * P], hk[:, hd, t * P:(t + 1) * P], ident)
                last.then_inc(*inc("hg_ketr", hd))
                user[5] = ("hg_ket", hd)
            own(4, 5, 6, 7)
            pe.wait_ge(*aft("hg_ket", 3))
            pe.wait_ge(*aft("hg_attm", 3))
            pe.wait_ge(*aft("hv_ev", "hv"))
            for c in range(8):
                pp = slice(64 * (c % 2), 64 * (c % 2) + 64)
                if c < 7:
                    own(c % 2)
                    for hd in range(4):
                        last = MM(ps[:, c % 2, hd * P:(hd + 1) * P], hk[pp, hd, c // 2 * P:(c // 2 + 1) * P], hv[pp, c // 2, hd * P:(hd + 1) * P],
                                  start=True, stop=True)
                    last.then_inc(*inc("hg_st", c))
                    user[c % 2] = ("hg_state", c)
                if c:
                    pe.wait_ge(*aft("hg_state", c - 1))
                for hd in range(4):
                    o = ps[:, 4 + hd, c * 64:(c + 1) * 64]
                    last = MM(o, hv[pp, c // 2, hd * P:(hd + 1) * P], hatt[pp, hd, c // 2], start=True, stop=c == 0)
                    if c > 0:
                        last = MM(o, hst2[:, hd], hq[:, hd, c * 64:(c + 1) * 64], start=False, stop=True)
                last.then_inc(*inc("hg_o", c))
            for hd in range(4):
                user[4 + hd] = ("yC_lo", hd)
            for hd in range(4):
                own(hd)
                pe.wait_ge(*aft("hg_sq", hd))
                MM(ps[:, hd], ones, hq[:, hd], start=True, stop=True).then_inc(*inc("hg_ss", hd))
                user[hd] = ("hg_rs", hd)
            fb[0] = 0
            for name in HG[4]:
                f_job(name, "sig_ready")
            for m in range(4):
                f_job(f"yC{m}", "merge_C", rhs=(y_hi, y_lo), nk=4, outs=2, first="yC_lo" if m == 0 else None)
            fb[0] = 0
            for m in range(8):
                f_job(f"o{m}", "res_o", first="merged_lo" if m == 0 else None)
                if m == 2:
                    own(5)
                    pe.wait_ge(*aft("mem_acc", "m"))
                    MM(ps[:, 5, :MEM], ones, macc[:], start=True, stop=True).then_inc(*inc("mem_sum", "m"))
                    user[5] = ("mem_rstd", "m")
            for m in range(4):
                f_job(f"xk{m}", None, rhs=(m_hi, m_lo), n=MEM, first="mem_lo" if m == 0 else None,
                      at=(m // 2, m % 2 * MEM))
                if m == 0:
                    pe.wait_ge(*aft("res_o", "o7"))
                    norm_sum("xa")
            user[0] = user[1] = ("xk_ev", "k")
            t_job("xv", "xv_ev", lhs=(m_hi, m_lo), banks=(4, 5))
            own(6, 7)
            pe.wait_ge(*aft("x_sq", "k"))
            for m in range(4):
                last = MM(ps[:, 6 + m // 2, m % 2 * MEM:(m % 2 + 1) * MEM], ones, sqx[:, m, :MEM], start=True, stop=True)
            last.then_inc(*inc("x_ss", "k"))
            user[6] = user[7] = ("x_rs", "k")

            def q_squares(m):
                own(4 + m)
                pe.wait_ge(*aft("x_sq", f"xq{m}"))
                MM(ps[:, 4 + m], ones, sqx[:, m], start=True, stop=True).then_inc(*inc("x_ss", f"xq{m}"))
                user[4 + m] = ("x_rs", f"xq{m}")

            fbanks[:] = [2, 3, 0, 1]
            fb[0] = 0
            for m in range(4):
                f_job(f"xq{m}", "xq_ev", first="h_xa" if m == 0 else None)
                if m:
                    q_squares(m - 1)
            q_squares(3)

            def xqk(hd):
                b = 4 + 2 * (hd % 2)
                own(b, b + 1)
                pe.wait_ge(*aft("xk_ev", "k"))
                pe.wait_ge(*aft("xq_ev", f"xq{hd}"))
                for t in range(NT):
                    last = MM(ps[:, b + t // 2, t % 2 * MEM:(t % 2 + 1) * MEM], qx[:, hd, t * P:(t + 1) * P], kx[:, hd],
                              start=True, stop=True)
                last.then_inc(*inc("xqk", hd))
                user[b] = user[b + 1] = ("xexp", hd)

            def xtr(hd):
                own(0, 1)
                pe.wait_ge(*aft("xpn", hd))
                for j in range(2):
                    for t in range(NT):
                        last = nc.tensor.transpose(ps[:, j, t * P:(t + 1) * P], px[:, hd % 2, t, j * P:(j + 1) * P], ident)
                    last.then_inc(*inc("xptr", (hd, j)))
                user[0], user[1] = ("xptc", hd), ("xptd", hd)

            def xpv(hd):
                b = 2 + hd % 2
                own(b)
                pe.wait_ge(*aft("xptc", hd))
                pe.wait_ge(*aft("xptd", hd))
                pe.wait_ge(*aft("xv_ev", "xv"))
                for j in range(2):
                    last = MM(ps[:, b], vx[:, j, hd * P:(hd + 1) * P], ptx[:, hd % 2, j], start=j == 0, stop=j == 1)
                last.then_inc(*inc("xpv", hd))
                user[b] = ("xo_lo", hd)

            xqk(0)
            xqk(1)
            for hd in range(4):
                xtr(hd)
                if hd < 2:
                    xqk(hd + 2)
                xpv(hd)
            fbanks[:] = [0, 1, 2, 3]
            fb[0] = 0
            for m in range(4):
                f_job(f"xo{m}", "res_xo", rhs=(y_hi, y_lo), nk=4, outs=2, first="xo_lo" if m == 0 else None)
            pe.wait_ge(*aft("res_xo", "xo3.1"))
            norm_sum("ffn")
            for p, n in enumerate(FFN_PASSES):
                for c in range(n):
                    f_job(f"fg{p}_{c}", "ffn_s", first="h_ffn" if p == 0 and c == 0 else None)
                    f_job(f"fu{p}_{c}", "ffn_t")
                for m in range(8):
                    f_job(f"fd{p}_{m}", f"res_f{p}" if p < 2 else "res_f2", rhs=(a_hi, a_lo), nk=n,
                          first=f"ffn_lo{p}" if m == 0 else None)

    @block.scalar
    def _(act):
        A = nc.scalar.activation
        act.wait_ge(sem("cst_loaded"), 16)
        A(identb[:], ident, ACT.Copy).then_inc(sem("masks_ready"), 1)
        A(maskqb[:], C("maskq"), ACT.Copy).then_inc(sem("masks_ready"), 1)
        A(masktb[:], C("maskt"), ACT.Copy).then_inc(sem("masks_ready"), 1)
        done = [0]

        def split_to(last):
            l = layer["l"]
            while done[0] <= min(last, NU - 1):
                u = done[0]
                slot = u % SLOTS
                act.wait_ge(sem(f"stage_loaded{slot}"), 16 * (l * (NU // SLOTS) + (u // SLOTS + 1)))
                if u in COPIED_U:
                    name = COPIED_U[u]
                    if name == "params":
                        A(prm[:], stage[:, slot, :NPRM], ACT.Copy).then_inc(sem("unit_rounded"), 1)
                    else:
                        A(w1[:, name == "w1v"], stage[:, slot], ACT.Copy).then_inc(sem("unit_rounded"), 1)
                    act.wait_ge(sem("unit_rounded"), l * NU + (u + 1))
                    act.sem_inc(*inc("copied_out", name))
                else:
                    if u <= SLOTS:
                        act.wait_ge(*x_ready(l, u % SLOTS + 4))
                    elif u - SLOTS in COPIED_U:
                        act.wait_ge(*aft("dense_done", ("unit", u - 2 * SLOTS)))
                    else:
                        act.wait_ge(*aft("dense_done", ("unit", u - SLOTS)))
                    A(w_hi[:, slot], stage[:, slot], ACT.Copy).then_inc(sem("unit_rounded"), 1)
                done[0] += 1

        def job(name):
            base_name = name.split(".")[0]
            n = dict(PLAN)[base_name]
            split_to(UNIT_OF[base_name] + n - 1 + 3)
            act.wait_ge(*aft("dense_done", name))

        def rs_from(bank, n, out, tag, src_sem, mid, dst_sem, scale):
            act.wait_ge(*aft(src_sem, tag))
            A(out, ps[:, bank, :n], ACT.Ln, bias=epsc, scale=scale).then_inc(*inc(mid, tag))
            act.wait_ge(*aft(mid, tag))
            A(out, out, ACT.Exp, scale=-0.5).then_inc(*inc(dst_sem, tag))

        def norm(tag, upto):
            rs_from(4, S, rstd[:], tag, "norm_sum", "norm_ln", "rstd_ready", 1.0 / D)
            for k in range(KC):
                act.wait_ge(*aft("norm_t", (tag, k)))
                A(h_hi[:, k], tmp[:, k % 2], ACT.Copy).then_inc(*inc("norm_hi", (tag, k)))
                if k in upto:
                    split_to(upto[k])

        def prep_silu(src, dst, sem_name, mark):
            A(dst, src, ACT.Tanh, scale=0.5).then_inc(*inc(sem_name, mark))

        with act.Fori(0, n_layers) as l:
            layer["l"] = l
            done[0] = 0
            split_to(2)
            norm("mix", {1: 3, 4: 4})
            act.wait_ge(*aft("lb", "args"))
            A(lbt[:, 3:5], lbt[:, 1:3], ACT.Exp).then_inc(*inc("lb_exp", "e"))
            job("q")
            for t in range(NT):
                A(qr[:, t], ps[:, t], ACT.Copy).then_inc(*inc("ev_q", "q" if t == 3 else ("q", t)))
            job("kv")
            for t in range(NT):
                A(kvr[:, t], ps[:, t], ACT.Copy).then_inc(*inc("ev_kv", "kv" if t == 3 else ("kv", t)))

            def nsa_rs(tag, src, out, scale):
                act.wait_ge(*aft("nsa_ss", tag))
                A(out, src, ACT.Ln, bias=epsc[:out.shape[0]], scale=scale).then_inc(*inc("nsa_ln", tag))
                act.wait_ge(*aft("nsa_ln", tag))
                A(out, out, ACT.Exp, scale=-0.5).then_inc(*inc("nsa_rs", tag))

            nsa_rs("q", ssq[:, :, 0:8], rsq[:, :, 0:8], 1.0 / 64)
            split_to(UNIT_OF["gd"] + 4)
            nsa_rs("k", ssq[:, :, 8:12], rsq[:, :, 8:12], 1.0 / 64)
            split_to(UNIT_OF["vc"] + 3)
            act.wait_ge(*aft("ev_nsa", "gd"))
            A(gth[:], gd[:, :, 0:24], ACT.Tanh, scale=0.5).then_inc(*inc("gate_th", "g"))
            for w in range(2):
                act.wait_ge(*aft("cmp_dve", ("pre", w)))
                A(h1[:, 2 + w], h1[:, w], ACT.Tanh, scale=0.5).then_inc(*inc("cmp_th", w))
            for m in range(8):
                job(f"gA{m}")
                A(sg[:, m], ps[:, bank_of[f"gA{m}"]], ACT.Tanh, scale=0.5).then_inc(*inc("sig_ready", f"gA{m}"))
            act.wait_ge(*aft("cmp_dve", "kc_ss"))
            A(ssc[0:64, 1:2], ssc[0:64, 0:1], ACT.Ln, bias=epsc[0:64], scale=1.0 / 64).then_inc(*inc("cmp_th", "ln"))
            act.wait_ge(*aft("cmp_th", "ln"))
            A(ssc[0:64, 1:2], ssc[0:64, 1:2], ACT.Exp, scale=-0.5).then_inc(*inc("cmp_th", "rs"))
            for c in range(4):
                act.wait_ge(*aft("q_tr", c))
                A(qT[:, c], ps[:, 4 + c], ACT.Copy).then_inc(*inc("q_trc", c))
            steps = [(i, br, h) for i in range(NT) for br in range(2) for h in range(8)]
            for n in range(65):
                if n < 64:
                    i, br, h = steps[n]
                    wid = (i + 1) * P
                    act.wait_ge(*aft("nmax", n))
                    if n >= 2:
                        act.wait_ge(*aft("ptr", n - 2))
                    A(Pb[:, n % 2, :wid], ps[:, 4 + n % 2, :wid], ACT.Exp, bias=nmx[:, n % 2:n % 2 + 1],
                      accum_out=sums[:, br, h:h + 1]).then_inc(*inc("exp", n))
                if n % 16 == 3 and n < 64:
                    i = n // 16
                    act.wait_ge(*aft("cmp_sub", i))
                    A(sc_c[:], sc_c[:], ACT.Exp).then_inc(*inc("cmp_exp", i))
                if n % 16 == 7 and n < 64:
                    i = n // 16
                    act.wait_ge(*aft("cmp_tr", i))
                    A(ptc[:], ps[:, 1, 0:256], ACT.Copy).then_inc(*inc("cmp_ptc", i))
                if n >= 1 and (n - 1) % 2 == 0:
                    m = n - 1
                    wid = (steps[m][0] + 1) * P
                    act.wait_ge(*aft("ptr", m))
                    if m >= 2:
                        act.wait_ge(*aft("pv", m - 2))
                    A(PTs[:, m % 2, :wid], ps[:, 6, :wid], ACT.Copy).then_inc(*inc("ptc_act", m))
            for c in range(4):
                act.wait_ge(*aft("o_tr", c))
                A(y_hi[:, c], ps[:, 4 + c], ACT.Copy).then_inc(*inc("yA_hi", c))
            for m in range(4):
                for o in range(2):
                    split_to(UNIT_OF[f"yA{m}"] + 3)
            act.wait_ge(*aft("dt", "nabs"))
            A(dtb[:, 2], dtb[:, 1], ACT.Exp).then_inc(*inc("dt_act", "u"))
            A(aexp[:], PR("a_log"), ACT.Exp).then_inc(*inc("dt_act", "a"))

            def conv_tanh(c):
                act.wait_ge(*aft("conv_raw", c))
                A(tmp[:, c % 2], cv[:, c], ACT.Tanh, scale=0.5).then_inc(*inc("conv_th", c))

            for m in range(6):
                job(f"xbc{m}")
                A(xr[:, m, 3:], ps[:, bank_of[f"xbc{m}"]], ACT.Copy).then_inc(*inc("xbc_ev", f"xbc{m}"))
                if m:
                    conv_tanh(m - 1)
            split_to(UNIT_OF["z"] + 2)
            conv_tanh(5)
            job("z")
            for t in range(NT):
                A(zs[:, t], ps[:, t], ACT.Tanh, scale=0.5).then_inc(*inc("z_th", t))

            def gate_b(ms):
                for m in ms:
                    job(f"gB{m}")
                    A(sg[:, m], ps[:, bank_of[f"gB{m}"]], ACT.Tanh, scale=0.5).then_inc(*inc("sig_ready", f"gB{m}"))

            gate_b(GB[0])
            act.wait_ge(*aft("dt", "args"))
            A(eac[:], eac[:], ACT.Exp).then_inc(*inc("dt_act", "eac"))
            A(edec[:], edec[:], ACT.Exp).then_inc(*inc("dt_act", "edec"))
            A(dend[:], dend[:], ACT.Exp).then_inc(*inc("dt_act", "dend"))
            for t in range(NT):
                act.wait_ge(*aft("xs_tr", t))
                A(xs[:, t], ps[:, 4 + t], ACT.Copy).then_inc(*inc("xs_ev", t))
            act.wait_ge(*aft("xs_tr", "B"))
            A(Bt[:].rearrange("p a b -> p (a b)"), ps[:, 0], ACT.Copy).then_inc(*inc("bt_ev", "B"))
            for t in range(NT):
                for g in range(2):
                    act.wait_ge(*aft("seg", (t, g)))
                    if t > 0:
                        act.wait_ge(*aft("ydiag", (t - 1, g)))
                    for h in range(4):
                        hh = 4 * g + h
                        A(dec[:, g, h], ps[:, 2 + g, h * P:(h + 1) * P], ACT.Exp, bias=nac[:, t, hh:hh + 1])\
                            .then_inc(*inc("ssd_dec", (t, g) if h == 3 else (t, g, h)))
                gate_b(GB[1 + t])
            act.wait_ge(*aft("ssd_ss", 3))
            A(ssy[:], ssy[:], ACT.Ln, bias=epsc, scale=1.0 / 1024).then_inc(*inc("ssd_rs", "ln"))
            act.wait_ge(*aft("ssd_rs", "ln"))
            A(ssy[:], ssy[:], ACT.Exp, scale=-0.5).then_inc(*inc("ssd_rs", "rs"))
            gate_b(GB[5])
            for c in range(4):
                act.wait_ge(*aft("yB_t", c))
                A(y_hi[:, c], tmp[:, c % 2], ACT.Copy).then_inc(*inc("yB_hi", c))
            for m in range(4):
                split_to(UNIT_OF[f"yB{m}"] + 3)
            for m in range(4):
                job(f"hf{m}")
                A(hb[:, m], ps[:, bank_of[f"hf{m}"]], ACT.Sigmoid).then_inc(*inc("hf_s", m))
                A(hk[:, m], ps[:, bank_of[f"hf{m}"]], ACT.Sigmoid, scale=-1.0).then_inc(*inc("hf_ev", f"hf{m}"))
            act.wait_ge(*aft("hf_ev", "hf3"))
            act.wait_ge(*aft("lb", "lb"))
            for m in range(4):
                A(hb[:, m], hb[:, m], ACT.Ln, bias=lbt[:, 6, m:m + 1], scale=lbt[:, 7, m:m + 1])\
                    .then_inc(*inc("hf_ln", m))
            for m in range(4):
                job(f"hq{m}")
                A(hq[:, m], ps[:, bank_of[f"hq{m}"]], ACT.Tanh, scale=0.5).then_inc(*inc("hq_th", m))
            job("hv")
            for t in range(NT):
                A(hv[:, t], ps[:, t], ACT.Copy).then_inc(*inc("hv_ev", "hv" if t == 3 else ("hv", t)))

            def fill(names):
                for name in names:
                    m = int(name[2:])
                    job(name)
                    if name[0] == "h":
                        A(hgt[:, m], ps[:, bank_of[name]], ACT.Tanh, scale=0.5).then_inc(*inc("hg_th", m))
                    else:
                        A(sg[:, m], ps[:, bank_of[name]], ACT.Tanh, scale=0.5).then_inc(*inc("sig_ready", name))

            for hd in range(4):
                act.wait_ge(*aft("hg_arg", (hd, "q")))
                A(het[:], het[:], ACT.Exp).then_inc(*inc("hg_ex", (hd, "q")))
                act.wait_ge(*aft("hg_arg", (hd, "kt")))
                for T in range(4):
                    A(hKT[:, T, :, :16 * (T + 1)], hKT[:, T, :, :16 * (T + 1)], ACT.Exp).then_inc(*inc("hg_ex", (hd, "kt", T)))
                act.wait_ge(*aft("hg_q", hd))
                A(het[:], hb[:, hd], ACT.Exp).then_inc(*inc("hg_ex", (hd, "b")))
                act.wait_ge(*aft("hg_arg", (hd, "e")))
                A(tmp[:, 0], tmp[:, 0], ACT.Exp).then_inc(*inc("hg_ex", (hd, "e")))
                A(eblast[:, hd], hb[:, hd, 63::64], ACT.Exp).then_inc(*inc("hg_ex", (hd, "l")))
                fill(HG[hd])
                act.wait_ge(*aft("hg_ketr", hd))
                A(hk[:, hd], ps[:, 5], ACT.Copy).then_inc(*inc("hg_ket", hd))
            act.wait_ge(*aft("hg_o", 7))
            for hd in range(4):
                A(hq[:, hd], ps[:, 4 + hd], ACT.Square).then_inc(*inc("hg_sq", hd))
            for hd in range(4):
                rs_from(hd, S, hk[:, hd], hd, "hg_ss", "hg_rl", "hg_rs", 1.0 / 128)
            for hd in range(4):
                act.wait_ge(*aft("yC_t", hd))
                A(y_hi[:, hd], tmp[:, hd % 2], ACT.Copy).then_inc(*inc("yC_hi", hd))
            act.wait_ge(*aft("yC_lo", 3))
            act.dma_start(mraw[:], mem_d).then_inc(*inc("mem_loaded", "m", 16))
            fill(HG[4])
            for m in range(8):
                split_to(UNIT_OF[f"yC{m // 2}"] + 3)
                act.wait_ge(*aft("merge_C", f"yC{m // 2}.{m % 2}"))
                A(h_hi[:, m], merged[:, m], ACT.Copy, scale=0.5).then_inc(*inc("merged_hi", m))
            for m in range(8):
                job(f"o{m}")
                if m == 2:
                    rs_from(5, MEM, mr[:], "m", "mem_sum", "mem_ln", "mem_rstd", 1.0 / D)
                    for k in range(KC):
                        act.wait_ge(*aft("mem_t", k))
                        A(m_hi[:, k], mt[:, k % 2], ACT.Copy).then_inc(*inc("mem_hi", k))
                        if k == 3:
                            split_to(UNIT_OF["o4"] + 2)
            split_to(UNIT_OF["xk0"] + 3)
            norm("xa", {k: UNIT_OF["xk0"] + 3 + (k + 1) // 2 for k in (1, 3, 5, 7)})
            job("xk3")
            A(sqx[:, :, :MEM], ps[:, 0:2].rearrange("p a (b n) -> p (a b) n", b=2), ACT.Square).then_inc(*inc("x_sq", "k"))
            job("xv")
            A(vx[:], ps[:, 4:6], ACT.Copy).then_inc(*inc("xv_ev", "xv"))
            act.wait_ge(*aft("x_ss", "k"))
            A(rsx[:, :, :MEM], ps[:, 6:8].rearrange("p a (b n) -> p (a b) n", b=2), ACT.Ln, bias=epsc, scale=1.0 / 128)\
                .then_inc(*inc("x_ln", "k"))
            act.wait_ge(*aft("x_ln", "k"))
            A(rsx[:, :, :MEM], rsx[:, :, :MEM], ACT.Exp, scale=-0.5).then_inc(*inc("x_rs", "k"))
            for m in range(5):
                if m < 4:
                    job(f"xq{m}")
                    A(sqx[:, m], ps[:, bank_of[f"xq{m}"]], ACT.Square).then_inc(*inc("x_sq", f"xq{m}"))
                if m == 1:
                    act.wait_ge(*aft("xk_ev", "k"))
                if m:
                    rs_from(3 + m, S, rsx[:, m - 1], f"xq{m - 1}", "x_ss", "x_ln", "x_rs", 1.0 / 128)

            def x_exp(hd):
                for t in range(NT):
                    if t == 0:
                        act.wait_ge(*aft("xnb", hd))
                    if t == 0 and hd >= 2:
                        act.wait_ge(*aft("xptr", (hd - 2, 1)))
                    A(px[:, hd % 2, t], ps[:, 4 + 2 * (hd % 2) + t // 2, t % 2 * MEM:(t % 2 + 1) * MEM], ACT.Exp,
                      bias=nbx[:, hd % 2, t:t + 1], scale=mq, accum_out=smx[:, hd % 2, t:t + 1])\
                        .then_inc(*inc("xexp", hd if t == 3 else (hd, t)))

            x_exp(0)
            x_exp(1)
            for hd in range(4):
                act.wait_ge(*aft("xptr", (hd, 0)))
                if hd >= 2:
                    act.wait_ge(*aft("xpv", hd - 2))
                A(ptx[:, hd % 2, 0], ps[:, 0], ACT.Copy).then_inc(*inc("xptc", hd))
                if hd < 2:
                    x_exp(hd + 2)
                act.wait_ge(*aft("xpv", hd))
                A(y_hi[:, hd], ps[:, 2 + hd % 2], ACT.Copy).then_inc(*inc("xo_hi", hd))
            for m in range(4):
                split_to(UNIT_OF[f"xo{m}"] + 3)
            norm("ffn", {})
            fus = [f"fu{p}_{c}" for p, n in enumerate(FFN_PASSES) for c in range(n)]
            j = 0
            for p, n in enumerate(FFN_PASSES):
                for c in range(n):
                    job(f"fg{p}_{c}")
                    if j >= 2:
                        act.wait_ge(*aft("ffn_t", fus[j - 2]))
                    A(sl[:, j % 2], ps[:, bank_of[f"fg{p}_{c}"]], ACT.Silu).then_inc(*inc("ffn_s", f"fg{p}_{c}"))
                    job(f"fu{p}_{c}")
                    act.wait_ge(*aft("ffn_t", f"fu{p}_{c}"))
                    A(a_hi[:, c], ft[:, j % 2], ACT.Copy).then_inc(*inc("ffn_hi", j))
                    j += 1
                for m in range(8):
                    job(f"fd{p}_{m}")

    @block.vector
    def _(v):
        V = nc.vector
        TT, TS, STT = V.tensor_tensor, V.tensor_scalar, V.scalar_tensor_tensor
        MU, AD, SU, MX = ALU.mult, ALU.add, ALU.subtract, ALU.max

        def then(ins, name="dve", mark=None):
            ins.then_inc(*inc(name, mark))
            v.wait_ge(*aft(name))

        def settle():
            v.wait_ge(*aft(recent[0]))

        def bc(ap, n):
            return ap.unsqueeze(ap.ndim if hasattr(ap, "ndim") else len(ap.shape)).to_broadcast(list(ap.shape) + [n])

        def residual(bank, m, name, key, last):
            v.wait_ge(*aft("dense_done", key))
            if not last:
                TT(xT[:, m], xT[:, m], ps[:, bank], AD).then_inc(*inc(name, key)); settle()
                return
            TT(xT[:, m], xT[:, m], ps[:, bank], AD).then_inc(*inc(name + "_x", key)); settle()
            v.wait_ge(*aft(name + "_x", key))
            squares(m, (name, key))

        def squares(m, key):
            if m == 0:
                ins = TT(acc[:], xT[:, 0], xT[:, 0], MU)
            else:
                then(TT(tmp[:, m % 2], xT[:, m], xT[:, m], MU))
                ins = TT(acc[:], acc[:], tmp[:, m % 2], AD)
            if key is None:
                ins.then_inc(sem("x_ready"), 1)
                v.wait_ge(*x_ready(layer["l"] + 1, m))
            else:
                ins.then_inc(*inc(*key)); settle()

        def norm(tag):
            v.wait_ge(*aft("rstd_ready", tag))

            def scaled(k):
                STT(tmp[:, k % 2], xT[:, k], col("norm_" + tag, k), rstd[:], MU, MU).then_inc(*inc("norm_t", (tag, k))); settle()

            def low(k):
                v.wait_ge(*aft("norm_hi", (tag, k)))
                TT(h_lo[:, k], tmp[:, k % 2], h_hi[:, k].bitcast(F32), SU).then_inc(*inc("h_" + tag, k)); settle()

            scaled(0)
            for k in range(KC):
                if k + 1 < KC:
                    scaled(k + 1)
                low(k)

        v.wait_ge(sem("x_loaded"), 16)
        v.wait_ge(sem("cst_loaded"), 16)
        for m in range(8):
            if m:
                TT(tmp[:, m % 2], xT[:, m], xT[:, m], MU).then_inc(sem("x_square"), 1)
                v.wait_ge(sem("x_square"), m)
                v.wait_ge(sem("x_ready"), m)
                TT(acc[:], acc[:], tmp[:, m % 2], AD).then_inc(sem("x_ready"), 1)
            else:
                TT(acc[:], xT[:, 0], xT[:, 0], MU).then_inc(sem("x_ready"), 1)

        with v.Fori(0, n_layers) as l:
            layer["l"] = l
            v.wait_ge(sem("stage_freed"), l * NU + 1)
            norm("mix")
            lbp = PR("lb").rearrange("p (a b) -> p a b", a=2)
            then(TT(lbt[:, 0], lbp[:, 0], lbp[:, 1], MX))
            TT(lbt[:, 1], lbp[:, 0], lbt[:, 0], SU).then_inc(*inc("dve")); settle()
            TT(lbt[:, 2], lbp[:, 1], lbt[:, 0], SU).then_inc(*inc("lb", "args")); settle()
            v.wait_ge(*aft("lb_exp", "e"))
            then(TT(lbt[:, 5], lbt[:, 3], lbt[:, 4], AD))
            then(V.reciprocal(lbt[:, 5], lbt[:, 5]))
            then(STT(lbt[:, 6], lbt[:, 4], col("layer", 0), lbt[:, 5], MU, MU))
            then(TS(lbt[:, 7], lbt[:, 6], -1.0, 1.0, MU, AD), "lb", "lb")

            def rope(x, n, cos, sin, t, heads, w, pre, signal, rs, tmpf):
                xh = x.rearrange("p (h f) -> p h f", h=heads)
                then(TT(xh, xh, bc(rs, 64), MU))
                then(STT(xh, xh, pre, w[:n].unsqueeze(1).to_broadcast([n, heads, 64]), MU, MU))
                x4 = x.rearrange("p (h a f) -> p h a f", h=heads, a=2)
                r4 = tmpf[:n, :heads * 64].rearrange("p (h a f) -> p h a f", h=heads, a=2)
                cb = cos.unsqueeze(1).to_broadcast([n, heads, 32])
                sb_ = sin.unsqueeze(1).to_broadcast([n, heads, 32])
                TT(r4[:, :, 0], x4[:, :, 1], sb_, MU).then_inc(*inc("dve")); settle()
                TT(r4[:, :, 1], x4[:, :, 0], sb_, MU).then_inc(*inc("dve")); settle()
                for a in range(2):
                    TT(x4[:, :, a], x4[:, :, a], cb, MU).then_inc(*inc("dve")); settle()
                v.wait_ge(*aft("dve"))
                TT(x4[:, :, 0], x4[:, :, 0], r4[:, :, 0], SU).then_inc(*inc("dve")); settle()
                TT(x4[:, :, 1], x4[:, :, 1], r4[:, :, 1], AD).then_inc(*inc(*signal)); settle()

            def head_squares(src, heads, c0, t, tag):
                then(TT(rt[:, t, :heads * 64], src, src, MU))
                V.reduce_sum(ssq[:, t, c0:c0 + heads], rt[:, t, :heads * 64].rearrange("p (h f) -> p h f", h=heads), AX)\
                    .then_inc(*inc("nsa_ss", tag if t == 3 else (tag, t))); settle()

            v.wait_ge(*aft("ev_q", "q"))
            for t in range(NT):
                head_squares(qr[:, t], 8, 0, t, "q")
            v.wait_ge(*aft("nsa_rs", "q"))
            for t in range(NT):
                rope(qr[:, t], P, C("cos")[:, t * 32:(t + 1) * 32], C("sin")[:, t * 32:(t + 1) * 32], t, 8, PR("q_norm"),
                     0.125, ("q_rot", t), rsq[:, t, 0:8], rt[:, t])
            v.wait_ge(*aft("ev_kv", "kv"))
            for t in range(NT):
                head_squares(kvr[:, t, 0:256], 4, 8, t, "k")
            v.wait_ge(*aft("dense_done", "gd"))
            V.tensor_copy(gd[:].rearrange("p a b -> p (a b)"), ps[:, 0, 0:128]).then_inc(*inc("ev_nsa", "gd")); settle()
            V.memset(kcs[:, :, :, 511:528], 0.0).then_inc(*inc("dve")); settle()
            V.memset(vcbd[:], 0.0).then_inc(*inc("dve")); settle()
            for w, name in enumerate(("kc", "vc")):
                v.wait_ge(*aft("dense_done", name))
                for g in range(2):
                    sp_ = slice(64 * g, 64 * g + 64)
                    V.tensor_copy(kcs[0:64, w, g, 0:512], ps[sp_, 1 + w, :]).then_inc(*inc("dve")); settle()
                    V.tensor_copy(kcs[64:128, w, g, 0:511], ps[sp_, 1 + w, 1:512]).then_inc(
                        *inc("ev_nsa", name if g == 1 else (name, g))); settle()
            v.wait_ge(*aft("nsa_rs", "k"))
            for t in range(NT):
                rope(kvr[:, t, 0:256], P, C("cos")[:, t * 32:(t + 1) * 32], C("sin")[:, t * 32:(t + 1) * 32], t, 4,
                     PR("k_norm"), 1.0, ("k_rot", t), rsq[:, t, 8:12], rt[:, t])
            v.wait_ge(*aft("cmp_mm", "h"))
            then(V.tensor_copy(posb[:], ps[0:64, 5, 128:130]))
            for w in range(2):
                TS(h1[:, w], ps[0:64, 5, w * 64:(w + 1) * 64], posb[:, w:w + 1], None, AD).then_inc(*inc("cmp_dve", ("pre", w))); settle()
            for w in range(2):
                v.wait_ge(*aft("cmp_th", w))
                then(TS(h1[:, 2 + w], h1[:, 2 + w], 0.5, 0.5, MU, AD))
                then(TT(h1[:, w], h1[:, w], h1[:, 2 + w], MU))
            V.tensor_copy(h1v[:], h1[:, 1].rearrange("p (g n) -> p g n", g=2).unsqueeze(2).to_broadcast([64, 2, 4, 32]))\
                .then_inc(*inc("cmp_dve", "h1")); settle()
            v.wait_ge(*aft("gate_th", "g"))
            TS(gth[:], gth[:], 0.5, 0.5, MU, AD).then_inc(*inc("dve")); settle()
            v.wait_ge(*aft("cmp_mm", "kv"))
            for r in range(4):
                rr = slice(32 * r, 32 * r + 32)
                V.tensor_copy(vcbd[rr, :, r, :], ps[rr, 5, 64:192].rearrange("p (g f) -> p g f", g=2)).then_inc(*inc("dve")); settle()
            then(V.tensor_copy(kcr[0:64, 0], ps[0:64, 5, 0:64]), "cmp_dve", "kc_raw")
            then(TT(kcr[0:64, 1], kcr[0:64, 0], kcr[0:64, 0], MU))
            V.reduce_sum(ssc[0:64, 0:1], kcr[0:64, 1], AX).then_inc(*inc("cmp_dve", "kc_ss")); settle()
            v.wait_ge(*aft("cmp_th", "rs"))
            rope(kcr[0:64, 0], 64, C("cosc")[0:64], C("sinc")[0:64], 0, 1, PR("k_norm"), 1.0,
                 ("cmp_dve", "kc_rot"), ssc[0:64, 1:2], rt[:, 0])
            for br in range(2):
                v.wait_ge(*aft("k_tr", br))
                for g in range(2):
                    for half in range(2):
                        V.tensor_copy(kT[64 * half:64 * half + 64, 2 * br + g], ps[64 * g:64 * g + 64, 4 + br]).then_inc(
                            *inc("k_trc", br if (g, half) == (1, 1) else (br, g, half))); settle()
            V.memset(kcbd[:], 0.0).then_inc(*inc("dve")); settle()
            v.wait_ge(*aft("cmp_mm", "kc_tr"))
            for half in range(2):
                V.tensor_copy(kcbd[64 * half:64 * half + 64, :, half, :],
                              ps[0:64, 6, 0:64].rearrange("p (g n) -> p g n", g=2)).then_inc(
                    *inc("cmp_dve", "kcbd" if half else "kcbd0")); settle()

            steps = [(i, br, h) for i in range(NT) for br in range(2) for h in range(8)]
            for n in range(67):
                if n < 64:
                    i, br, h = steps[n]
                    wid = (i + 1) * P
                    v.wait_ge(*aft("qk", n))
                    V.reduce_max(nmx[:, n % 2:n % 2 + 1], ps[:, 4 + n % 2, :wid], AX, negate=True).then_inc(*inc("nmax", n)); settle()
                if n % 16 == 1 and n < 64:
                    i = n // 16
                    v.wait_ge(*aft("cmp_qk", i))
                    then(TT(sc_c[:], ps[:, 0, 0:256].rearrange("p (h n) -> p h n", h=8),
                            C("maskc")[:, i * 32:(i + 1) * 32].unsqueeze(1).to_broadcast([P, 8, 32]), AD), "cmp_sc", i)
                    then(V.reduce_max(mx_c[:], sc_c[:], AX))
                    TT(sc_c[:], sc_c[:], bc(mx_c[:], 32), SU).then_inc(*inc("cmp_sub", i)); settle()
                if n % 16 == 4 and n < 64:
                    i = n // 16
                    v.wait_ge(*aft("cmp_exp", i))
                    then(V.reduce_sum(sum_c[:], sc_c[:], AX))
                    then(V.reciprocal(sum_c[:], sum_c[:]))
                    then(STT(sum_c[:], sum_c[:], C("valid")[:, i:i + 1],
                             gth[:, i].rearrange("p (h b) -> p h b", b=3)[:, :, 0], MU, MU))
                    TT(sc_c[:], sc_c[:], bc(sum_c[:], 32), MU).then_inc(*inc("cmp_p", i)); settle()
                if n % 16 == 11 and n < 64:
                    i = n // 16
                    v.wait_ge(*aft("cmp_pv", i))
                    then(TT(o_acc[:, i], o_acc[:, i], ps[:, 0], AD), "cmp_o", i)
                if n >= 1 and n <= 64 and (n - 1) % 2 == 1:
                    m = n - 1
                    wid = (steps[m][0] + 1) * P
                    v.wait_ge(*aft("ptr", m))
                    if m >= 2:
                        v.wait_ge(*aft("pv", m - 2))
                    V.tensor_copy(PTs[:, m % 2, :wid], ps[:, 3, :wid]).then_inc(*inc("ptc_dve", m)); settle()
                m = n - 2
                if m >= 0 and m < 64 and m % 8 == 7:
                    i, br, _ = steps[m]
                    b = (7, 2)[(m // 8) % 2]
                    v.wait_ge(*aft("exp", m))
                    then(V.reciprocal(coef[:], sums[:, br]))
                    then(TT(coef[:], coef[:], gth[:, i].rearrange("p (h b) -> p h b", b=3)[:, :, 1 + br], MU))
                    v.wait_ge(*aft("pv", m))
                    pso = ps[:, b].rearrange("p (h f) -> p h f", h=8)
                    if br == 0:
                        then(TT(o_acc[:, i].rearrange("p (h f) -> p h f", h=8), pso, bc(coef[:], 64), MU), "o_add", m // 8)
                    else:
                        then(TT(tmp[:, 0].rearrange("p (h f) -> p h f", h=8), pso, bc(coef[:], 64), MU))
                        then(TT(o_acc[:, i], o_acc[:, i], tmp[:, 0], AD), "o_add", m // 8)
            for c in range(4):
                v.wait_ge(*aft("yA_hi", c))
                TT(y_lo[:, c], ps[:, 4 + c], y_hi[:, c].bitcast(F32), SU).then_inc(*inc("yA_lo", c)); settle()

            def merge(which, m):
                key = f"y{which}{m // 2}.{m % 2}"
                bank = bank_of[key]
                v.wait_ge(*aft("sig_ready", f"g{which}{m}"))
                v.wait_ge(*aft("dense_done", key))
                if which == "A":
                    STT(merged[:, m], sg[:, m], 1.0, ps[:, bank], AD, MU).then_inc(*inc("merge_A", key)); settle()
                else:
                    then(STT(tmp[:, m % 2], sg[:, m], 1.0, ps[:, bank], AD, MU))
                    TT(merged[:, m], merged[:, m], tmp[:, m % 2], AD).then_inc(*inc("merge_" + which, key)); settle()

            dt_x, dt_n, dt_u, dt_w, dt_w2, dt_p = (dtb[:, k].rearrange("p (t h) -> p t h", h=8) for k in range(6))
            then(TT(dt_x, gd[:, :, 24:32], PR("dt_bias").unsqueeze(1).to_broadcast([P, NT, 8]), AD))
            then(TS(dt_n, dt_x, -1.0, None, MU))
            then(TT(dt_n, dt_x, dt_n, ALU.min), "dt", "nabs")
            for m in range(8):
                merge("A", m)

            V.memset(xr[:, :, 0:3], 0.0).then_inc(*inc("dve")); settle()
            v.wait_ge(*aft("dt_act", "u"))
            then(TS(dt_w, dt_u, 2.0, None, AD))
            then(V.reciprocal(dt_w, dt_w))
            then(TT(dt_w, dt_w, dt_u, MU))
            then(TT(dt_w2, dt_w, dt_w, MU))
            then(TS(dt_p, dt_w2, 1.0 / 17, None, MU))
            for k in (15, 13, 11, 9, 7, 5, 3):
                then(STT(dt_p, dt_p, 1.0 / k, dt_w2, AD, MU))
            then(STT(dt_p, dt_p, 1.0, dt_w, AD, MU))
            then(TS(dt_x, dt_x, 0.0, None, MX))
            then(STT(dt_x, dt_p, 2.0, dt_x, MU, AD))
            v.wait_ge(*aft("dt_act", "a"))
            then(STT(da[:], dt_x, -1.0, aexp[:].unsqueeze(1).to_broadcast([P, NT, 8]), MU, MU), "dt", "da")
            then(TS(dth[:], dt_x, 0.5, None, MU))
            then(TS(dsk[:], PR("ssm_d"), 0.5, None, MU))
            for c in range(6):
                v.wait_ge(*aft("xbc_ev", f"xbc{c}"))
                w = PC["conv_w"][0] + 4 * c
                then(TS(cv[:, c], xr[:, c, 3:515], prm[:, w + 3:w + 4], col("conv_b", c), MU, AD))
                for k in (2, 1, 0):
                    ins = STT(cv[:, c], xr[:, c, k:k + 512], prm[:, w + k:w + k + 1], cv[:, c], MU, AD)
                    if k:
                        then(ins)
                    else:
                        ins.then_inc(*inc("conv_raw", c)); settle()
                v.wait_ge(*aft("conv_th", c - 1)) if c else None
                if c:
                    STT(cv[:, c - 1], tmp[:, (c - 1) % 2], 1.0, cv[:, c - 1], AD, MU).then_inc(*inc("conv", c - 1)); settle()
            v.wait_ge(*aft("conv_th", 5))
            STT(cv[:, 5], tmp[:, 1], 1.0, cv[:, 5], AD, MU).then_inc(*inc("conv", 5)); settle()
            for t in range(NT):
                v.wait_ge(*aft("z_th", t))
                STT(zs[:, t], zs[:, t], 1.0, ps[:, t], AD, MU).then_inc(*inc("z_ev", "z" if t == 3 else ("z", t))); settle()
            v.wait_ge(*aft("acum", "a"))
            pa = ps[:, 4, 0:32].rearrange("p (t h) -> p t h", h=8)
            pl = ps[:, 4, 32:64].rearrange("p (t h) -> p t h", h=8)
            V.tensor_copy(eac[:], pa).then_inc(*inc("dve")); settle()
            then(V.tensor_copy(edec[:], pl))
            then(TT(dend[:], edec[:], eac[:], SU))
            TS(nac[:], eac[:], -1.0, None, MU).then_inc(*inc("dt", "args")); settle()
            v.wait_ge(*aft("dt_act", "dend"))
            then(TS(eac[:], eac[:], 0.25, None, MU))
            for t in range(NT):
                v.wait_ge(*aft("xs_ev", t))
                TT(xdt[:, t].rearrange("p (h f) -> p h f", h=8), xs[:, t].rearrange("p (h f) -> p h f", h=8),
                   bc(dth[:, t], 64), MU).then_inc(*inc("xdt", t)); settle()
            v.wait_ge(*aft("xdt", 3))
            for t in range(NT):
                if t < NT - 1:
                    if t:
                        v.wait_ge(*aft("st", t - 1))
                    TT(xe[:].rearrange("p (h f) -> p h f", h=8), xdt[:, t].rearrange("p (h f) -> p h f", h=8),
                       bc(dend[:, t], 64), MU).then_inc(*inc("ssd_xe", t)); settle()
                v.wait_ge(*aft("cb", t))
                for g in range(2):
                    v.wait_ge(*aft("ssd_dec", (t, g)))
                    STT(dec[:, g], ps[:, 5 + 2 * g, 0:P].unsqueeze(1).to_broadcast([P, 4, P]), 0.25, dec[:, g],
                        MU, MU).then_inc(*inc("ssd_m", (t, g))); settle()
                y8 = ssd_y[:, t].rearrange("p (h f) -> p h f", h=8)
                then(TT(y8, xs[:, t].rearrange("p (h f) -> p h f", h=8), bc(dsk[:], 64), MU))
                v.wait_ge(*aft("ydiag", (t, 1)))
                ins = TT(ssd_y[:, t], ssd_y[:, t], ps[:, 4], AD)
                if t == 0:
                    then(ins, "ssd_y", t)
                else:
                    then(ins)
                    v.wait_ge(*aft("yoff", t))
                    for g in range(2):
                        then(TT(tmp[:, 0, g * 256:(g + 1) * 256].rearrange("p (h f) -> p h f", h=4),
                                ps[:, 5 + 2 * g, 256:512].rearrange("p (h f) -> p h f", h=4),
                                bc(eac[:, t, 4 * g:4 * g + 4], 64), MU), "ssd_y", t if g else (t, 0))
                    then(TT(ssd_y[:, t], ssd_y[:, t], tmp[:, 0], AD))
                if t < NT - 1:
                    v.wait_ge(*aft("st", t))
                    for g in range(2):
                        gp = slice(64 * g, 64 * g + 64)
                        src = ps[gp, 6, g * 256:(g + 1) * 256]
                        key = t if g == 1 else (t, 0)
                        if t == 0:
                            V.tensor_copy(hst[gp], src).then_inc(*inc("ssd_st", key)); settle()
                        else:
                            then(TT(hst[gp].rearrange("p (h f) -> p h f", h=4), hst[gp].rearrange("p (h f) -> p h f", h=4),
                                    bc(edec[gp, t, 4 * g:4 * g + 4], 64), MU))
                            TT(hst[gp], hst[gp], src, AD).then_inc(*inc("ssd_st", key)); settle()
                then(TT(ssd_y[:, t], ssd_y[:, t], zs[:, t], MU))
                then(TT(tmp[:, 1], ssd_y[:, t], ssd_y[:, t], MU))
                V.reduce_sum(ssy[:, t], tmp[:, 1].rearrange("p (g f) -> p g f", g=2), AX).then_inc(*inc("ssd_ss", t)); settle()
            v.wait_ge(*aft("ssd_rs", "rs"))
            for t in range(NT):
                y2 = ssd_y[:, t].rearrange("p (g f) -> p g f", g=2)
                STT(y2, y2, 0.5, bc(ssy[:, t], 256), MU, MU).then_inc(*inc("ssd_yn", t)); settle()

            def y_t(c):
                v.wait_ge(*aft("y_tr", c))
                TS(tmp[:, c % 2], ps[:, 4 + c], col("ssm_norm", c), None, MU).then_inc(*inc("yB_t", c)); settle()

            v.wait_ge(*aft("y_tr", 3))
            y_t(0)
            for c in range(4):
                if c < 3:
                    y_t(c + 1)
                v.wait_ge(*aft("yB_hi", c))
                TT(y_lo[:, c], tmp[:, c % 2], y_hi[:, c].bitcast(F32), SU).then_inc(*inc("yB_lo", c)); settle()
            for m in range(8):
                merge("B", m)

            V.memset(hKT[:], 0.0).then_inc(*inc("dve")); settle()
            for m in range(4):
                v.wait_ge(*aft("hf_ev", f"hf{m}"))
                TS(hk[:, m], hk[:, m], lbt[:, 7, m:m + 1], None, MU).then_inc(*inc("dve")); settle()
            then(V.memset(hQ[:], 1.0))
            then(V.memset(hQ[:, 0:S:64], 0.0))
            for m in range(4):
                v.wait_ge(*aft("hf_ln", m))
                then(V.tensor_tensor_scan(hb[:, m], hQ[:], hb[:, m], 0.0, MU, AD), "hb", m)
            for m in range(4):
                v.wait_ge(*aft("hq_th", m))
                STT(hq[:, m], hq[:, m], 1.0, ps[:, bank_of[f"hq{m}"]], AD, MU).then_inc(*inc("hq_ev", f"hq{m}")); settle()

            def hg_ev(m):
                v.wait_ge(*aft("hg_th", m))
                STT(hgt[:, m], hgt[:, m], 1.0, ps[:, bank_of[f"hg{m}"]], AD, MU).then_inc(*inc("hg_ev", f"hg{m}")); settle()

            qs = 0.5 * mq
            for hd in range(4):
                b8 = hb[:, hd].rearrange("p (c s) -> p c s", c=8)
                b32 = hb[:, hd].rearrange("p (c s) -> p c s", c=32)
                mid = b32[:, :, 8]
                if hd:
                    v.wait_ge(*aft("hg_qb", hd - 1))
                TT(het[:].rearrange("p (c s) -> p c s", c=32), b32, bc(mid, 16), SU).then_inc(*inc("hg_arg", (hd, "q"))); settle()
                if hd:
                    v.wait_ge(*aft("hg_att", hd - 1))
                for T in range(4):
                    w = 16 * (T + 1)
                    midT = hb[:, hd, 16 * T + 8:16 * T + 8 + 449:64]
                    TT(hKT[:, T, :, :w], bc(midT, w), b8[:, :, :w], SU).then_inc(
                        *inc("hg_arg", (hd, "kt") if T == 3 else (hd, "kt", T))); settle()
                v.wait_ge(*aft("hg_ex", (hd, "q")))
                STT(hQ[:], hq[:, hd], qs, het[:], MU, MU).then_inc(*inc("hg_q", hd)); settle()
                if hd:
                    v.wait_ge(*aft("hg_ke", hd - 1))
                TT(tmp[:, 0].rearrange("p (c s) -> p c s", c=8), bc(b8[:, :, 63], 64), b8, SU).then_inc(*inc("hg_arg", (hd, "e"))); settle()
                for T in range(4):
                    w = 16 * (T + 1)
                    v.wait_ge(*aft("hg_ex", (hd, "kt", T)))
                    TT(hKT[:, T, :, :w], hKT[:, T, :, :w], hk[:, hd].rearrange("p (c s) -> p c s", c=8)[:, :, :w], MU).then_inc(
                        *inc("hg_kt", hd if T == 3 else (hd, T))); settle()
                v.wait_ge(*aft("hg_ex", (hd, "b")))
                STT(hq[:, hd], hq[:, hd], qs, het[:], MU, MU).then_inc(*inc("hg_qb", hd)); settle()
                v.wait_ge(*aft("hg_ex", (hd, "e")))
                TT(hk[:, hd], hk[:, hd], tmp[:, 0], MU).then_inc(*inc("hg_ke", hd)); settle()
                for name in HG[hd]:
                    if name[0] == "h":
                        hg_ev(int(name[2:]))
                v.wait_ge(*aft("hg_att", hd))
                TT(hatt[:, hd], ps[:, 4, 0:256].rearrange("p (a b) -> p a b", a=4),
                   C("hgmask").unsqueeze(1).to_broadcast([P, 4, 64]), MU).then_inc(*inc("hg_attm", hd)); settle()
            v.wait_ge(*aft("hg_ex", (3, "l")))
            for c in range(7):
                v.wait_ge(*aft("hg_st", c))
                v.wait_ge(*aft("hg_o", c))
                for hd in range(4):
                    src = ps[:, c % 2, hd * P:(hd + 1) * P]
                    sig = inc("hg_state", c if hd == 3 else (c, hd))
                    if c == 0:
                        V.tensor_copy(hst2[:, hd], src).then_inc(*sig); settle()
                    else:
                        if hd == 0:
                            v.wait_ge(*aft("hg_state", c - 1))
                        STT(hst2[:, hd], hst2[:, hd], eblast[:, hd, c:c + 1], src, MU, AD).then_inc(*sig); settle()
            def yc(hd):
                v.wait_ge(*aft("hg_rs", hd))
                then(STT(hk[:, hd], ps[:, 4 + hd], col("hg_norm", 0), hk[:, hd], MU, MU))
                STT(tmp[:, hd % 2], hk[:, hd], 0.5, hgt[:, hd], MU, MU).then_inc(*inc("yC_t", hd)); settle()

            yc(0)
            for hd in range(4):
                if hd < 3:
                    yc(hd + 1)
                v.wait_ge(*aft("yC_hi", hd))
                TT(y_lo[:, hd], tmp[:, hd % 2], y_hi[:, hd].bitcast(F32), SU).then_inc(*inc("yC_lo", hd)); settle()
            for m in range(9):
                if m < 8:
                    merge("C", m)
                if m:
                    v.wait_ge(*aft("merged_hi", m - 1))
                    STT(h_lo[:, m - 1], merged[:, m - 1], 0.5, h_hi[:, m - 1].bitcast(F32), MU, SU)\
                        .then_inc(*inc("merged_lo", m - 1)); settle()
            v.wait_ge(*aft("mem_loaded", "m"))
            then(TT(macc[:], mraw[:, 0], mraw[:, 0], MU))
            for k in range(1, KC):
                then(TT(mt[:, 0], mraw[:, k], mraw[:, k], MU))
                then(TT(macc[:], macc[:], mt[:, 0], AD), *(("mem_acc", "m") if k == KC - 1 else ("dve",)))

            def m_t(k):
                STT(mt[:, k % 2], mraw[:, k], col("norm_mem", k), mr[:], MU, MU).then_inc(*inc("mem_t", k)); settle()

            for m in range(8):
                residual(bank_of[f"o{m}"], m, "res_o", f"o{m}", True)
                if m == 2:
                    v.wait_ge(*aft("mem_rstd", "m"))
                    m_t(0)
                    for k in range(KC):
                        if k + 1 < KC:
                            m_t(k + 1)
                        v.wait_ge(*aft("mem_hi", k))
                        TT(m_lo[:, k], mt[:, k % 2], m_hi[:, k].bitcast(F32), SU).then_inc(*inc("mem_lo", k)); settle()
            norm("xa")
            v.wait_ge(*aft("x_rs", "k"))
            STT(kx[:], ps[:, 0:2].rearrange("p a (b n) -> p (a b) n", b=2), col("xa_k", 0), rsx[:, :, :MEM], MU, MU)\
                .then_inc(*inc("xk_ev", "k")); settle()
            for m in range(4):
                v.wait_ge(*aft("x_rs", f"xq{m}"))
                STT(qx[:, m], ps[:, bank_of[f"xq{m}"]], col("xa_q", 0), rsx[:, m], MU, MU).then_inc(*inc("xq_ev", f"xq{m}")); settle()

            def x_max(hd):
                v.wait_ge(*aft("xqk", hd))
                b = 4 + 2 * (hd % 2)
                then(V.reduce_max(nbx[:, hd % 2], ps[:, b:b + 2].rearrange("p a (b n) -> p (a b) n", b=2), AX, negate=True))
                TS(nbx[:, hd % 2], nbx[:, hd % 2], mq, None, MU).then_inc(*inc("xnb", hd)); settle()

            x_max(0)
            x_max(1)
            for hd in range(4):
                v.wait_ge(*aft("xexp", hd))
                then(V.reciprocal(smx[:, hd % 2], smx[:, hd % 2]))
                TT(px[:, hd % 2], px[:, hd % 2], bc(smx[:, hd % 2], MEM), MU).then_inc(*inc("xpn", hd)); settle()
                v.wait_ge(*aft("xptr", (hd, 1)))
                if hd >= 2:
                    v.wait_ge(*aft("xpv", hd - 2))
                V.tensor_copy(ptx[:, hd % 2, 1], ps[:, 1]).then_inc(*inc("xptd", hd)); settle()
                if hd < 2:
                    x_max(hd + 2)
                v.wait_ge(*aft("xo_hi", hd))
                TT(y_lo[:, hd], ps[:, 2 + hd % 2], y_hi[:, hd].bitcast(F32), SU).then_inc(*inc("xo_lo", hd)); settle()
            for m in range(8):
                residual(m % 4, m, "res_xo", f"xo{m // 2}.{m % 2}", True)
            norm("ffn")
            j = 0
            for p, n in enumerate(FFN_PASSES):
                def lo(c, j):
                    v.wait_ge(*aft("ffn_hi", j))
                    TT(a_lo[:, c], ft[:, j % 2], a_hi[:, c].bitcast(F32), SU).then_inc(*inc(f"ffn_lo{p}", c)); settle()
                for c in range(n):
                    v.wait_ge(*aft("ffn_s", f"fg{p}_{c}"))
                    v.wait_ge(*aft("dense_done", f"fu{p}_{c}"))
                    TT(ft[:, j % 2], sl[:, j % 2], ps[:, bank_of[f"fu{p}_{c}"]], MU).then_inc(*inc("ffn_t", f"fu{p}_{c}")); settle()
                    lo(c, j)
                    j += 1
                for m in range(8):
                    bank = bank_of[f"fd{p}_{m}"]
                    if p < 2:
                        residual(bank, m, f"res_f{p}", f"fd{p}_{m}", False)
                    else:
                        v.wait_ge(*aft("dense_done", f"fd2_{m}"))
                        then(TT(xT[:, m], xT[:, m], ps[:, bank], AD), "res_f2", f"fd2_{m}")
                        squares(m, None)
    ctx.close()
    return {"count": count, "marks": marks}


SPLIT = (("q", 512), ("kc", 128), ("vc", 128), ("ks", 128), ("vs", 128), ("kw", 128), ("vw", 128), ("gate", 24),
         ("z", 512), ("xbc", 768), ("dt", 8), ("hq", 512), ("hf", 512), ("hi", 512), ("hg", 512),
         ("gA", 1024), ("gB", 1024), ("gC", 1024))


def constants():
    c = np.zeros((P, NCST), np.float32)

    def put(name, a):
        c[:a.shape[0], CC[name][0]:CC[name][1]] = a

    p, f = np.arange(P)[:, None], np.arange(P)[None, :]
    put("ident", np.eye(P))
    put("triu", (p <= f) * 1.0)
    put("ones", np.ones((P, P)))
    put("maskq", np.where(f > p, NEG, 0.0))
    put("maskt", np.where(f < p, NEG, 0.0))
    put("hgmask", (np.arange(64)[None, :] >= p % 64) * 1.0)
    inv = np.float32(1.0) / (np.float32(10000.0) ** (np.arange(32, dtype=np.float32) / np.float32(32)))
    ang = np.arange(S, dtype=np.float32)[:, None] * inv[None, :]
    put("cos", np.cos(ang).reshape(NT, P, 32).transpose(1, 0, 2).reshape(P, NT * 32))
    put("sin", np.sin(ang).reshape(NT, P, 32).transpose(1, 0, 2).reshape(P, NT * 32))
    posc = (np.arange(64) % 32 * 16 + 31).astype(np.float32)
    put("cosc", np.cos(posc[:, None] * inv[None, :]))
    put("sinc", np.sin(posc[:, None] * inv[None, :]))
    t = np.arange(NT)[None, :, None] * P + np.arange(P)[:, None, None]
    put("maskc", np.where(16 * np.arange(32)[None, None, :] + 31 <= t, 0.0, NEG).reshape(P, NT * 32))
    put("valid", (t[:, :, 0] >= 31) * 1.0)
    put("eps", np.full((P, 1), EPS))
    return c


def pack(i):
    w = np.zeros((DEPTH, NU, P, UNIT), np.float32)
    at, c = {}, 0
    for name, n in SPLIT:
        at[name] = slice(c, c + n)
        c += n
    for l in range(DEPTH):
        win = i["w_in"][l]
        kv = np.concatenate([win[:, at[n]] for n in ("ks", "kw", "vs", "vw")], axis=1)
        gd = np.concatenate([win[:, at["gate"]], win[:, at["dt"]]], axis=1)

        def t_units(name, m):
            u = UNIT_OF[name]
            w[l, u:u + 4] = m.reshape(4, 2, P, 512).transpose(0, 2, 1, 3).reshape(4, P, UNIT)

        def f_units(name, m):
            nk, n = m.shape[0] // P, m.shape[1] // P
            m = m.reshape(nk, P, n, P).transpose(2, 1, 0, 3).reshape(n, P, nk * P)
            for o in range(n):
                w[l, UNIT_OF[name.format(o)], :, :nk * P] = m[o]

        def h_units(name, m):
            m = m.reshape(4, P, 4, 2, P).transpose(2, 1, 3, 0, 4).reshape(4, P, UNIT)
            for o in range(4):
                w[l, UNIT_OF[name.format(o)]] = m[o]

        t_units("q", win[:, at["q"]])
        t_units("kv", kv)
        t_units("z", win[:, at["z"]])
        t_units("hv", win[:, at["hi"]])
        t_units("xv", i["xa_w_v"][l])
        w[l, UNIT_OF["gd"], :, :256] = gd.reshape(KC, P, 32).transpose(1, 0, 2).reshape(P, 256)
        for n in ("kc", "vc"):
            f_units(n, win[:, at[n]])
        for n, a in (("xbc{}", "xbc"), ("hf{}", "hf"), ("hq{}", "hq"), ("hg{}", "hg"), ("gA{}", "gA"), ("gB{}", "gB"),
                     ("gC{}", "gC")):
            f_units(n, win[:, at[a]])
        for n, a in (("w1k", "nsa_cmp_w1_k"), ("w1v", "nsa_cmp_w1_v")):
            w[l, UNIT_OF[n]] = i[a][l].reshape(16, P, 64).transpose(1, 0, 2).reshape(P, UNIT)
        for n, a in (("yA{}", "w_nsa_o"), ("yB{}", "w_ssm_o"), ("yC{}", "w_hg_o"), ("xo{}", "xa_w_o")):
            h_units(n, i[a][l])
        f_units("o{}", i["w_out"][l])
        f_units("xk{}", i["xa_w_k"][l])
        f_units("xq{}", i["xa_w_q"][l])
        c0 = 0
        for p, n in enumerate(FFN_PASSES):
            cols = slice(c0 * P, (c0 + n) * P)
            f_units(f"fg{p}_{{}}", i["ffn_w_gate"][l][:, cols])
            f_units(f"fu{p}_{{}}", i["ffn_w_up"][l][:, cols])
            f_units(f"fd{p}_{{}}", i["ffn_w_down"][l][cols])
            c0 += n
        prm = w[l, 0]

        def put(name, a):
            prm[:a.shape[0], PC[name][0]:PC[name][1]] = a

        for n in ("norm_mix", "norm_xa", "norm_mem", "norm_ffn"):
            put(n, i[n][l].reshape(KC, P).T)
        put("conv_w", i["ssm_conv_w"][l].reshape(4, 6, P).transpose(2, 1, 0).reshape(P, 24))
        put("conv_b", i["ssm_conv_b"][l].reshape(6, P).T)
        put("lb", i["hg_lb_logits"].reshape(DEPTH * 4, P).T)
        put("hg_norm", i["hg_norm"][l][:, None])
        put("xa_q", i["xa_q_norm"][l][:, None])
        put("xa_k", i["xa_k_norm"][l][:, None])
        put("ssm_norm", i["ssm_norm"][l].reshape(4, P).T)
        for n, a in (("q_norm", "nsa_q_norm"), ("k_norm", "nsa_k_norm"), ("dt_bias", "ssm_dt_bias"),
                     ("a_log", "ssm_a_log"), ("ssm_d", "ssm_d")):
            put(n, np.broadcast_to(i[a][l][None, :], (P, i[a].shape[-1])))
        put("pos_k", i["nsa_cmp_pos_k"][l].reshape(16, P).T)
        put("pos_v", i["nsa_cmp_pos_v"][l].reshape(16, P).T)
        put("w2k", i["nsa_cmp_w2_k"][l])
        put("w2v", i["nsa_cmp_w2_v"][l])
        put("layer", np.full((P, 1), float(l), np.float32))
    return w.reshape(DEPTH * NU, P, UNIT)


def program(nc, totals=None, n_layers=DEPTH):
    nc.disable_value_cache = True
    x = nc.dram_tensor("x_in", [P, KC, S], F32, kind="ExternalInput").ap()
    mem = nc.dram_tensor("mem_in", [P, KC, MEM], F32, kind="ExternalInput").ap()
    w = nc.dram_tensor("w_in_units", [DEPTH * NU, P, UNIT], F32, kind="ExternalInput").ap()
    cst = nc.dram_tensor("constants", [P, NCST], F32, kind="ExternalInput").ap()
    out = nc.dram_tensor("out", [P, KC, S], F32, kind="ExternalOutput").ap()
    return build(nc, x, mem, w, cst, out, totals, n_layers)


def kernel(**inputs):
    import concourse.bacc as bacc
    from concourse.bass_utils import run_bass_kernel_spmd
    i = {k: np.asarray(a) for k, a in inputs.items()}
    x = np.ascontiguousarray(i["x"][0].reshape(S, KC, P).transpose(2, 1, 0))
    mem = np.ascontiguousarray(i["mem"][0].reshape(MEM, KC, P).transpose(2, 1, 0))
    totals = program(bacc.Bacc("TRN2", target_bir_lowering=False, num_devices=1))
    nc = bacc.Bacc("TRN2", target_bir_lowering=False, num_devices=1)
    program(nc, totals)
    r = run_bass_kernel_spmd(nc, [{"x_in": x, "mem_in": mem, "w_in_units": pack(i), "constants": constants()}],
                             core_ids=[0])
    o = np.asarray(r.results[0]["out"])
    return np.ascontiguousarray(o.transpose(2, 1, 0)).reshape(1, S, D)
```

```python
import numpy as np
import concourse.bass as bass
from concourse import mybir
from contextlib import ExitStack

F32, F32R, BF16 = mybir.dt.float32, mybir.dt.float32r, mybir.dt.bfloat16
ACT, ALU = mybir.ActivationFunctionType, mybir.AluOpType
AX = mybir.AxisListType.X

DEPTH, D, S, MEM = 2, 1024, 512, 256
GB = ((0,), (1,), (2,), (3,), (4,), (5, 6, 7))
HG = (("hg0", "hg1"), ("hg2",), ("hg3",), ("gC0",), ("gC5", "gC6", "gC7"),
      {0: ("gC1",), 2: ("gC2",), 4: ("gC3",), 6: ("gC4",)})
P = 128
KC = D // P
NT = S // P
EPS = 1e-6
NEG = -float(2 ** 100)
SCORE_BANKS = (4, 5, 1)
FFN_PASSES = (8, 8, 6)
SLOTS = 4
UNIT = 1024

PLAN = ([("params", 1), ("q", 4), ("kv", 4), ("gd", 1), ("kc", 1), ("vc", 1), ("w1k", 1), ("w1v", 1)]
        + [(f"gA{m}", 1) for m in range(8)] + [("xbc0", 1)] + [(f"yA{m}", 1) for m in range(4)]
        + [(f"xbc{m}", 1) for m in range(1, 6)] + [("z", 4)]
        + [(f"gB{m}", 1) for m in range(8)] + [(f"yB{m}", 1) for m in range(4)]
        + [(f"hf{m}", 1) for m in range(4)] + [(f"hq{m}", 1) for m in range(4)] + [("hv", 4)]
        + [(f"hg{m}", 1) for m in range(4)]
        + [(f"gC{m}", 1) for m in range(8)] + [(f"yC{m}", 1) for m in range(4)]
        + [(f"o{m}", 1) for m in range(8)]
        + [(f"xk{m}", 1) for m in range(4)] + [("xv", 4)]
        + [(f"xq{m}", 1) for m in range(4)] + [(f"xo{m}", 1) for m in range(4)])
for _p, _n in enumerate(FFN_PASSES):
    for _c in range(_n):
        PLAN += [(f"fg{_p}_{_c}", 1), (f"fu{_p}_{_c}", 1)]
    PLAN += [(f"fd{_p}_{m}", 1) for m in range(8)]
UNIT_OF, NU = {}, 0
for _name, _n in PLAN:
    UNIT_OF[_name] = NU
    NU += _n
assert NU % SLOTS == 0, NU
COPIED = ("params", "w1k", "w1v")
COPIED_U = {UNIT_OF[n]: n for n in COPIED}

PC, _c = {}, 0
for _name, _n in (("norm_mix", 8), ("norm_xa", 8), ("norm_mem", 8), ("norm_ffn", 8), ("conv_w", 24), ("conv_b", 6),
                  ("lb", 8), ("hg_norm", 1), ("xa_q", 1), ("xa_k", 1), ("ssm_norm", 4), ("q_norm", 64),
                  ("k_norm", 64), ("dt_bias", 8), ("a_log", 8), ("ssm_d", 8), ("pos_k", 16), ("pos_v", 16),
                  ("w2k", 64), ("w2v", 64), ("layer", 1)):
    PC[_name] = (_c, _c + _n)
    _c += _n
NPRM = _c

CC, _c = {}, 0
for _name, _n in (("ident", 128), ("triu", 128), ("ones", 128), ("maskq", 128), ("maskt", 128), ("hgmask", 64),
                  ("cos", 128), ("sin", 128), ("cosc", 32), ("sinc", 32), ("maskc", 128), ("valid", 4), ("eps", 1)):
    CC[_name] = (_c, _c + _n)
    _c += _n
NCST = _c


SHARED = {name: s for s, names in {
    "y_hi": ("yA_hi", "yB_hi", "yC_hi", "xo_hi"), "y_lo": ("yA_lo", "yB_lo", "yC_lo", "xo_lo"),
    "y_scaled": ("yB_t", "yC_t"), "merged": ("merge_A", "merge_B", "merge_C"),
    "residual": ("res_o", "res_o_x", "res_xo", "res_xo_x", "res_f0", "res_f1", "res_f2"),
    "h_lo": ("h_mix", "h_xa", "h_ffn"), "ffn_lo": ("ffn_lo0", "ffn_lo1", "ffn_lo2"),
    "compress_pe": ("cmp_mm", "cmp_qk", "cmp_tr", "cmp_pv"),
    "compress_dve": ("cmp_dve", "cmp_sc", "cmp_sub", "cmp_p", "cmp_o"),
    "compress_act": ("cmp_th", "cmp_exp", "cmp_ptc"),
    "ssd_pe": ("acum", "xs_tr", "cb", "seg", "ydiag", "yoff", "st"),
    "ssd_dve": ("dt", "conv_raw", "conv", "xdt", "ssd_xe", "ssd_m", "ssd_y", "ssd_st", "ssd_ss", "ssd_yn"),
    "ssd_act": ("dt_act", "z_th", "conv_th", "xs_ev", "bt_ev", "ssd_dec", "ssd_rs"),
    "hgrn_pe": ("hg_att", "hg_ketr", "hg_st", "hg_o", "hg_ss"),
    "hgrn_dve": ("lb", "hb", "hq_ev", "hg_ev", "hg_arg", "hg_q", "hg_kt", "hg_qb", "hg_ke", "hg_attm", "hg_state"),
    "hgrn_act": ("lb_exp", "hf_s", "hf_ev", "hf_ln", "hq_th", "hg_th", "hg_ex", "hg_ket", "hg_sq", "hg_rs"),
    "cross_pe": ("x_ss", "xqk", "xptr", "xpv"), "cross_act": ("x_sq", "x_rs", "xexp", "xptc", "xv_ev"),
    "cross_dve": ("xk_ev", "xq_ev", "xnb", "xpn", "xptd", "xrq"),
}.items() for name in names}


def build(nc, x_d, mem_d, w_d, cst_d, out_d, totals, n_layers=DEPTH):
    count, marks = {}, {}
    ctx = ExitStack()
    sems = {}

    def sem(name):
        if name not in sems:
            sems[name] = ctx.enter_context(nc.semaphore("s_" + name))
        return sems[name]

    layer, recent = {"l": 0}, [None]

    def inc(name, mark=None, by=1):
        recent[0] = name
        s = SHARED.get(name, name)
        count[s] = count.get(s, 0) + by
        if mark is not None:
            assert (name, mark) not in marks, (name, mark)
            marks[name, mark] = count[s]
        return sem(s), by

    def aft(name, mark=None):
        s = SHARED.get(name, name)
        if mark is None:
            n = count[s]
        elif totals is None:
            n = 1
        else:
            n = totals["marks"][name, mark]
        per_layer = 1 if totals is None else totals["count"][s]
        return sem(s), layer["l"] * per_layer + n

    for name in ([] if totals is None else sorted(totals["count"])):
        sem(name)

    base = -(-nc.sbuf_base // 64) * 64
    end = nc.sbuf_usable_end
    top = [base]

    def place(name, shape, dt=F32, at=None):
        size = int(np.prod(shape[1:])) * (2 if dt == BF16 else 4)
        size = -(-size // 32) * 32
        off = top[0] if at is None else at
        if at is None:
            top[0] += size
        assert off + size <= end, (name, off + size - end)
        return nc.alloc_sbuf_tensor_at(name, list(shape), dt, offset=off)

    xT = place("xT", [P, KC, S])
    h_hi, h_lo = place("h_hi", [P, KC, S], F32R), place("h_lo", [P, KC, S], F32R)
    stage = place("stage", [P, SLOTS, UNIT])
    w_hi, w_lo = place("w_hi", [P, SLOTS, UNIT], F32R), place("w_lo", [P, SLOTS, UNIT], F32R)
    cst = place("cst", [P, NCST])
    identb, maskqb, masktb = (place(n, [P, P], BF16) for n in ("identb", "maskqb", "masktb"))
    prm = place("prm", [P, NPRM])
    rstd, acc = place("rstd", [P, S]), place("acc", [P, S])
    tmp = place("tmp", [P, 2, S])
    region = top[0]

    def C(name):
        return cst[:, CC[name][0]:CC[name][1]]

    def PR(name, i=0, n=None):
        a, b = PC[name]
        return prm[:, a + i:(a + i + n if n else b)]

    def col(name, i):
        return prm[:, PC[name][0] + i:PC[name][0] + i + 1]

    ident, triu, ones = C("ident"), C("triu"), C("ones")
    epsc = C("eps")

    merged = place("merged", [P, KC, S])
    w1 = place("w1", [P, 2, UNIT], at=region)
    sg_at = top[0]
    sg = place("sg", [P, KC, S])
    y_at = top[0]
    y_hi, y_lo = place("y_hi", [P, 4, S], F32R), place("y_lo", [P, 4, S], F32R)
    scratch = top[0]

    def row(start):
        at = [start]

        def take(name, shape, dt=F32):
            t = place(name, shape, dt, at=at[0])
            at[0] += -(-int(np.prod(shape[1:])) * (2 if dt == BF16 else 4) // 32) * 32
            return t
        return take

    t_ = row(scratch)
    qr = t_("qr", [P, NT, S])
    kvr = t_("kvr", [P, NT, S])
    rt = t_("rt", [P, NT, S])
    qk_at = scratch + 3 * 4 * NT * S
    qsq, ksq = t_("qsq", [P, NT, S]), t_("ksq", [P, NT, S])
    qT = place("qT", [P, 8, S], F32R, at=qk_at)
    k_hi = place("k_hi", [P, 4, S], F32R, at=scratch)
    k_lo = place("k_lo", [P, 4, S], F32R, at=region)
    o_acc = rt
    gd = t_("gd", [P, NT, 32])
    kcs = place("kcs", [P, 2, 2, 544], at=y_at)
    t_ = row(y_at)
    Pb = t_("Pb", [P, 3, S])
    PTs = t_("PTs", [P, 3, S])
    kcbd = t_("kcbd", [P, 2, 32])
    vcbd = t_("vcbd", [P, 2, 4, 64])
    kcr = t_("kcr", [P, 2, 64])
    h1 = place("h1", [64, 4, 64], at=y_at + 8704)
    h1v = place("h1v", [64, 2, 4, 32], at=y_at + 9728)
    posb = t_("posb", [64, 2])
    ptc = t_("ptc", [P, 256])
    gdT = place("gdT", [P, S], at=sg_at)
    small = (end - 5120) // 64 * 64
    t_ = row(small)
    ssq = t_("ssq", [P, NT, 12])
    rsq = t_("rsq", [P, NT, 12])
    ssc = t_("ssc", [P, 2])
    sc_c = t_("sc_c", [P, 8, 32])
    mx_c = t_("mx_c", [P, 8])
    sum_c = t_("sum_c", [P, 8])
    nmx = t_("nmx", [P, 3])
    sums = t_("sums", [P, 2, 8])
    coef = t_("coef", [P, 8])
    gth = t_("gth", [P, NT, 24])
    dtb = t_("dtb", [P, 6, 32])
    da, nac, eac, edec, dend, dth = (t_(n, [P, NT, 8]) for n in ("da", "nac", "eac", "edec", "dend", "dth"))
    aexp = t_("aexp", [P, 8])
    dsk = t_("dsk", [P, 8])
    ssy = t_("ssy", [P, NT, 2])
    lbt = t_("lbt", [P, 8, 4])
    eblast = t_("eblast", [P, 4, 8])
    warm = t_("warm", [P, 1])
    pool_mark = t_("pool_mark", [P, 4])

    t_ = row(scratch)
    xr = t_("xr", [P, 6, S + 3])
    xdt = place("xdt", [P, NT, S], at=scratch)
    cv = t_("cv", [P, 6, S])
    xs = t_("xs", [P, NT, S])
    zs = t_("zs", [P, NT, S])
    Bt = t_("Bt", [P, NT, P])
    assert scratch + 4 * (6 * 515 + 6 * 512 + 8 * 512 + 4 * 128) <= small
    t_ = row(y_at)
    dec = t_("dec", [P, 2, 4, P])
    xe = t_("xe", [P, S])
    ssd_state = t_("ssd_state", [P, 256])
    ssd_y = place("ssd_y", [P, NT, S], at=y_at + 8192)

    t_ = row(scratch)
    hq, hk, hb, hgt, hv = (t_(n, [P, 4, S]) for n in ("hq", "hk", "hb", "hgt", "hv"))
    hQ = t_("hQ", [P, S])
    hKT = place("hKT", [P, 4, 8, 64], at=y_at)
    assert scratch + 4 * 21 * S <= small
    t_ = row(y_at + 8192)
    hatt = t_("hatt", [P, 4, 4, 64])
    het = place("het", [P, S], at=y_at + 8192 + 6144)
    hst = (t_("hst_even", [P, 4, P]), place("hst_odd", [P, 4, P], at=y_at + 8192 + 6144))

    t_ = row(scratch)
    kx, vx = t_("kx", [P, 4, MEM]), t_("vx", [P, 2, S])
    rsx = place("rsx", [P, 4, S], at=scratch + 8192)
    mraw = t_("mraw", [P, KC, MEM])
    m_hi, m_lo = t_("m_hi", [P, KC, MEM], F32R), t_("m_lo", [P, KC, MEM], F32R)
    macc, mr, mt = t_("macc", [P, MEM]), t_("mr", [P, MEM]), t_("mt", [P, 2, MEM])
    t_ = row(region)
    qx = t_("qx", [P, 4, S])
    sqx = t_("sqx", [P, 4, S])
    px = t_("px", [P, 2, 4, MEM])
    ptx = t_("ptx", [P, 2, 2, S])
    nbx, smx = (place(n, [P, 2, 4], at=small + 4096 + o) for n, o in (("nbx", 0), ("smx", 32)))
    rq = place("rq", [P, 16], at=small + 4160)
    t_ = row(region)
    a_hi, a_lo = t_("a_hi", [P, 8, S], F32R), t_("a_lo", [P, 8, S], F32R)
    sl = t_("sl", [P, 2, S])
    ft = t_("ft", [P, 2, S])

    ps = ctx.enter_context(nc.psum_tensor("ps", [P, 8, S], F32))

    block = ctx.enter_context(nc.Block())

    mq = 128 ** -0.5

    def x_ready(l, m=7):
        return sem("x_ready"), l * 8 + (m + 1)

    @block.sync
    def _(sp):
        load = [sem(f"stage_loaded{i}") for i in range(SLOTS)]
        for i in range(4):
            sp.dma_start(xT[:, 2 * i:2 * i + 2], x_d[:, 2 * i:2 * i + 2]).then_inc(sem(f"x_loaded{i}"), 16)
        sp.dma_start(cst[:], cst_d).then_inc(sem("cst_loaded"), 16)
        for i in range(SLOTS):
            sp.dma_start(stage[:, i], w_d[i]).then_inc(load[i], 16)
        with sp.Fori(1, n_layers * NU // SLOTS) as g:
            freed = [sp.snap(g * SLOTS - (SLOTS - 1 - i)) for i in range(SLOTS)]
            src = [sp.snap(g * SLOTS + i) for i in range(SLOTS)]
            for i in range(SLOTS):
                sp.wait_ge(sem("stage_freed"), freed[i])
                sp.dma_start(stage[:, i], w_d[bass.ds(src[i], 1)].rearrange("a p n -> (a p) n")).then_inc(load[i], 16)
        sp.wait_ge(sem("x_ready"), 8 * (n_layers + 1))
        sp.dma_start(out_d, xT[:]).then_inc(sem("x_stored"), 16)
        sp.wait_ge(sem("x_stored"), 16)

    @block.gpsimd
    def _(pool):
        with pool.Fori(0, n_layers) as l:
            for u in range(NU):
                slot = u % SLOTS
                pool.wait_ge(sem("unit_rounded"), l * NU + (u + 1))
                if u in COPIED_U:
                    one = stage[:, slot, 0:1]
                    nc.gpsimd.tensor_tensor(pool_mark[:, u % 4:u % 4 + 1], one, one, ALU.subtract)\
                        .then_inc(sem("stage_freed"), 1)
                else:
                    nc.gpsimd.tensor_tensor(w_lo[:, slot], stage[:, slot], w_hi[:, slot].bitcast(F32),
                                            ALU.subtract).then_inc(sem("stage_freed"), 1)

    bank_of = {}

    @block.tensor
    def _(pe):
        MM = nc.tensor.matmul
        pe.wait_ge(sem("cst_loaded"), 16)
        pe.wait_ge(sem("masks_ready"), 3)
        user = {}

        def own(*banks):
            for key in sorted({user[b] for b in banks if user.get(b)}):
                pe.wait_ge(*aft(*key))
            for b in banks:
                user[b] = None

        def unit(u):
            pe.wait_ge(sem("stage_freed"), layer["l"] * NU + (u + 1))

        fb, fbanks = [0], [0, 1, 2, 3]

        def f_job(name, reader, rhs=None, nk=KC, outs=1, n=S, first=None, at=None):
            u = UNIT_OF[name]
            slot = u % SLOTS
            ah, al = rhs or (h_hi, h_lo)
            unit(u)
            for o in range(outs):
                b, c0 = at or (fbanks[fb[0] % len(fbanks)], 0)
                fb[0] += not at
                own(b)
                for k in range(nk):
                    c = (o * nk + k) * P
                    if first and o == 0:
                        pe.wait_ge(*aft(first, k))
                    lh, ll = w_hi[:, slot, c:c + P], w_lo[:, slot, c:c + P]
                    MM(ps[:, b, c0:c0 + n], lh, ah[:, k, :n], start=k == 0, stop=False)
                    MM(ps[:, b, c0:c0 + n], lh, al[:, k, :n], start=False, stop=False)
                    last = MM(ps[:, b, c0:c0 + n], ll, ah[:, k, :n], start=False, stop=k == nk - 1)
                job = name if outs == 1 else f"{name}.{o}"
                last.then_inc(*inc("dense_done", job))
                user[b] = (reader, job) if reader else None
                bank_of[job] = b
            marks["dense_done", ("unit", u)] = count["dense_done"]

        def t_job(name, reader, lhs=None, banks=(0, 1, 2, 3), first=None, between=None):
            u = UNIT_OF[name]
            ah, al = lhs or (h_hi, h_lo)
            own(*banks)
            for j in range(4):
                unit(u + j)
                slot = (u + j) % SLOTS
                for t, b in enumerate(banks):
                    for kk in range(2):
                        k = 2 * j + kk
                        if first and t == 0:
                            pe.wait_ge(*aft(first, k))
                        rh, rl = w_hi[:, slot, kk * S:(kk + 1) * S], w_lo[:, slot, kk * S:(kk + 1) * S]
                        lh, ll = ah[:, k, t * P:(t + 1) * P], al[:, k, t * P:(t + 1) * P]
                        MM(ps[:, b], lh, rh, start=k == 0, stop=False)
                        MM(ps[:, b], lh, rl, start=False, stop=False)
                        last = MM(ps[:, b], ll, rh, start=False, stop=k == KC - 1)
                last.then_inc(*inc("dense_done", name if j == 3 else None))
                marks["dense_done", ("unit", u + j)] = count["dense_done"]
                if between:
                    between(j)
            for b in banks:
                user[b] = (reader, name)
            fb[0] = 0

        def pair_job(names, readers, first):
            us = [UNIT_OF[n] for n in names]
            bs = [(fb[0] + i) % 4 for i in range(2)]
            fb[0] += 2
            own(*bs)
            for u in us:
                unit(u)
            for k in range(KC):
                pe.wait_ge(*aft(first, k))
                for u, b, name in zip(us, bs, names):
                    c, slot = k * P, u % SLOTS
                    lh, ll = w_hi[:, slot, c:c + P], w_lo[:, slot, c:c + P]
                    MM(ps[:, b], lh, h_hi[:, k], start=k == 0, stop=False)
                    MM(ps[:, b], lh, h_lo[:, k], start=False, stop=False)
                    last = MM(ps[:, b], ll, h_hi[:, k], start=False, stop=k == KC - 1)
                    if k == KC - 1:
                        last.then_inc(*inc("dense_done", name))
            for u, b, name, reader in zip(us, bs, names, readers):
                marks["dense_done", ("unit", u)] = marks["dense_done", name]
                user[b] = (reader, name)
                bank_of[name] = b

        def norm_sum(tag):
            own(4)
            MM(ps[:, 4], ones, acc[:], start=True, stop=True).then_inc(*inc("norm_sum", tag))
            user[4] = ("rstd_ready", tag)

        with pe.Fori(0, n_layers) as l:
            layer["l"] = l
            pe.wait_ge(*x_ready(l))
            norm_sum("mix")
            t_job("q", "ev_q", first="h_mix")
            t_job("kv", "ev_kv", banks=(4, 5, 6, 7))
            fb[0] = 0
            f_job("gd", "gd_t")
            f_job("kc", "ev_kv")
            pe.wait_ge(*aft("gd_t", "gd"))
            own(3)
            f_job("vc", "ev_kv")
            for t in range(NT):
                last = nc.tensor.transpose(ps[:, 3, t * 32:(t + 1) * 32], gdT[0:32, t * P:(t + 1) * P], ident[0:32, 0:32])
            last.then_inc(*inc("cmp_mm", "gd"))
            user[3] = ("ev_nsa", "gd")
            pe.wait_ge(*aft("ev_kv", "vc"))
            pe.wait_ge(*aft("copied_out", "w1v"))
            own(5)
            for w in range(2):
                for m in range(16):
                    last = MM(ps[0:64, 5, w * 66:(w + 1) * 66].rearrange("p (a b) -> p a b", a=2), w1[:, w, m * 64:(m + 1) * 64],
                              kcs[:, w, :, 2 * m:2 * m + 513:16], start=m == 0, stop=m == 15)
            last.then_inc(*inc("cmp_mm", "h"))
            user[5] = ("cmp_dve", "h1")
            for m in range(8):
                f_job(f"gA{m}", "sig_ready")
                if m == 1:
                    pe.wait_ge(*aft("cmp_dve", "h1"))
                    own(5)
                    for g in range(2):
                        MM(ps[:, 5, 64 + g * 64:128 + g * 64], h1v[:, g].rearrange("p a b -> p (a b)"),
                           PR("w2v")[0:64], start=True, stop=True)
                    MM(ps[0:64, 5, 0:64], h1[:, 0], PR("w2k")[0:64], start=True, stop=True).then_inc(*inc("cmp_mm", "kv"))
                    user[5] = ("cmp_dve", "kc_raw")
                if m == 2:
                    pe.wait_ge(*aft("q_rot", 3))
                    for c in range(4):
                        own(4 + c)
                        for t in range(NT):
                            last = nc.tensor.transpose(ps[:, 4 + c, t * P:(t + 1) * P], qr[:, t, c * P:(c + 1) * P], ident)
                        last.then_inc(*inc("q_tr", c))
                        user[4 + c] = ("q_lo", c)
                if m == 4:
                    pe.wait_ge(*aft("k_rot", 3))
                    for br in range(2):
                        own(4 + br)
                        for t in range(NT):
                            last = nc.tensor.transpose(ps[:, 4 + br, t * P:(t + 1) * P], kvr[:, t, br * P:(br + 1) * P], ident)
                        last.then_inc(*inc("k_tr", br))
                        user[4 + br] = ("k_lo", br)
                if m == 6:
                    own(6)
                    pe.wait_ge(*aft("cmp_dve", "kc_rot"))
                if m == 7:
                    nc.tensor.transpose(ps[0:64, 6, 0:64], kcr[0:64, 0], ident[0:64, 0:64]).then_inc(*inc("cmp_mm", "kc_tr"))
                    user[6] = ("cmp_dve", "kcbd")
            steps = [(i, br, h) for i in range(NT) for br in range(2) for h in range(8)]
            pe.wait_ge(*aft("k_lo", 1))

            def qk(n):
                i, br, h = steps[n]
                b = SCORE_BANKS[n % 3]
                own(b)
                wid, q = (i + 1) * P, qT[:, h, i * P:(i + 1) * P]
                MM(ps[:, b, 0:wid], q, k_hi[:, 2 * br + h // 4, 0:wid], start=True, stop=False)
                MM(ps[:, b, 0:wid], q, k_lo[:, 2 * br + h // 4, 0:wid], start=False, stop=False)
                MM(ps[:, b, i * P:wid], identb[:], maskqb[:], start=False, stop=True).then_inc(*inc("qk", n))
                user[b] = ("exp", n)

            def tr(n):
                i = steps[n][0]
                b = (6, 3)[n % 2]
                pe.wait_ge(*aft("exp", n))
                own(b)
                for j in range(i + 1):
                    last = nc.tensor.transpose(ps[:, b, j * P:(j + 1) * P], Pb[:, n % 3, j * P:(j + 1) * P], ident)
                last.then_inc(*inc("ptr", n))
                user[b] = ("ptc_act" if n % 2 == 0 else "ptc_dve", n)

            def pv(n):
                i, br, h = steps[n]
                b = (7, 2)[(n // 8) % 2]
                pe.wait_ge(*aft("ptc_act" if n % 2 == 0 else "ptc_dve", n))
                if h == 0:
                    own(b)
                for j in range(i + 1):
                    v0 = 256 + br * P + (h // 4) * 64
                    last = MM(ps[:, b, h * 64:(h + 1) * 64], PTs[:, n % 3, j * P:(j + 1) * P],
                              kvr[:, j, v0:v0 + 64], start=j == 0, stop=j == i)
                last.then_inc(*inc("pv", n))
                if h == 7:
                    user[b] = ("o_add", n // 8)

            def cmp_part(i, part):
                if part == 0:
                    own(0)
                    if i == 0:
                        pe.wait_ge(*aft("cmp_dve", "kcbd"))
                    for h in range(8):
                        last = MM(ps[:, 0, h * 32:(h + 1) * 32], qT[:, h, i * P:(i + 1) * P].bitcast(F32),
                                  kcbd[:, h // 4], start=True, stop=True)
                    last.then_inc(*inc("cmp_qk", i))
                    user[0] = ("cmp_sc", i)
                elif part == 1:
                    pe.wait_ge(*aft("cmp_p", i))
                    own(0)
                    for g in range(2):
                        last = nc.tensor.transpose(ps[:, 0, g * P:(g + 1) * P],
                                                   sc_c[:, 4 * g:4 * g + 4].rearrange("p a b -> p (a b)"), ident)
                    last.then_inc(*inc("cmp_tr", i))
                    user[0] = ("cmp_ptc", i)
                else:
                    pe.wait_ge(*aft("cmp_ptc", i))
                    own(0)
                    for g in range(2):
                        last = MM(ps[:, 0, g * 256:(g + 1) * 256], ptc[:, g * P:(g + 1) * P],
                                  vcbd[:, g].rearrange("p a b -> p (a b)"), start=True, stop=True)
                    last.then_inc(*inc("cmp_pv", i))
                    user[0] = ("cmp_o", i)

            for n in range(-2, 66):
                if n + 2 < 64:
                    if (n + 2) % 16 == 1:
                        cmp_part((n + 2) // 16, 0)
                    qk(n + 2)
                if 0 <= n < 64:
                    tr(n)
                if n % 16 == 5 and n < 64:
                    cmp_part(n // 16, 1)
                if n % 16 == 9 and n < 64:
                    cmp_part(n // 16, 2)
                if 0 <= n - 2:
                    pv(n - 2)
            pe.wait_ge(*aft("o_add", 7))
            for c in range(4):
                own(4 + c)
                for t in range(NT):
                    last = nc.tensor.transpose(ps[:, 4 + c, t * P:(t + 1) * P], o_acc[:, t, c * P:(c + 1) * P], ident)
                last.then_inc(*inc("o_tr", c))
                user[4 + c] = ("yA_lo", c)
            f_job("xbc0", "xbc_ev")
            for m in range(4):
                f_job(f"yA{m}", "merge_A", rhs=(y_hi, y_lo), nk=4, outs=2, first="yA_lo" if m == 0 else None)
            for m in range(1, 6):
                f_job(f"xbc{m}", "xbc_ev")
            t_job("z", "z_ev", banks=(4, 5, 6, 7))
            for m in GB[0]:
                f_job(f"gB{m}", "sig_ready")
            own(4)
            pe.wait_ge(*aft("dt", "da"))
            for k in range(2):
                for t in range(NT):
                    last = MM(ps[:, 4, k * 32 + t * 8:k * 32 + t * 8 + 8], (triu, ones)[k], da[:, t],
                              start=True, stop=True)
            last.then_inc(*inc("acum", "a"))
            user[4] = ("dt", "args")
            for t in range(NT):
                b = 4 + t
                own(b)
                for c in range(4):
                    if t == 0:
                        pe.wait_ge(*aft("conv", c))
                    last = nc.tensor.transpose(ps[:, b, c * P:(c + 1) * P], cv[:, c, t * P:(t + 1) * P], ident)
                last.then_inc(*inc("xs_tr", t))
                user[b] = ("xs_ev", t)
            own(0)
            pe.wait_ge(*aft("conv", 5))
            for t in range(NT):
                last = nc.tensor.transpose(ps[:, 0, t * P:(t + 1) * P], cv[:, 4, t * P:(t + 1) * P], ident)
            last.then_inc(*inc("xs_tr", "B"))
            user[0] = ("bt_ev", "B")
            fbanks[:] = [0, 1]
            for t in range(NT):
                tk = slice(t * P, (t + 1) * P)
                own(5, 7)
                for g in range(2):
                    gp = slice(64 * g, 64 * g + 64)
                    last = MM(ps[:, 5 + 2 * g, 0:P], cv[gp, 4, tk], cv[gp, 5, tk], start=True, stop=True)
                last.then_inc(*inc("cb", t))
                user[5] = user[7] = ("ssd_m", (t, 1))
                for g in range(2):
                    own(2 + g)
                    for h in range(4):
                        o = ps[:, 2 + g, h * P:(h + 1) * P]
                        hh = 4 * g + h
                        MM(o, da[:, t, hh:hh + 1].to_broadcast([P, P]), triu, start=True, stop=False)
                        last = MM(o, identb[:], masktb[:], start=False, stop=True)
                    last.then_inc(*inc("seg", (t, g)))
                    user[2 + g] = ("ssd_dec", (t, g))
                for m in GB[1 + t]:
                    f_job(f"gB{m}", "sig_ready")
                own(4)
                if t == 0:
                    pe.wait_ge(*aft("xdt", 3))
                for g in range(2):
                    pe.wait_ge(*aft("ssd_m", (t, g)))
                    for h in range(4):
                        hc = slice((4 * g + h) * 64, (4 * g + h + 1) * 64)
                        last = MM(ps[:, 4, hc], dec[:, g, h], xdt[:, t, hc], start=True, stop=True)
                    last.then_inc(*inc("ydiag", (t, g)))
                user[4] = ("ssd_y", t)
                if t > 0:
                    own(5, 7)
                    pe.wait_ge(*aft("ssd_st", t - 1))
                    for g in range(2):
                        gp = slice(64 * g, 64 * g + 64)
                        last = MM(ps[:, 5 + 2 * g, 256:512], cv[gp, 5, tk], ssd_state[gp], start=True, stop=True)
                    last.then_inc(*inc("yoff", t))
                    user[5] = user[7] = ("ssd_y", t)
                if t < NT - 1:
                    own(6)
                    if t == 0:
                        pe.wait_ge(*aft("bt_ev", "B"))
                    pe.wait_ge(*aft("ssd_xe", t))
                    MM(ps[:, 6], Bt[:, t], xe[:], start=True, stop=True).then_inc(*inc("st", t))
                    user[6] = ("ssd_st", t)
            fbanks[:] = [0, 1, 2, 3]
            for m in GB[5][:-1]:
                f_job(f"gB{m}", "sig_ready")
            pe.wait_ge(*aft("ssd_yn", 3))
            for c in range(4):
                own(4 + c)
                for t in range(NT):
                    last = nc.tensor.transpose(ps[:, 4 + c, t * P:(t + 1) * P], ssd_y[:, t, c * P:(c + 1) * P], ident)
                last.then_inc(*inc("y_tr", c))
                user[4 + c] = ("yB_t", c)
            f_job(f"gB{GB[5][-1]}", "sig_ready")
            for m in range(4):
                f_job(f"yB{m}", "merge_B", rhs=(y_hi, y_lo), nk=4, outs=2, first="yB_lo" if m == 0 else None)
            for m in range(4):
                f_job(f"hf{m}", "hf_ev")
            for m in range(4):
                f_job(f"hq{m}", "hq_ev")
            t_job("hv", "hv_ev", banks=(4, 5, 6, 7))
            for hd in range(4):
                for name in HG[hd]:
                    f_job(name, "hg_ev" if name[0] == "h" else "sig_ready")
                own(4)
                pe.wait_ge(*aft("hg_kt", hd))
                pe.wait_ge(*aft("hg_q", hd))
                for c in range(8):
                    pp = 64 * (c % 2)
                    for T in range(4):
                        o = (c // 2) * 64 + 16 * T
                        last = MM(ps[pp:pp + 64, 4, o:o + 16], hKT[:, T, c], hQ[:, c * 64 + 16 * T:c * 64 + 16 * T + 16],
                                  start=True, stop=True)
                last.then_inc(*inc("hg_att", hd))
                user[4] = ("hg_attm", hd)
                own(5)
                pe.wait_ge(*aft("hg_ke", hd))
                for t in range(NT):
                    last = nc.tensor.transpose(ps[:, 5, t * P:(t + 1) * P], hk[:, hd, t * P:(t + 1) * P], ident)
                last.then_inc(*inc("hg_ketr", hd))
                user[5] = ("hg_ket", hd)
            own(4, 5, 6, 7)
            pe.wait_ge(*aft("hg_ket", 3))
            pe.wait_ge(*aft("hg_attm", 3))
            pe.wait_ge(*aft("hv_ev", "hv"))

            def state_part(c):
                pp = slice(64 * (c % 2), 64 * (c % 2) + 64)
                own(c % 2)
                for hd in range(4):
                    last = MM(ps[:, c % 2, hd * P:(hd + 1) * P], hk[pp, hd, c // 2 * P:(c // 2 + 1) * P],
                              hv[pp, c // 2, hd * P:(hd + 1) * P], start=True, stop=True)
                last.then_inc(*inc("hg_st", c))
                user[c % 2] = ("hg_state", c)

            state_part(0)
            fbanks[:] = [2, 3]
            for c in range(8):
                pp = slice(64 * (c % 2), 64 * (c % 2) + 64)
                if c < 6:
                    state_part(c + 1)
                for name in HG[5].get(c, ()):
                    f_job(name, "sig_ready")
                if c:
                    pe.wait_ge(*aft("hg_state", c - 1))
                    pe.wait_ge(*aft("hg_o", c - 1))
                for hd in range(4):
                    o = ps[:, 4 + hd, c * 64:(c + 1) * 64]
                    last = MM(o, hv[pp, c // 2, hd * P:(hd + 1) * P], hatt[pp, hd, c // 2], start=True, stop=c == 0)
                    if c > 0:
                        last = MM(o, hst[c % 2][:, hd], hq[:, hd, c * 64:(c + 1) * 64], start=False, stop=True)
                last.then_inc(*inc("hg_o", c))
            for hd in range(4):
                user[4 + hd] = ("yC_lo", hd)
            fbanks[:] = [0, 1, 2, 3]
            fb[0] = 0
            for name in HG[4][:1]:
                f_job(name, "sig_ready")
            for hd in range(4):
                b = (1 + hd) % 4
                own(b)
                pe.wait_ge(*aft("hg_sq", hd))
                MM(ps[:, b], ones, hq[:, hd], start=True, stop=True).then_inc(*inc("hg_ss", hd))
                user[b] = ("rs_log", ("hg", hd))
            for name in HG[4][1:]:
                f_job(name, "sig_ready")
            for m in range(4):
                f_job(f"yC{m}", "merge_C", rhs=(y_hi, y_lo), nk=4, outs=2, first="yC_lo" if m == 0 else None)
            fb[0] = 0
            for m in range(8):
                f_job(f"o{m}", "res_o", first="merged_lo" if m == 0 else None)
                if m == 2:
                    own(5)
                    pe.wait_ge(*aft("mem_acc", "m"))
                    MM(ps[:, 5, :MEM], ones, macc[:], start=True, stop=True).then_inc(*inc("mem_sum", "m"))
                    user[5] = ("mem_rstd", "m")
            for m in range(4):
                f_job(f"xk{m}", None, rhs=(m_hi, m_lo), n=MEM, first="mem_lo" if m == 0 else None,
                      at=(m // 2, m % 2 * MEM))
                if m == 0:
                    pe.wait_ge(*aft("res_o", "o7"))
                    norm_sum("xa")
            user[0] = user[1] = ("xk_ev", "k")
            t_job("xv", "xv_ev", lhs=(m_hi, m_lo), banks=(4, 5))
            own(6, 7)
            pe.wait_ge(*aft("x_sq", "k"))
            for m in range(4):
                last = MM(ps[:, 6 + m // 2, m % 2 * MEM:(m % 2 + 1) * MEM], ones, sqx[:, m, :MEM], start=True, stop=True)
            last.then_inc(*inc("x_ss", "k"))
            user[6] = user[7] = ("x_rs", "k")

            def q_squares(m):
                b = 6 + m // 2
                own(b)
                pe.wait_ge(*aft("x_sq", f"xq{m}"))
                for t in range(NT):
                    c = m % 2 * NT + t
                    last = MM(ps[:, b, c:c + 1], sqx[:, m, t * P:(t + 1) * P], ones[:, 0:1], start=True, stop=True)
                last.then_inc(*inc("x_ss", f"xq{m}"))
                if m % 2:
                    user[b] = ("x_rs", f"xq{m}")

            fbanks[:] = [2, 3, 0, 1]
            fb[0] = 0
            for m in range(4):
                f_job(f"xq{m}", "xq_ev", first="h_xa" if m == 0 else None)
                if m:
                    q_squares(m - 1)
            def xqk(hd):
                b = 4 + 2 * (hd % 2)
                own(b, b + 1)
                pe.wait_ge(*aft("xk_ev", "k"))
                pe.wait_ge(*aft("xq_ev", f"xq{hd}"))
                for t in range(NT):
                    last = MM(ps[:, b + t // 2, t % 2 * MEM:(t % 2 + 1) * MEM], qx[:, hd, t * P:(t + 1) * P], kx[:, hd],
                              start=True, stop=True)
                last.then_inc(*inc("xqk", hd))
                user[b] = user[b + 1] = ("xexp", hd)

            def xtr(hd):
                own(0, 1)
                pe.wait_ge(*aft("xpn", hd))
                for j in range(2):
                    for t in range(NT):
                        last = nc.tensor.transpose(ps[:, j, t * P:(t + 1) * P], px[:, hd % 2, t, j * P:(j + 1) * P], ident)
                    last.then_inc(*inc("xptr", (hd, j)))
                user[0], user[1] = ("xptc", hd), ("xptd", hd)

            def xpv(hd):
                b = 2 + hd % 2
                own(b)
                pe.wait_ge(*aft("xptc", hd))
                pe.wait_ge(*aft("xptd", hd))
                pe.wait_ge(*aft("xv_ev", "xv"))
                for j in range(2):
                    last = MM(ps[:, b], vx[:, j, hd * P:(hd + 1) * P], ptx[:, hd % 2, j], start=j == 0, stop=j == 1)
                last.then_inc(*inc("xpv", hd))
                user[b] = ("xo_lo", hd)

            q_squares(3)
            xqk(0)
            xqk(1)
            for hd in range(4):
                xtr(hd)
                if hd < 2:
                    xqk(hd + 2)
                xpv(hd)
            fbanks[:] = [0, 1, 2, 3]
            fb[0] = 0
            for m in range(4):
                f_job(f"xo{m}", "res_xo", rhs=(y_hi, y_lo), nk=4, outs=2, first="xo_lo" if m == 0 else None)
            pe.wait_ge(*aft("res_xo", "xo3.1"))
            norm_sum("ffn")
            for p, n in enumerate(FFN_PASSES):
                for c in range(n):
                    if p == 0 and c == 0:
                        pair_job(("fg0_0", "fu0_0"), ("ffn_s", "ffn_t"), "h_ffn")
                    else:
                        f_job(f"fg{p}_{c}", "ffn_s")
                        f_job(f"fu{p}_{c}", "ffn_t")
                for m in range(8):
                    f_job(f"fd{p}_{m}", f"res_f{p}" if p < 2 else "res_f2", rhs=(a_hi, a_lo), nk=n,
                          first=f"ffn_lo{p}" if m == 0 else None)

    @block.scalar
    def _(act):
        A = nc.scalar.activation
        act.wait_ge(sem("cst_loaded"), 16)
        A(identb[:], ident, ACT.Copy).then_inc(sem("masks_ready"), 1)
        A(maskqb[:], C("maskq"), ACT.Copy).then_inc(sem("masks_ready"), 1)
        A(masktb[:], C("maskt"), ACT.Copy).then_inc(sem("masks_ready"), 1)
        done = [0]

        def split_to(last):
            l = layer["l"]
            while done[0] <= min(last, NU - 1):
                u = done[0]
                slot = u % SLOTS
                act.wait_ge(sem(f"stage_loaded{slot}"), 16 * (l * (NU // SLOTS) + (u // SLOTS + 1)))
                if u in COPIED_U:
                    name = COPIED_U[u]
                    if name == "params":
                        A(prm[:], stage[:, slot, :NPRM], ACT.Copy).then_inc(sem("unit_rounded"), 1)
                    else:
                        A(w1[:, name == "w1v"], stage[:, slot], ACT.Copy).then_inc(sem("unit_rounded"), 1)
                    act.wait_ge(sem("unit_rounded"), l * NU + (u + 1))
                    act.sem_inc(*inc("copied_out", name))
                else:
                    if u <= SLOTS:
                        act.wait_ge(*x_ready(l, u % SLOTS + 4))
                    elif u - SLOTS in COPIED_U:
                        act.wait_ge(*aft("dense_done", ("unit", u - 2 * SLOTS)))
                    else:
                        act.wait_ge(*aft("dense_done", ("unit", u - SLOTS)))
                    A(w_hi[:, slot], stage[:, slot], ACT.Copy).then_inc(sem("unit_rounded"), 1)
                done[0] += 1

        def job(name):
            base_name = name.split(".")[0]
            n = dict(PLAN)[base_name]
            split_to(UNIT_OF[base_name] + n - 1 + 3)
            act.wait_ge(*aft("dense_done", name))

        def log_table():
            A(warm[:], epsc, ACT.Ln).then_inc(*inc("log_table"))
            act.wait_ge(*aft("log_table"))

        def rs_from(bank, n, out, tag, src_sem, dst_sem, scale):
            act.wait_ge(*aft(src_sem, tag))
            A(out, ps[:, bank, :n], ACT.Ln, bias=epsc, scale=scale).then_inc(*inc("rs_log"))
            act.wait_ge(*aft("rs_log"))
            A(out, out, ACT.Exp, scale=-0.5).then_inc(*inc(dst_sem, tag))

        def norm(tag, upto):
            if tag != "mix":
                log_table()
            rs_from(4, S, rstd[:], tag, "norm_sum", "rstd_ready", 1.0 / D)
            for k in range(KC):
                act.wait_ge(*aft("norm_t", (tag, k)))
                A(h_hi[:, k], tmp[:, k % 2], ACT.Copy).then_inc(*inc("norm_hi", (tag, k)))
                if k in upto:
                    split_to(upto[k])

        with act.Fori(0, n_layers) as l:
            layer["l"] = l
            done[0] = 0
            log_table()
            split_to(2)
            norm("mix", {1: 3, 4: 4})
            act.wait_ge(*aft("lb", "args"))
            A(lbt[:, 3:5], lbt[:, 1:3], ACT.Exp).then_inc(*inc("lb_exp", "e"))
            job("q")
            for t in range(NT):
                A(qr[:, t], ps[:, t], ACT.Copy).then_inc(*inc("ev_q", ("q", t)))
                A(qsq[:, t], ps[:, t], ACT.Square).then_inc(*inc("ev_q", "q" if t == 3 else ("square", t)))

            def nsa_rs(tag, src, out, scale):
                act.wait_ge(*aft("nsa_ss", tag))
                A(out, src, ACT.Ln, bias=epsc[:out.shape[0]], scale=scale).then_inc(*inc("rs_log"))
                act.wait_ge(*aft("rs_log"))
                A(out, out, ACT.Exp, scale=-0.5).then_inc(*inc("nsa_rs", tag))

            nsa_rs("q", ssq[:, :, 0:8], rsq[:, :, 0:8], 1.0 / 64)
            job("kv")
            for t in range(NT):
                A(kvr[:, t], ps[:, 4 + t], ACT.Copy).then_inc(*inc("ev_kv", ("kv", t)))
                A(ksq[:, t, 0:256], ps[:, 4 + t, 0:256], ACT.Square).then_inc(*inc("ev_kv", "kv" if t == 3 else ("square", t)))
            split_to(UNIT_OF["gd"] + 4)
            nsa_rs("k", ssq[:, :, 8:12], rsq[:, :, 8:12], 1.0 / 64)
            act.wait_ge(*aft("dve", "kcs_pos"))
            for w, name in enumerate(("kc", "vc")):
                job(name)
                for g in range(2):
                    sp_ = slice(64 * g, 64 * g + 64)
                    A(kcs[0:64, w, g, 0:512], ps[sp_, 1 + w, :], ACT.Copy).then_inc(*inc("ev_kv", (name, g, 0)))
                    A(kcs[64:128, w, g, 0:511], ps[sp_, 1 + w, 1:512], ACT.Copy).then_inc(
                        *inc("ev_kv", name if g == 1 else (name, g, 1)))
            split_to(UNIT_OF["gA3"])
            act.wait_ge(*aft("ev_nsa", "gd"))
            A(gth[:], gd[:, :, 0:24], ACT.Tanh, scale=0.5).then_inc(*inc("gate_th", "g"))
            for w in range(2):
                act.wait_ge(*aft("cmp_dve", ("pre", w)))
                A(h1[:, 2 + w], h1[:, w], ACT.Tanh, scale=0.5).then_inc(*inc("cmp_th", w))
            for m in range(8):
                job(f"gA{m}")
                A(sg[:, m], ps[:, bank_of[f"gA{m}"]], ACT.Tanh, scale=0.5).then_inc(*inc("sig_ready", f"gA{m}"))
                if m == 2:
                    for c in range(4):
                        act.wait_ge(*aft("q_tr", c))
                        for e in range(2):
                            hp = slice(64 * e, 64 * e + 64)
                            A(qT[hp, 2 * c + e], ps[hp, 4 + c], ACT.Copy).then_inc(*inc("q_trc", c if e else (c, 0)))
                if m == 4:
                    act.wait_ge(*aft("k_tr", 1))
                    for g in range(2):
                        for half in range(2):
                            A(k_hi[64 * half:64 * half + 64, 2 + g], ps[64 * g:64 * g + 64, 5], ACT.Copy)\
                                .then_inc(*inc("q_trc", "k" if (g, half) == (1, 1) else ("k", g, half)))
                    act.wait_ge(*aft("cmp_dve", "kc_ss"))
                    A(ssc[0:64, 1:2], ssc[0:64, 0:1], ACT.Ln, bias=epsc[0:64], scale=1.0 / 64).then_inc(*inc("rs_log"))
                    act.wait_ge(*aft("rs_log"))
                    A(ssc[0:64, 1:2], ssc[0:64, 1:2], ACT.Exp, scale=-0.5).then_inc(*inc("cmp_th", "rs"))
            steps = [(i, br, h) for i in range(NT) for br in range(2) for h in range(8)]
            for n in range(66):
                if n < 64:
                    i, br, h = steps[n]
                    wid = (i + 1) * P
                    act.wait_ge(*aft("nmax", n))
                    if n >= 3:
                        act.wait_ge(*aft("ptr", n - 3))
                    A(Pb[:, n % 3, :wid], ps[:, SCORE_BANKS[n % 3], :wid], ACT.Exp, bias=nmx[:, n % 3:n % 3 + 1],
                      accum_out=sums[:, br, h:h + 1]).then_inc(*inc("exp", n))
                if n % 16 == 3 and n < 64:
                    i = n // 16
                    act.wait_ge(*aft("cmp_sub", i))
                    A(sc_c[:], sc_c[:], ACT.Exp).then_inc(*inc("cmp_exp", i))
                if n % 16 == 7 and n < 64:
                    i = n // 16
                    act.wait_ge(*aft("cmp_tr", i))
                    A(ptc[:], ps[:, 0, 0:256], ACT.Copy).then_inc(*inc("cmp_ptc", i))
                m = n - 2
                if m >= 0 and m % 2 == 0:
                    wid = (steps[m][0] + 1) * P
                    act.wait_ge(*aft("ptr", m))
                    if m >= 3:
                        act.wait_ge(*aft("pv", m - 3))
                    A(PTs[:, m % 3, :wid], ps[:, 6, :wid], ACT.Copy).then_inc(*inc("ptc_act", m))
            for c in range(4):
                act.wait_ge(*aft("o_tr", c))
                A(y_hi[:, c], ps[:, 4 + c], ACT.Copy).then_inc(*inc("yA_hi", c))
            job("xbc0")
            A(xr[:, 0, 3:], ps[:, bank_of["xbc0"]], ACT.Copy).then_inc(*inc("xbc_ev", "xbc0"))
            for m in range(4):
                for o in range(2):
                    split_to(UNIT_OF[f"yA{m}"] + 3)
            act.wait_ge(*aft("dt", "nabs"))
            A(dtb[:, 2], dtb[:, 1], ACT.Exp).then_inc(*inc("dt_act", "u"))
            A(aexp[:], PR("a_log"), ACT.Exp).then_inc(*inc("dt_act", "a"))

            def conv_tanh(c):
                act.wait_ge(*aft("conv_raw", c))
                A(tmp[:, c % 2], cv[:, c], ACT.Tanh, scale=0.5).then_inc(*inc("conv_th", c))

            for m in range(1, 6):
                job(f"xbc{m}")
                A(xr[:, m, 3:], ps[:, bank_of[f"xbc{m}"]], ACT.Copy).then_inc(*inc("xbc_ev", f"xbc{m}"))
                conv_tanh(m - 1)
            split_to(UNIT_OF["z"] + 3)
            conv_tanh(5)
            job("z")
            for t in range(NT):
                A(zs[:, t], ps[:, 4 + t], ACT.Tanh, scale=0.5).then_inc(*inc("z_th", t))

            def gate_b(ms):
                for m in ms:
                    job(f"gB{m}")
                    A(sg[:, m], ps[:, bank_of[f"gB{m}"]], ACT.Tanh, scale=0.5).then_inc(*inc("sig_ready", f"gB{m}"))

            gate_b(GB[0])
            act.wait_ge(*aft("dt", "args"))
            A(eac[:], eac[:], ACT.Exp).then_inc(*inc("dt_act", "eac"))
            A(edec[:], edec[:], ACT.Exp).then_inc(*inc("dt_act", "edec"))
            A(dend[:], dend[:], ACT.Exp).then_inc(*inc("dt_act", "dend"))
            for t in range(NT):
                act.wait_ge(*aft("xs_tr", t))
                A(xs[:, t], ps[:, 4 + t], ACT.Copy).then_inc(*inc("xs_ev", t))
            act.wait_ge(*aft("xs_tr", "B"))
            A(Bt[:].rearrange("p a b -> p (a b)"), ps[:, 0], ACT.Copy).then_inc(*inc("bt_ev", "B"))
            for t in range(NT):
                for g in range(2):
                    act.wait_ge(*aft("seg", (t, g)))
                    if t > 0:
                        act.wait_ge(*aft("ydiag", (t - 1, g)))
                    for h in range(4):
                        hh = 4 * g + h
                        A(dec[:, g, h], ps[:, 2 + g, h * P:(h + 1) * P], ACT.Exp, bias=nac[:, t, hh:hh + 1])\
                            .then_inc(*inc("ssd_dec", (t, g) if h == 3 else (t, g, h)))
                gate_b(GB[1 + t])
            act.wait_ge(*aft("ssd_ss", 3))
            A(ssy[:], ssy[:], ACT.Ln, bias=epsc, scale=1.0 / 1024).then_inc(*inc("rs_log"))
            act.wait_ge(*aft("rs_log"))
            A(ssy[:], ssy[:], ACT.Exp, scale=-0.5).then_inc(*inc("ssd_rs", "rs"))
            gate_b(GB[5][:-1])
            split_to(UNIT_OF["yB0"] + 2)
            for c in range(4):
                act.wait_ge(*aft("yB_t", c))
                A(y_hi[:, c], tmp[:, c % 2], ACT.Copy).then_inc(*inc("yB_hi", c))
            gate_b(GB[5][-1:])
            for m in range(4):
                split_to(UNIT_OF[f"yB{m}"] + 3)
            for m in range(4):
                job(f"hf{m}")
                A(hb[:, m], ps[:, bank_of[f"hf{m}"]], ACT.Sigmoid).then_inc(*inc("hf_s", m))
                A(hk[:, m], ps[:, bank_of[f"hf{m}"]], ACT.Sigmoid, scale=-1.0).then_inc(*inc("hf_ev", f"hf{m}"))
            act.wait_ge(*aft("hf_ev", "hf3"))
            act.wait_ge(*aft("lb", "lb"))
            for m in range(4):
                A(hb[:, m], hb[:, m], ACT.Ln, bias=lbt[:, 6, m:m + 1], scale=lbt[:, 7, m:m + 1])\
                    .then_inc(*inc("hf_ln", m))
            for m in range(4):
                job(f"hq{m}")
                A(hq[:, m], ps[:, bank_of[f"hq{m}"]], ACT.Tanh, scale=0.5).then_inc(*inc("hq_th", m))
            job("hv")
            for t in range(NT):
                A(hv[:, t], ps[:, 4 + t], ACT.Copy).then_inc(*inc("hv_ev", "hv" if t == 3 else ("hv", t)))

            def fill(names):
                for name in names:
                    m = int(name[2:])
                    job(name)
                    if name[0] == "h":
                        A(hgt[:, m], ps[:, bank_of[name]], ACT.Tanh, scale=0.5).then_inc(*inc("hg_th", m))
                    else:
                        A(sg[:, m], ps[:, bank_of[name]], ACT.Tanh, scale=0.5).then_inc(*inc("sig_ready", name))

            for hd in range(4):
                act.wait_ge(*aft("hg_arg", (hd, "q")))
                A(het[:], het[:], ACT.Exp).then_inc(*inc("hg_ex", (hd, "q")))
                act.wait_ge(*aft("hg_arg", (hd, "kt")))
                for T in range(4):
                    A(hKT[:, T, :, :16 * (T + 1)], hKT[:, T, :, :16 * (T + 1)], ACT.Exp).then_inc(*inc("hg_ex", (hd, "kt", T)))
                act.wait_ge(*aft("hg_q", hd))
                A(het[:], hb[:, hd], ACT.Exp).then_inc(*inc("hg_ex", (hd, "b")))
                act.wait_ge(*aft("hg_arg", (hd, "e")))
                A(tmp[:, 0], tmp[:, 0], ACT.Exp).then_inc(*inc("hg_ex", (hd, "e")))
                A(eblast[:, hd], hb[:, hd, 63::64], ACT.Exp).then_inc(*inc("hg_ex", (hd, "l")))
                fill(HG[hd])
                act.wait_ge(*aft("hg_ketr", hd))
                A(hk[:, hd], ps[:, 5], ACT.Copy).then_inc(*inc("hg_ket", hd))
            for c in range(8):
                fill(HG[5].get(c, ()))
            act.wait_ge(*aft("hg_o", 7))
            for hd in range(4):
                A(hq[:, hd], ps[:, 4 + hd], ACT.Square).then_inc(*inc("hg_sq", hd))
            fill(HG[4][:1])
            log_table()
            for hd in range(4):
                act.wait_ge(*aft("hg_ss", hd))
                A(hk[:, hd], ps[:, (1 + hd) % 4], ACT.Ln, bias=epsc, scale=1.0 / 128).then_inc(*inc("rs_log", ("hg", hd)))
            act.wait_ge(*aft("rs_log"))
            for hd in range(4):
                A(hk[:, hd], hk[:, hd], ACT.Exp, scale=-0.5).then_inc(*inc("hg_rs", hd))
            for hd in range(4):
                act.wait_ge(*aft("yC_t", hd))
                A(y_hi[:, hd], tmp[:, hd % 2], ACT.Copy).then_inc(*inc("yC_hi", hd))
            act.wait_ge(*aft("yC_lo", 3))
            act.dma_start(mraw[:], mem_d).then_inc(*inc("mem_loaded", "m", 16))
            fill(HG[4][1:])
            for m in range(8):
                split_to(UNIT_OF[f"yC{m // 2}"] + 3)
                act.wait_ge(*aft("merge_C", f"yC{m // 2}.{m % 2}"))
                A(h_hi[:, m], merged[:, m], ACT.Copy, scale=0.5).then_inc(*inc("merged_hi", m))
            for m in range(8):
                job(f"o{m}")
                if m == 2:
                    log_table()
                    rs_from(5, MEM, mr[:], "m", "mem_sum", "mem_rstd", 1.0 / D)
                    for k in range(KC):
                        act.wait_ge(*aft("mem_t", k))
                        A(m_hi[:, k], mt[:, k % 2], ACT.Copy).then_inc(*inc("mem_hi", k))
                        if k == 3:
                            split_to(UNIT_OF["o4"] + 2)
            split_to(UNIT_OF["xk0"] + 3)
            norm("xa", {k: UNIT_OF["xk0"] + 3 + (k + 1) // 2 for k in (1, 3, 5, 7)})
            job("xk3")
            A(sqx[:, :, :MEM], ps[:, 0:2].rearrange("p a (b n) -> p (a b) n", b=2), ACT.Square).then_inc(*inc("x_sq", "k"))
            job("xv")
            A(vx[:], ps[:, 4:6], ACT.Copy).then_inc(*inc("xv_ev", "xv"))
            act.wait_ge(*aft("x_ss", "k"))
            A(rsx[:, :, :MEM], ps[:, 6:8].rearrange("p a (b n) -> p (a b) n", b=2), ACT.Ln, bias=epsc, scale=1.0 / 128)\
                .then_inc(*inc("rs_log"))
            act.wait_ge(*aft("rs_log"))
            A(rsx[:, :, :MEM], rsx[:, :, :MEM], ACT.Exp, scale=-0.5).then_inc(*inc("x_rs", "k"))

            def x_exp(hd):
                for t in range(NT):
                    if t == 0:
                        act.wait_ge(*aft("xnb", hd))
                    if t == 0 and hd >= 2:
                        act.wait_ge(*aft("xptr", (hd - 2, 1)))
                    A(px[:, hd % 2, t], ps[:, 4 + 2 * (hd % 2) + t // 2, t % 2 * MEM:(t % 2 + 1) * MEM], ACT.Exp,
                      bias=nbx[:, hd % 2, t:t + 1], scale=rq[:, hd * 4 + t:hd * 4 + t + 1], accum_out=smx[:, hd % 2, t:t + 1])\
                        .then_inc(*inc("xexp", hd if t == 3 else (hd, t)))

            for m in range(5):
                if m < 4:
                    job(f"xq{m}")
                    A(sqx[:, m], ps[:, bank_of[f"xq{m}"]], ACT.Square).then_inc(*inc("x_sq", f"xq{m}"))
                if m == 2 or m == 4:
                    act.wait_ge(*aft("x_ss", f"xq{m - 1}"))
                    r = rq[:, m * 4 - 8:m * 4]
                    A(r, ps[:, 5 + m // 2, 0:8], ACT.Ln, bias=epsc, scale=1.0 / 128).then_inc(*inc("rs_log"))
                    act.wait_ge(*aft("rs_log"))
                    A(r, r, ACT.Exp, scale=-0.5).then_inc(*inc("x_rs", f"xq{m - 1}"))

            def x_out(hd):
                act.wait_ge(*aft("xpv", hd))
                A(y_hi[:, hd], ps[:, 2 + hd % 2], ACT.Copy).then_inc(*inc("xo_hi", hd))

            x_exp(0)
            x_exp(1)
            for hd in range(4):
                act.wait_ge(*aft("xptr", (hd, 0)))
                if hd >= 2:
                    act.wait_ge(*aft("xpv", hd - 2))
                A(ptx[:, hd % 2, 0], ps[:, 0], ACT.Copy).then_inc(*inc("xptc", hd))
                if hd:
                    x_out(hd - 1)
                if hd < 2:
                    x_exp(hd + 2)
            x_out(3)
            for m in range(4):
                split_to(UNIT_OF[f"xo{m}"] + 3)
            norm("ffn", {})
            fus = [f"fu{p}_{c}" for p, n in enumerate(FFN_PASSES) for c in range(n)]
            j = 0
            for p, n in enumerate(FFN_PASSES):
                for c in range(n):
                    job(f"fg{p}_{c}")
                    if j >= 2:
                        act.wait_ge(*aft("ffn_t", fus[j - 2]))
                    A(sl[:, j % 2], ps[:, bank_of[f"fg{p}_{c}"]], ACT.Silu).then_inc(*inc("ffn_s", f"fg{p}_{c}"))
                    job(f"fu{p}_{c}")
                    act.wait_ge(*aft("ffn_t", f"fu{p}_{c}"))
                    A(a_hi[:, c], ft[:, j % 2], ACT.Copy).then_inc(*inc("ffn_hi", j))
                    j += 1
                for m in range(8):
                    job(f"fd{p}_{m}")

    @block.vector
    def _(v):
        V = nc.vector
        TT, TS, STT = V.tensor_tensor, V.tensor_scalar, V.scalar_tensor_tensor
        MU, AD, SU, MX = ALU.mult, ALU.add, ALU.subtract, ALU.max

        def then(ins, name="dve", mark=None):
            ins.then_inc(*inc(name, mark))
            v.wait_ge(*aft(name))

        def settle():
            v.wait_ge(*aft(recent[0]))

        def bc(ap, n):
            return ap.unsqueeze(ap.ndim if hasattr(ap, "ndim") else len(ap.shape)).to_broadcast(list(ap.shape) + [n])

        def residual(bank, m, name, key, last):
            v.wait_ge(*aft("dense_done", key))
            if not last:
                TT(xT[:, m], xT[:, m], ps[:, bank], AD).then_inc(*inc(name, key)); settle()
                return
            TT(xT[:, m], xT[:, m], ps[:, bank], AD).then_inc(*inc(name + "_x", key)); settle()
            v.wait_ge(*aft(name + "_x", key))
            squares(m, (name, key))

        def squares(m, key):
            if m == 0:
                ins = TT(acc[:], xT[:, 0], xT[:, 0], MU)
            else:
                then(TT(tmp[:, m % 2], xT[:, m], xT[:, m], MU))
                ins = TT(acc[:], acc[:], tmp[:, m % 2], AD)
            if key is None:
                ins.then_inc(sem("x_ready"), 1)
                v.wait_ge(*x_ready(layer["l"] + 1, m))
            else:
                ins.then_inc(*inc(*key)); settle()

        def norm(tag):
            v.wait_ge(*aft("rstd_ready", tag))

            def scaled(k):
                STT(tmp[:, k % 2], xT[:, k], col("norm_" + tag, k), rstd[:], MU, MU).then_inc(*inc("norm_t", (tag, k))); settle()

            def low(k):
                v.wait_ge(*aft("norm_hi", (tag, k)))
                TT(h_lo[:, k], tmp[:, k % 2], h_hi[:, k].bitcast(F32), SU).then_inc(*inc("h_" + tag, k)); settle()

            scaled(0)
            for k in range(KC):
                if k + 1 < KC:
                    scaled(k + 1)
                low(k)

        for m in range(8):
            if m % 2 == 0:
                v.wait_ge(sem(f"x_loaded{m // 2}"), 16)
            if m:
                TT(tmp[:, m % 2], xT[:, m], xT[:, m], MU).then_inc(sem("x_square"), 1)
                v.wait_ge(sem("x_square"), m)
                v.wait_ge(sem("x_ready"), m)
                TT(acc[:], acc[:], tmp[:, m % 2], AD).then_inc(sem("x_ready"), 1)
            else:
                TT(acc[:], xT[:, 0], xT[:, 0], MU).then_inc(sem("x_ready"), 1)

        with v.Fori(0, n_layers) as l:
            layer["l"] = l
            v.wait_ge(sem("stage_freed"), l * NU + 1)
            norm("mix")
            lbp = PR("lb").rearrange("p (a b) -> p a b", a=2)
            then(TT(lbt[:, 0], lbp[:, 0], lbp[:, 1], MX))
            TT(lbt[:, 1], lbp[:, 0], lbt[:, 0], SU).then_inc(*inc("dve")); settle()
            TT(lbt[:, 2], lbp[:, 1], lbt[:, 0], SU).then_inc(*inc("lb", "args")); settle()
            v.wait_ge(*aft("lb_exp", "e"))
            then(TT(lbt[:, 5], lbt[:, 3], lbt[:, 4], AD))
            then(V.reciprocal(lbt[:, 5], lbt[:, 5]))
            then(STT(lbt[:, 6], lbt[:, 4], col("layer", 0), lbt[:, 5], MU, MU))
            then(TS(lbt[:, 7], lbt[:, 6], -1.0, 1.0, MU, AD), "lb", "lb")

            def rope(x, n, cos, sin, t, heads, w, pre, signal, rs, tmpf):
                xh = x.rearrange("p (h f) -> p h f", h=heads)
                then(TT(xh, xh, bc(rs, 64), MU))
                then(STT(xh, xh, pre, w[:n].unsqueeze(1).to_broadcast([n, heads, 64]), MU, MU))
                x4 = x.rearrange("p (h a f) -> p h a f", h=heads, a=2)
                r4 = tmpf[:n, :heads * 64].rearrange("p (h a f) -> p h a f", h=heads, a=2)
                cb = cos.unsqueeze(1).to_broadcast([n, heads, 32])
                sb_ = sin.unsqueeze(1).to_broadcast([n, heads, 32])
                TT(r4[:, :, 0], x4[:, :, 1], sb_, MU).then_inc(*inc("dve")); settle()
                TT(r4[:, :, 1], x4[:, :, 0], sb_, MU).then_inc(*inc("dve")); settle()
                for a in range(2):
                    TT(x4[:, :, a], x4[:, :, a], cb, MU).then_inc(*inc("dve")); settle()
                TT(x4[:, :, 0], x4[:, :, 0], r4[:, :, 0], SU).then_inc(*inc("dve")); settle()
                TT(x4[:, :, 1], x4[:, :, 1], r4[:, :, 1], AD).then_inc(*inc(*signal)); settle()

            def head_squares(src, heads, c0, t, tag):
                V.reduce_sum(ssq[:, t, c0:c0 + heads], src.rearrange("p (h f) -> p h f", h=heads), AX)\
                    .then_inc(*inc("nsa_ss", tag if t == 3 else (tag, t))); settle()

            for w, name in enumerate(("pos_k", "pos_v")):
                V.tensor_copy(kcs[:, w, :, 512:544:2], PR(name).unsqueeze(1).to_broadcast([P, 2, 16])).then_inc(
                    *inc("dve", "kcs_pos" if w else None)); settle()
            V.memset(vcbd[:], 0.0).then_inc(*inc("dve")); settle()
            v.wait_ge(*aft("ev_q", "q"))
            for t in range(NT):
                head_squares(qsq[:, t], 8, 0, t, "q")
            v.wait_ge(*aft("nsa_rs", "q"))
            for t in range(NT):
                rope(qr[:, t], P, C("cos")[:, t * 32:(t + 1) * 32], C("sin")[:, t * 32:(t + 1) * 32], t, 8, PR("q_norm"),
                     0.125, ("q_rot", t), rsq[:, t, 0:8], rt[:, t])
            v.wait_ge(*aft("ev_kv", "kv"))
            v.wait_ge(*aft("dense_done", "gd"))
            V.tensor_copy(gdT[0:32], ps[0:32, 0]).then_inc(*inc("gd_t", "gd")); settle()
            for t in range(NT):
                head_squares(ksq[:, t, 0:256], 4, 8, t, "k")
            v.wait_ge(*aft("cmp_mm", "gd"))
            V.tensor_copy(gd[:].rearrange("p a b -> p (a b)"), ps[:, 3, 0:128]).then_inc(*inc("ev_nsa", "gd")); settle()
            v.wait_ge(*aft("nsa_rs", "k"))
            for t in range(NT):
                rope(kvr[:, t, 0:256], P, C("cos")[:, t * 32:(t + 1) * 32], C("sin")[:, t * 32:(t + 1) * 32], t, 4,
                     PR("k_norm"), 1.0, ("k_rot", t), rsq[:, t, 8:12], rt[:, t])
            v.wait_ge(*aft("cmp_mm", "h"))
            then(V.tensor_copy(posb[:], ps[0:64, 5, 32:99:66]))
            for w in range(2):
                TS(h1[:, w].rearrange("p (a b) -> p a b", a=2),
                   ps[0:64, 5, w * 66:(w + 1) * 66].rearrange("p (a b) -> p a b", a=2)[:, :, 0:32],
                   posb[:, w:w + 1], None, AD).then_inc(*inc("cmp_dve", ("pre", w))); settle()
            for w in range(2):
                v.wait_ge(*aft("cmp_th", w))
                then(TS(h1[:, 2 + w], h1[:, 2 + w], 0.5, 0.5, MU, AD))
                then(TT(h1[:, w], h1[:, w], h1[:, 2 + w], MU))
            V.tensor_copy(h1v[:], h1[:, 1].rearrange("p (g n) -> p g n", g=2).unsqueeze(2).to_broadcast([64, 2, 4, 32]))\
                .then_inc(*inc("cmp_dve", "h1")); settle()
            v.wait_ge(*aft("gate_th", "g"))
            TS(gth[:], gth[:], 0.5, 0.5, MU, AD).then_inc(*inc("dve")); settle()
            v.wait_ge(*aft("cmp_mm", "kv"))
            for r in range(4):
                rr = slice(32 * r, 32 * r + 32)
                V.tensor_copy(vcbd[rr, :, r, :], ps[rr, 5, 64:192].rearrange("p (g f) -> p g f", g=2)).then_inc(*inc("dve")); settle()
            then(V.tensor_copy(kcr[0:64, 0], ps[0:64, 5, 0:64]), "cmp_dve", "kc_raw")
            then(TT(kcr[0:64, 1], kcr[0:64, 0], kcr[0:64, 0], MU))
            V.reduce_sum(ssc[0:64, 0:1], kcr[0:64, 1], AX).then_inc(*inc("cmp_dve", "kc_ss")); settle()
            for c in range(4):
                v.wait_ge(*aft("q_trc", c))
                for e in range(2):
                    hp, other = slice(64 * e, 64 * e + 64), slice(64 - 64 * e, 128 - 64 * e)
                    TT(qT[other, 2 * c + e], ps[hp, 4 + c], qT[hp, 2 * c + e].bitcast(F32), SU).then_inc(
                        *inc("q_lo", c if e else (c, 0))); settle()
            v.wait_ge(*aft("k_tr", 0))
            for g in range(2):
                for half in range(2):
                    V.tensor_copy(k_hi[64 * half:64 * half + 64, g], ps[64 * g:64 * g + 64, 4]).then_inc(*inc("dve")); settle()
            for br in range(2):
                if br:
                    v.wait_ge(*aft("q_trc", "k"))
                for g in range(2):
                    gp = slice(64 * g, 64 * g + 64)
                    for half in range(2):
                        TT(k_lo[64 * half:64 * half + 64, 2 * br + g], ps[gp, 4 + br], k_hi[gp, 2 * br + g].bitcast(F32), SU)\
                            .then_inc(*inc("k_lo", br if (g, half) == (1, 1) else (br, g, half))); settle()
            v.wait_ge(*aft("cmp_th", "rs"))
            rope(kcr[0:64, 0], 64, C("cosc")[0:64], C("sinc")[0:64], 0, 1, PR("k_norm"), 1.0,
                 ("cmp_dve", "kc_rot"), ssc[0:64, 1:2], rt[:, 0])
            v.wait_ge(*aft("cmp_mm", "kc_tr"))
            for half in range(2):
                V.tensor_copy(kcbd[64 * half:64 * half + 64],
                              ps[0:64, 6, 0:64].rearrange("p (g n) -> p g n", g=2)).then_inc(
                    *inc("cmp_dve", "kcbd" if half else "kcbd0")); settle()

            steps = [(i, br, h) for i in range(NT) for br in range(2) for h in range(8)]
            for n in range(69):
                if n < 64:
                    i, br, h = steps[n]
                    wid = (i + 1) * P
                    v.wait_ge(*aft("qk", n))
                    V.reduce_max(nmx[:, n % 3:n % 3 + 1], ps[:, SCORE_BANKS[n % 3], :wid], AX, negate=True).then_inc(*inc("nmax", n)); settle()
                if n % 16 == 1 and n < 64:
                    i = n // 16
                    v.wait_ge(*aft("cmp_qk", i))
                    then(TT(sc_c[:], ps[:, 0, 0:256].rearrange("p (h n) -> p h n", h=8),
                            C("maskc")[:, i * 32:(i + 1) * 32].unsqueeze(1).to_broadcast([P, 8, 32]), AD), "cmp_sc", i)
                    then(V.reduce_max(mx_c[:], sc_c[:], AX))
                    TT(sc_c[:], sc_c[:], bc(mx_c[:], 32), SU).then_inc(*inc("cmp_sub", i)); settle()
                if n % 16 == 4 and n < 64:
                    i = n // 16
                    v.wait_ge(*aft("cmp_exp", i))
                    then(V.reduce_sum(sum_c[:], sc_c[:], AX))
                    then(V.reciprocal(sum_c[:], sum_c[:]))
                    then(STT(sum_c[:], sum_c[:], C("valid")[:, i:i + 1],
                             gth[:, i].rearrange("p (h b) -> p h b", b=3)[:, :, 0], MU, MU))
                    TT(sc_c[:], sc_c[:], bc(sum_c[:], 32), MU).then_inc(*inc("cmp_p", i)); settle()
                if n % 16 == 12 and n < 64:
                    i = n // 16
                    v.wait_ge(*aft("cmp_pv", i))
                    then(TT(o_acc[:, i], o_acc[:, i], ps[:, 0], AD), "cmp_o", i)
                m = n - 2
                if 0 <= m < 64 and m % 2 == 1:
                    wid = (steps[m][0] + 1) * P
                    v.wait_ge(*aft("ptr", m))
                    if m >= 3:
                        v.wait_ge(*aft("pv", m - 3))
                    V.tensor_copy(PTs[:, m % 3, :wid], ps[:, 3, :wid]).then_inc(*inc("ptc_dve", m)); settle()
                m = n - 4
                if m >= 0 and m < 64 and m % 8 == 7:
                    i, br, _ = steps[m]
                    b = (7, 2)[(m // 8) % 2]
                    v.wait_ge(*aft("exp", m))
                    then(V.reciprocal(coef[:], sums[:, br]))
                    then(TT(coef[:], coef[:], gth[:, i].rearrange("p (h b) -> p h b", b=3)[:, :, 1 + br], MU))
                    v.wait_ge(*aft("pv", m))
                    pso = ps[:, b].rearrange("p (h f) -> p h f", h=8)
                    if br == 0:
                        then(TT(o_acc[:, i].rearrange("p (h f) -> p h f", h=8), pso, bc(coef[:], 64), MU), "o_add", m // 8)
                    else:
                        then(TT(tmp[:, 0].rearrange("p (h f) -> p h f", h=8), pso, bc(coef[:], 64), MU))
                        then(TT(o_acc[:, i], o_acc[:, i], tmp[:, 0], AD), "o_add", m // 8)
            for c in range(4):
                v.wait_ge(*aft("yA_hi", c))
                TT(y_lo[:, c], ps[:, 4 + c], y_hi[:, c].bitcast(F32), SU).then_inc(*inc("yA_lo", c)); settle()

            def merge(which, m):
                key = f"y{which}{m // 2}.{m % 2}"
                bank = bank_of[key]
                v.wait_ge(*aft("sig_ready", f"g{which}{m}"))
                v.wait_ge(*aft("dense_done", key))
                if which == "A":
                    STT(merged[:, m], sg[:, m], 1.0, ps[:, bank], AD, MU).then_inc(*inc("merge_A", key)); settle()
                else:
                    then(STT(tmp[:, m % 2], sg[:, m], 1.0, ps[:, bank], AD, MU))
                    TT(merged[:, m], merged[:, m], tmp[:, m % 2], AD).then_inc(*inc("merge_" + which, key)); settle()

            dt_x, dt_n, dt_u, dt_w, dt_w2, dt_p = (dtb[:, k].rearrange("p (t h) -> p t h", h=8) for k in range(6))
            then(TT(dt_x, gd[:, :, 24:32], PR("dt_bias").unsqueeze(1).to_broadcast([P, NT, 8]), AD))
            then(TS(dt_n, dt_x, -1.0, None, MU))
            then(TT(dt_n, dt_x, dt_n, ALU.min), "dt", "nabs")
            for m in range(8):
                merge("A", m)

            V.memset(xr[:, :, 0:3], 0.0).then_inc(*inc("dve")); settle()
            v.wait_ge(*aft("dt_act", "u"))
            then(TS(dt_w, dt_u, 2.0, None, AD))
            then(V.reciprocal(dt_w, dt_w))
            then(TT(dt_w, dt_w, dt_u, MU))
            then(TT(dt_w2, dt_w, dt_w, MU))
            then(TS(dt_p, dt_w2, 1.0 / 17, None, MU))
            for k in (15, 13, 11, 9, 7, 5, 3):
                then(STT(dt_p, dt_p, 1.0 / k, dt_w2, AD, MU))
            then(STT(dt_p, dt_p, 1.0, dt_w, AD, MU))
            then(TS(dt_x, dt_x, 0.0, None, MX))
            then(STT(dt_x, dt_p, 2.0, dt_x, MU, AD))
            v.wait_ge(*aft("dt_act", "a"))
            then(STT(da[:], dt_x, -1.0, aexp[:].unsqueeze(1).to_broadcast([P, NT, 8]), MU, MU), "dt", "da")
            then(TS(dth[:], dt_x, 0.5, None, MU))
            then(TS(dsk[:], PR("ssm_d"), 0.5, None, MU))
            for c in range(6):
                v.wait_ge(*aft("xbc_ev", f"xbc{c}"))
                w = PC["conv_w"][0] + 4 * c
                then(TS(cv[:, c], xr[:, c, 3:515], prm[:, w + 3:w + 4], col("conv_b", c), MU, AD))
                for k in (2, 1, 0):
                    ins = STT(cv[:, c], xr[:, c, k:k + 512], prm[:, w + k:w + k + 1], cv[:, c], MU, AD)
                    if k:
                        then(ins)
                    else:
                        ins.then_inc(*inc("conv_raw", c)); settle()
                if c:
                    v.wait_ge(*aft("conv_th", c - 1))
                    STT(cv[:, c - 1], tmp[:, (c - 1) % 2], 1.0, cv[:, c - 1], AD, MU).then_inc(*inc("conv", c - 1)); settle()
            v.wait_ge(*aft("conv_th", 5))
            STT(cv[:, 5], tmp[:, 1], 1.0, cv[:, 5], AD, MU).then_inc(*inc("conv", 5)); settle()
            for t in range(NT):
                v.wait_ge(*aft("z_th", t))
                STT(zs[:, t], zs[:, t], 1.0, ps[:, 4 + t], AD, MU).then_inc(*inc("z_ev", "z" if t == 3 else ("z", t))); settle()
            v.wait_ge(*aft("acum", "a"))
            pa = ps[:, 4, 0:32].rearrange("p (t h) -> p t h", h=8)
            pl = ps[:, 4, 32:64].rearrange("p (t h) -> p t h", h=8)
            V.tensor_copy(eac[:], pa).then_inc(*inc("dve")); settle()
            then(V.tensor_copy(edec[:], pl))
            then(TT(dend[:], edec[:], eac[:], SU))
            TS(nac[:], eac[:], -1.0, None, MU).then_inc(*inc("dt", "args")); settle()
            v.wait_ge(*aft("dt_act", "dend"))
            then(TS(eac[:], eac[:], 0.25, None, MU))
            for t in range(NT):
                v.wait_ge(*aft("xs_ev", t))
                TT(xdt[:, t].rearrange("p (h f) -> p h f", h=8), xs[:, t].rearrange("p (h f) -> p h f", h=8),
                   bc(dth[:, t], 64), MU).then_inc(*inc("xdt", t)); settle()
            v.wait_ge(*aft("xdt", 3))
            for t in range(NT):
                if t < NT - 1:
                    if t:
                        v.wait_ge(*aft("st", t - 1))
                    TT(xe[:].rearrange("p (h f) -> p h f", h=8), xdt[:, t].rearrange("p (h f) -> p h f", h=8),
                       bc(dend[:, t], 64), MU).then_inc(*inc("ssd_xe", t)); settle()
                v.wait_ge(*aft("cb", t))
                for g in range(2):
                    v.wait_ge(*aft("ssd_dec", (t, g)))
                    STT(dec[:, g], ps[:, 5 + 2 * g, 0:P].unsqueeze(1).to_broadcast([P, 4, P]), 0.25, dec[:, g],
                        MU, MU).then_inc(*inc("ssd_m", (t, g))); settle()
                y8 = ssd_y[:, t].rearrange("p (h f) -> p h f", h=8)
                then(TT(y8, xs[:, t].rearrange("p (h f) -> p h f", h=8), bc(dsk[:], 64), MU))
                v.wait_ge(*aft("ydiag", (t, 1)))
                ins = TT(ssd_y[:, t], ssd_y[:, t], ps[:, 4], AD)
                if t == 0:
                    then(ins, "ssd_y", t)
                else:
                    then(ins)
                    v.wait_ge(*aft("yoff", t))
                    for g in range(2):
                        then(TT(tmp[:, 0, g * 256:(g + 1) * 256].rearrange("p (h f) -> p h f", h=4),
                                ps[:, 5 + 2 * g, 256:512].rearrange("p (h f) -> p h f", h=4),
                                bc(eac[:, t, 4 * g:4 * g + 4], 64), MU), "ssd_y", t if g else (t, 0))
                    then(TT(ssd_y[:, t], ssd_y[:, t], tmp[:, 0], AD))
                if t < NT - 1:
                    v.wait_ge(*aft("st", t))
                    for g in range(2):
                        gp = slice(64 * g, 64 * g + 64)
                        src = ps[gp, 6, g * 256:(g + 1) * 256]
                        key = t if g == 1 else (t, 0)
                        if t == 0:
                            V.tensor_copy(ssd_state[gp], src).then_inc(*inc("ssd_st", key)); settle()
                        else:
                            then(TT(ssd_state[gp].rearrange("p (h f) -> p h f", h=4), ssd_state[gp].rearrange("p (h f) -> p h f", h=4),
                                    bc(edec[gp, t, 4 * g:4 * g + 4], 64), MU))
                            TT(ssd_state[gp], ssd_state[gp], src, AD).then_inc(*inc("ssd_st", key)); settle()
                then(TT(ssd_y[:, t], ssd_y[:, t], zs[:, t], MU))
                then(TT(tmp[:, 1], ssd_y[:, t], ssd_y[:, t], MU))
                V.reduce_sum(ssy[:, t], tmp[:, 1].rearrange("p (g f) -> p g f", g=2), AX).then_inc(*inc("ssd_ss", t)); settle()
            v.wait_ge(*aft("ssd_rs", "rs"))
            for t in range(NT):
                y2 = ssd_y[:, t].rearrange("p (g f) -> p g f", g=2)
                STT(y2, y2, 0.5, bc(ssy[:, t], 256), MU, MU).then_inc(*inc("ssd_yn", t)); settle()

            def y_t(c):
                v.wait_ge(*aft("y_tr", c))
                TS(tmp[:, c % 2], ps[:, 4 + c], col("ssm_norm", c), None, MU).then_inc(*inc("yB_t", c)); settle()

            v.wait_ge(*aft("y_tr", 3))
            y_t(0)
            for c in range(4):
                if c < 3:
                    y_t(c + 1)
                v.wait_ge(*aft("yB_hi", c))
                TT(y_lo[:, c], tmp[:, c % 2], y_hi[:, c].bitcast(F32), SU).then_inc(*inc("yB_lo", c)); settle()
            for m in range(8):
                merge("B", m)

            V.memset(hKT[:], 0.0).then_inc(*inc("dve")); settle()
            for m in range(4):
                v.wait_ge(*aft("hf_ev", f"hf{m}"))
                TS(hk[:, m], hk[:, m], lbt[:, 7, m:m + 1], None, MU).then_inc(*inc("dve")); settle()
            then(V.memset(hQ[:], 1.0))
            then(V.memset(hQ[:, 0:S:64], 0.0))
            for m in range(4):
                v.wait_ge(*aft("hf_ln", m))
                then(V.tensor_tensor_scan(hb[:, m], hQ[:], hb[:, m], 0.0, MU, AD), "hb", m)
            for m in range(4):
                v.wait_ge(*aft("hq_th", m))
                STT(hq[:, m], hq[:, m], 1.0, ps[:, bank_of[f"hq{m}"]], AD, MU).then_inc(*inc("hq_ev", f"hq{m}")); settle()

            def hg_ev(m):
                v.wait_ge(*aft("hg_th", m))
                STT(hgt[:, m], hgt[:, m], 1.0, ps[:, bank_of[f"hg{m}"]], AD, MU).then_inc(*inc("hg_ev", f"hg{m}")); settle()

            qs = 0.5 * mq
            for hd in range(4):
                b8 = hb[:, hd].rearrange("p (c s) -> p c s", c=8)
                b32 = hb[:, hd].rearrange("p (c s) -> p c s", c=32)
                mid = b32[:, :, 8]
                if hd:
                    v.wait_ge(*aft("hg_qb", hd - 1))
                TT(het[:].rearrange("p (c s) -> p c s", c=32), b32, bc(mid, 16), SU).then_inc(*inc("hg_arg", (hd, "q"))); settle()
                if hd:
                    v.wait_ge(*aft("hg_att", hd - 1))
                for T in range(4):
                    w = 16 * (T + 1)
                    midT = hb[:, hd, 16 * T + 8:16 * T + 8 + 449:64]
                    TT(hKT[:, T, :, :w], bc(midT, w), b8[:, :, :w], SU).then_inc(
                        *inc("hg_arg", (hd, "kt") if T == 3 else (hd, "kt", T))); settle()
                v.wait_ge(*aft("hg_ex", (hd, "q")))
                STT(hQ[:], hq[:, hd], qs, het[:], MU, MU).then_inc(*inc("hg_q", hd)); settle()
                if hd:
                    v.wait_ge(*aft("hg_ke", hd - 1))
                TT(tmp[:, 0].rearrange("p (c s) -> p c s", c=8), bc(b8[:, :, 63], 64), b8, SU).then_inc(*inc("hg_arg", (hd, "e"))); settle()
                for T in range(4):
                    w = 16 * (T + 1)
                    v.wait_ge(*aft("hg_ex", (hd, "kt", T)))
                    TT(hKT[:, T, :, :w], hKT[:, T, :, :w], hk[:, hd].rearrange("p (c s) -> p c s", c=8)[:, :, :w], MU).then_inc(
                        *inc("hg_kt", hd if T == 3 else (hd, T))); settle()
                v.wait_ge(*aft("hg_ex", (hd, "b")))
                STT(hq[:, hd], hq[:, hd], qs, het[:], MU, MU).then_inc(*inc("hg_qb", hd)); settle()
                v.wait_ge(*aft("hg_ex", (hd, "e")))
                TT(hk[:, hd], hk[:, hd], tmp[:, 0], MU).then_inc(*inc("hg_ke", hd)); settle()
                for name in HG[hd]:
                    if name[0] == "h":
                        hg_ev(int(name[2:]))
                v.wait_ge(*aft("hg_att", hd))
                TT(hatt[:, hd], ps[:, 4, 0:256].rearrange("p (a b) -> p a b", a=4),
                   C("hgmask").unsqueeze(1).to_broadcast([P, 4, 64]), MU).then_inc(*inc("hg_attm", hd)); settle()
            v.wait_ge(*aft("hg_ex", (3, "l")))
            for c in range(7):
                v.wait_ge(*aft("hg_st", c))
                if c:
                    v.wait_ge(*aft("hg_o", c - 1))
                for hd in range(4):
                    src = ps[:, c % 2, hd * P:(hd + 1) * P]
                    sig = inc("hg_state", c if hd == 3 else (c, hd))
                    if c == 0:
                        V.tensor_copy(hst[1][:, hd], src).then_inc(*sig); settle()
                    else:
                        if hd == 0:
                            v.wait_ge(*aft("hg_state", c - 1))
                        STT(hst[(c + 1) % 2][:, hd], hst[c % 2][:, hd], eblast[:, hd, c:c + 1], src, MU, AD).then_inc(*sig); settle()
            def yc(hd):
                v.wait_ge(*aft("hg_rs", hd))
                then(STT(hk[:, hd], ps[:, 4 + hd], col("hg_norm", 0), hk[:, hd], MU, MU))
                STT(tmp[:, hd % 2], hk[:, hd], 0.5, hgt[:, hd], MU, MU).then_inc(*inc("yC_t", hd)); settle()

            yc(0)
            for hd in range(4):
                if hd < 3:
                    yc(hd + 1)
                v.wait_ge(*aft("yC_hi", hd))
                TT(y_lo[:, hd], tmp[:, hd % 2], y_hi[:, hd].bitcast(F32), SU).then_inc(*inc("yC_lo", hd)); settle()
            for m in range(9):
                if m < 8:
                    merge("C", m)
                if m:
                    v.wait_ge(*aft("merged_hi", m - 1))
                    STT(h_lo[:, m - 1], merged[:, m - 1], 0.5, h_hi[:, m - 1].bitcast(F32), MU, SU)\
                        .then_inc(*inc("merged_lo", m - 1)); settle()
            v.wait_ge(*aft("mem_loaded", "m"))
            then(TT(macc[:], mraw[:, 0], mraw[:, 0], MU))
            for k in range(1, KC):
                then(TT(mt[:, 0], mraw[:, k], mraw[:, k], MU))
                then(TT(macc[:], macc[:], mt[:, 0], AD), *(("mem_acc", "m") if k == KC - 1 else ("dve",)))

            def m_t(k):
                STT(mt[:, k % 2], mraw[:, k], col("norm_mem", k), mr[:], MU, MU).then_inc(*inc("mem_t", k)); settle()

            for m in range(8):
                residual(bank_of[f"o{m}"], m, "res_o", f"o{m}", True)
                if m == 2:
                    v.wait_ge(*aft("mem_rstd", "m"))
                    m_t(0)
                    for k in range(KC):
                        if k + 1 < KC:
                            m_t(k + 1)
                        v.wait_ge(*aft("mem_hi", k))
                        TT(m_lo[:, k], mt[:, k % 2], m_hi[:, k].bitcast(F32), SU).then_inc(*inc("mem_lo", k)); settle()
            norm("xa")
            v.wait_ge(*aft("x_rs", "k"))
            STT(kx[:], ps[:, 0:2].rearrange("p a (b n) -> p (a b) n", b=2), col("xa_k", 0), rsx[:, :, :MEM], MU, MU)\
                .then_inc(*inc("xk_ev", "k")); settle()

            for m in range(4):
                v.wait_ge(*aft("x_sq", f"xq{m}"))
                TS(qx[:, m], ps[:, bank_of[f"xq{m}"]], col("xa_q", 0), None, MU).then_inc(*inc("xq_ev", f"xq{m}")); settle()
                if m % 2:
                    r = rq[:, m * 4 - 4:m * 4 + 4]
                    v.wait_ge(*aft("x_rs", f"xq{m}"))
                    TS(r, r, mq, None, MU).then_inc(*inc("xrq", m)); settle()

            def x_max(hd):
                v.wait_ge(*aft("xqk", hd))
                b = 4 + 2 * (hd % 2)
                n = nbx[:, hd % 2]
                then(V.reduce_max(n, ps[:, b:b + 2].rearrange("p a (b n) -> p (a b) n", b=2), AX, negate=True))
                TT(n, n, rq[:, hd * 4:hd * 4 + 4], MU).then_inc(*inc("xnb", hd)); settle()

            def x_norm(hd):
                v.wait_ge(*aft("xexp", hd))
                then(V.reciprocal(smx[:, hd % 2], smx[:, hd % 2]))
                TT(px[:, hd % 2], px[:, hd % 2], bc(smx[:, hd % 2], MEM), MU).then_inc(*inc("xpn", hd)); settle()

            def x_low(hd):
                v.wait_ge(*aft("xo_hi", hd))
                TT(y_lo[:, hd], ps[:, 2 + hd % 2], y_hi[:, hd].bitcast(F32), SU).then_inc(*inc("xo_lo", hd)); settle()

            x_max(0)
            x_max(1)
            x_norm(0)
            x_norm(1)
            for hd in range(4):
                v.wait_ge(*aft("xptr", (hd, 1)))
                if hd >= 2:
                    v.wait_ge(*aft("xpv", hd - 2))
                V.tensor_copy(ptx[:, hd % 2, 1], ps[:, 1]).then_inc(*inc("xptd", hd)); settle()
                if hd in (1, 2):
                    x_norm(hd + 1)
                if hd:
                    x_low(hd - 1)
                if hd < 2:
                    x_max(hd + 2)
            x_low(3)
            for m in range(8):
                residual(m % 4, m, "res_xo", f"xo{m // 2}.{m % 2}", True)
            norm("ffn")
            j = 0
            for p, n in enumerate(FFN_PASSES):
                def lo(c, j):
                    v.wait_ge(*aft("ffn_hi", j))
                    TT(a_lo[:, c], ft[:, j % 2], a_hi[:, c].bitcast(F32), SU).then_inc(*inc(f"ffn_lo{p}", c)); settle()
                for c in range(n):
                    v.wait_ge(*aft("ffn_s", f"fg{p}_{c}"))
                    v.wait_ge(*aft("dense_done", f"fu{p}_{c}"))
                    TT(ft[:, j % 2], sl[:, j % 2], ps[:, bank_of[f"fu{p}_{c}"]], MU).then_inc(*inc("ffn_t", f"fu{p}_{c}")); settle()
                    lo(c, j)
                    j += 1
                for m in range(8):
                    bank = bank_of[f"fd{p}_{m}"]
                    if p < 2:
                        residual(bank, m, f"res_f{p}", f"fd{p}_{m}", False)
                    else:
                        v.wait_ge(*aft("dense_done", f"fd2_{m}"))
                        then(TT(xT[:, m], xT[:, m], ps[:, bank], AD), "res_f2", f"fd2_{m}")
                        squares(m, None)
    ctx.close()
    return {"count": count, "marks": marks}


SPLIT = (("q", 512), ("kc", 128), ("vc", 128), ("ks", 128), ("vs", 128), ("kw", 128), ("vw", 128), ("gate", 24),
         ("z", 512), ("xbc", 768), ("dt", 8), ("hq", 512), ("hf", 512), ("hi", 512), ("hg", 512),
         ("gA", 1024), ("gB", 1024), ("gC", 1024))


def constants():
    c = np.zeros((P, NCST), np.float32)

    def put(name, a):
        c[:a.shape[0], CC[name][0]:CC[name][1]] = a

    p, f = np.arange(P)[:, None], np.arange(P)[None, :]
    put("ident", np.eye(P))
    put("triu", (p <= f) * 1.0)
    put("ones", np.ones((P, P)))
    put("maskq", np.where(f > p, NEG, 0.0))
    put("maskt", np.where(f < p, NEG, 0.0))
    put("hgmask", (np.arange(64)[None, :] >= p % 64) * 1.0)
    inv = np.float32(1.0) / (np.float32(10000.0) ** (np.arange(32, dtype=np.float32) / np.float32(32)))
    ang = np.arange(S, dtype=np.float32)[:, None] * inv[None, :]
    put("cos", np.cos(ang).reshape(NT, P, 32).transpose(1, 0, 2).reshape(P, NT * 32))
    put("sin", np.sin(ang).reshape(NT, P, 32).transpose(1, 0, 2).reshape(P, NT * 32))
    posc = (np.arange(64) % 32 * 16 + 31).astype(np.float32)
    put("cosc", np.cos(posc[:, None] * inv[None, :]))
    put("sinc", np.sin(posc[:, None] * inv[None, :]))
    t = np.arange(NT)[None, :, None] * P + np.arange(P)[:, None, None]
    put("maskc", np.where(16 * np.arange(32)[None, None, :] + 31 <= t, 0.0, NEG).reshape(P, NT * 32))
    put("valid", (t[:, :, 0] >= 31) * 1.0)
    put("eps", np.full((P, 1), EPS))
    return c


def pack(i):
    w = np.zeros((DEPTH, NU, P, UNIT), np.float32)
    at, c = {}, 0
    for name, n in SPLIT:
        at[name] = slice(c, c + n)
        c += n
    for l in range(DEPTH):
        win = i["w_in"][l]
        kv = np.concatenate([win[:, at[n]] for n in ("ks", "kw", "vs", "vw")], axis=1)
        gd = np.concatenate([win[:, at["gate"]], win[:, at["dt"]]], axis=1)

        def t_units(name, m):
            u = UNIT_OF[name]
            w[l, u:u + 4] = m.reshape(4, 2, P, 512).transpose(0, 2, 1, 3).reshape(4, P, UNIT)

        def f_units(name, m):
            nk, n = m.shape[0] // P, m.shape[1] // P
            m = m.reshape(nk, P, n, P).transpose(2, 1, 0, 3).reshape(n, P, nk * P)
            for o in range(n):
                w[l, UNIT_OF[name.format(o)], :, :nk * P] = m[o]

        def h_units(name, m):
            m = m.reshape(4, P, 4, 2, P).transpose(2, 1, 3, 0, 4).reshape(4, P, UNIT)
            for o in range(4):
                w[l, UNIT_OF[name.format(o)]] = m[o]

        t_units("q", win[:, at["q"]])
        t_units("kv", kv)
        t_units("z", win[:, at["z"]])
        t_units("hv", win[:, at["hi"]])
        t_units("xv", i["xa_w_v"][l])
        w[l, UNIT_OF["gd"]].reshape(P, KC, P)[:, :, :32] = gd.reshape(KC, P, 32).transpose(1, 0, 2)
        for n in ("kc", "vc"):
            f_units(n, win[:, at[n]])
        for n, a in (("xbc{}", "xbc"), ("hf{}", "hf"), ("hq{}", "hq"), ("hg{}", "hg"), ("gA{}", "gA"), ("gB{}", "gB"),
                     ("gC{}", "gC")):
            f_units(n, win[:, at[a]])
        for n, a in (("w1k", "nsa_cmp_w1_k"), ("w1v", "nsa_cmp_w1_v")):
            w[l, UNIT_OF[n]] = i[a][l].reshape(16, P, 64).transpose(1, 0, 2).reshape(P, UNIT)
        for n, a in (("yA{}", "w_nsa_o"), ("yB{}", "w_ssm_o"), ("yC{}", "w_hg_o"), ("xo{}", "xa_w_o")):
            h_units(n, i[a][l])
        f_units("o{}", i["w_out"][l])
        f_units("xk{}", i["xa_w_k"][l])
        f_units("xq{}", i["xa_w_q"][l])
        c0 = 0
        for p, n in enumerate(FFN_PASSES):
            cols = slice(c0 * P, (c0 + n) * P)
            f_units(f"fg{p}_{{}}", i["ffn_w_gate"][l][:, cols])
            f_units(f"fu{p}_{{}}", i["ffn_w_up"][l][:, cols])
            f_units(f"fd{p}_{{}}", i["ffn_w_down"][l][cols])
            c0 += n
        prm = w[l, 0]

        def put(name, a):
            prm[:a.shape[0], PC[name][0]:PC[name][1]] = a

        for n in ("norm_mix", "norm_xa", "norm_mem", "norm_ffn"):
            put(n, i[n][l].reshape(KC, P).T)
        put("conv_w", i["ssm_conv_w"][l].reshape(4, 6, P).transpose(2, 1, 0).reshape(P, 24))
        put("conv_b", i["ssm_conv_b"][l].reshape(6, P).T)
        put("lb", i["hg_lb_logits"].reshape(DEPTH * 4, P).T)
        put("hg_norm", i["hg_norm"][l][:, None])
        put("xa_q", i["xa_q_norm"][l][:, None])
        put("xa_k", i["xa_k_norm"][l][:, None])
        put("ssm_norm", i["ssm_norm"][l].reshape(4, P).T)
        for n, a in (("q_norm", "nsa_q_norm"), ("k_norm", "nsa_k_norm"), ("dt_bias", "ssm_dt_bias"),
                     ("a_log", "ssm_a_log"), ("ssm_d", "ssm_d")):
            put(n, np.broadcast_to(i[a][l][None, :], (P, i[a].shape[-1])))
        put("pos_k", i["nsa_cmp_pos_k"][l].reshape(16, P).T)
        put("pos_v", i["nsa_cmp_pos_v"][l].reshape(16, P).T)
        put("w2k", i["nsa_cmp_w2_k"][l])
        put("w2v", i["nsa_cmp_w2_v"][l])
        put("layer", np.full((P, 1), float(l), np.float32))
    return w.reshape(DEPTH * NU, P, UNIT)


def program(nc, totals=None, n_layers=DEPTH):
    nc.disable_value_cache = True
    x = nc.dram_tensor("x_in", [P, KC, S], F32, kind="ExternalInput").ap()
    mem = nc.dram_tensor("mem_in", [P, KC, MEM], F32, kind="ExternalInput").ap()
    w = nc.dram_tensor("w_in_units", [DEPTH * NU, P, UNIT], F32, kind="ExternalInput").ap()
    cst = nc.dram_tensor("constants", [P, NCST], F32, kind="ExternalInput").ap()
    out = nc.dram_tensor("out", [P, KC, S], F32, kind="ExternalOutput").ap()
    return build(nc, x, mem, w, cst, out, totals, n_layers)


def kernel(**inputs):
    import concourse.bacc as bacc
    from concourse.bass_utils import run_bass_kernel_spmd
    i = {k: np.asarray(a) for k, a in inputs.items()}
    x = np.ascontiguousarray(i["x"][0].reshape(S, KC, P).transpose(2, 1, 0))
    mem = np.ascontiguousarray(i["mem"][0].reshape(MEM, KC, P).transpose(2, 1, 0))
    totals = program(bacc.Bacc("TRN2", target_bir_lowering=False, num_devices=1))
    nc = bacc.Bacc("TRN2", target_bir_lowering=False, num_devices=1)
    program(nc, totals)
    r = run_bass_kernel_spmd(nc, [{"x_in": x, "mem_in": mem, "w_in_units": pack(i), "constants": constants()}],
                             core_ids=[0])
    o = np.asarray(r.results[0]["out"])
    return np.ascontiguousarray(o.transpose(2, 1, 0)).reshape(1, S, D)
```
